# Optimizing a Trainium2 kernel written in Bass

```python
import math
import jax, jax.numpy as jnp
from jax import lax
import numpy as np

D_MODEL = 1024
BATCH = 1
SEQ = 1024
DEPTH = 1

N_MIXERS = 2
MLSTM_HEADS = 4
MLSTM_DQK = D_MODEL // (2 * MLSTM_HEADS)
MLSTM_DV = D_MODEL // MLSTM_HEADS
MLSTM_QK = MLSTM_HEADS * MLSTM_DQK
MLSTM_V = MLSTM_HEADS * MLSTM_DV
MLSTM_IN = 2 * MLSTM_QK + 2 * MLSTM_V + 2 * MLSTM_HEADS
CHUNK = 64
SCONV_WIDTH = D_MODEL
CONV_K = 3
D_FF = 2816
EPS = 1e-6


def rmsnorm(x, g):
    xf = x.astype(jnp.float32)
    y = xf * lax.rsqrt(jnp.mean(xf * xf, axis=-1, keepdims=True) + EPS) * g.astype(jnp.float32)
    return y.astype(x.dtype)

def causal_dwconv(x, w, b):
    c = x.shape[-1]
    rhs = w.astype(x.dtype)[:, None, :]
    y = lax.conv_general_dilated(
        x, rhs, window_strides=(1,), padding=[(CONV_K - 1, 0)],
        dimension_numbers=('NWC', 'WIO', 'NWC'), feature_group_count=c)
    return y + b.astype(x.dtype)

def mlstm_mixer(x, w_in, b_gates, head_norm, w_out):
    bsz, s, _ = x.shape
    h_, dqk, dv, L = MLSTM_HEADS, MLSTM_DQK, MLSTM_DV, CHUNK
    nc = s // L
    proj = x @ w_in
    i0 = MLSTM_QK
    i1 = i0 + MLSTM_QK
    i2 = i1 + MLSTM_V
    i3 = i2 + MLSTM_V
    i4 = i3 + MLSTM_HEADS
    q = proj[..., :i0].astype(jnp.float32) * (dqk ** -0.5)
    k = proj[..., i0:i1].astype(jnp.float32)
    v = proj[..., i1:i2].astype(jnp.float32)
    o_gate = jax.nn.sigmoid(proj[..., i2:i3].astype(jnp.float32))
    bg = b_gates.astype(jnp.float32)
    log_i = proj[..., i3:i4].astype(jnp.float32) + bg[:MLSTM_HEADS]
    log_f = jax.nn.log_sigmoid(proj[..., i4:].astype(jnp.float32) + bg[MLSTM_HEADS:])

    def to_chunks(t, d):
        return t.reshape(bsz, nc, L, h_, d).transpose(1, 0, 3, 2, 4)

    qc = to_chunks(q, dqk)
    kc = to_chunks(k, dqk)
    vc = to_chunks(v, dv)
    lic = log_i.reshape(bsz, nc, L, h_).transpose(1, 0, 3, 2)
    lfc = log_f.reshape(bsz, nc, L, h_).transpose(1, 0, 3, 2)
    causal = jnp.tril(jnp.ones((L, L), dtype=bool))

    def step(carry, xs):
        C, n, m = carry
        qb, kb, vb, li, lf = xs
        b = jnp.cumsum(lf, axis=-1)
        logD = b[..., :, None] - b[..., None, :] + li[..., None, :]
        logD = jnp.where(causal, logD, -jnp.inf)
        inter = b + m[..., None]
        m_t = jnp.maximum(inter, jnp.max(logD, axis=-1))
        Dm = jnp.exp(logD - m_t[..., None])
        sc = jnp.exp(inter - m_t)
        sk = jnp.einsum('bhtd,bhsd->bhts', qb, kb) * Dm
        num = jnp.einsum('bhts,bhsv->bhtv', sk, vb) + sc[..., None] * jnp.einsum('bhtd,bhdv->bhtv', qb, C)
        den = jnp.sum(sk, axis=-1) + sc * jnp.einsum('bhtd,bhd->bht', qb, n)
        hb = num / jnp.maximum(jnp.abs(den), jnp.exp(-m_t))[..., None]
        bL = b[..., -1]
        logw = bL[..., None] - b + li
        m_new = jnp.maximum(bL + m, jnp.max(logw, axis=-1))
        w = jnp.exp(logw - m_new[..., None])
        decay = jnp.exp(bL + m - m_new)
        C_new = decay[..., None, None] * C + jnp.einsum('bhs,bhsd,bhsv->bhdv', w, kb, vb)
        n_new = decay[..., None] * n + jnp.einsum('bhs,bhsd->bhd', w, kb)
        return (C_new, n_new, m_new), hb

    init = (jnp.zeros((bsz, h_, dqk, dv), jnp.float32),
            jnp.zeros((bsz, h_, dqk), jnp.float32),
            jnp.zeros((bsz, h_), jnp.float32))
    _, hs = lax.scan(step, init, (qc, kc, vc, lic, lfc))
    hs = hs.transpose(1, 0, 3, 2, 4).reshape(bsz, s, h_, dv)
    hs = hs * lax.rsqrt(jnp.mean(hs * hs, axis=-1, keepdims=True) + EPS) * head_norm.astype(jnp.float32)
    hs = hs.reshape(bsz, s, MLSTM_V) * o_gate
    return hs.astype(x.dtype) @ w_out

def short_conv_mixer(x, w_in, conv_w, conv_b, w_out):
    proj = x @ w_in
    bgate = proj[..., :SCONV_WIDTH]
    cgate = proj[..., SCONV_WIDTH:2 * SCONV_WIDTH]
    xin = proj[..., 2 * SCONV_WIDTH:]
    y = causal_dwconv(cgate * xin, conv_w, conv_b)
    return (bgate * y) @ w_out

def conv_ffn(x, w_up, conv_w, conv_b, w_down):
    u = causal_dwconv(x @ w_up, conv_w, conv_b)
    gate = u[..., :D_FF]
    val = u[..., D_FF:]
    return (jax.nn.silu(gate) * val) @ w_down

def first_inputs(seed: int = 0) -> dict:
    key = jax.random.key(seed)
    ks = jax.random.split(key, 24)
    f32 = jnp.float32

    def nrm(k, shape, scale):
        return jax.random.normal(k, shape, f32) * scale

    def gain(k, shape):
        return 1.0 + 0.02 * jax.random.normal(k, shape, f32)

    b_i = 0.1 * jax.random.normal(ks[3], (MLSTM_HEADS,), f32)
    b_f = 3.0 + 0.5 * jax.random.normal(ks[4], (MLSTM_HEADS,), f32)
    return {
        "x": jax.random.normal(ks[0], (BATCH, SEQ, D_MODEL), f32),
        "l0_norm_mix": gain(ks[1], (D_MODEL,)),
        "l0_mlstm_w_in": nrm(ks[2], (D_MODEL, MLSTM_IN), D_MODEL ** -0.5),
        "l0_mlstm_b_gates": jnp.concatenate([b_i, b_f]),
        "l0_mlstm_head_norm": gain(ks[5], (MLSTM_HEADS, MLSTM_DV)),
        "l0_mlstm_w_out": nrm(ks[6], (MLSTM_V, D_MODEL), MLSTM_V ** -0.5),
        "l0_norm_ffn": gain(ks[7], (D_MODEL,)),
        "l0_ffn_w_up": nrm(ks[8], (D_MODEL, 2 * D_FF), D_MODEL ** -0.5),
        "l0_ffn_conv_w": nrm(ks[9], (CONV_K, 2 * D_FF), CONV_K ** -0.5),
        "l0_ffn_conv_b": nrm(ks[10], (2 * D_FF,), 0.02),
        "l0_ffn_w_down": nrm(ks[11], (D_FF, D_MODEL), D_FF ** -0.5),
        "l1_norm_mix": gain(ks[12], (D_MODEL,)),
        "l1_sconv_w_in": nrm(ks[13], (D_MODEL, 3 * SCONV_WIDTH), D_MODEL ** -0.5),
        "l1_sconv_conv_w": nrm(ks[14], (CONV_K, SCONV_WIDTH), CONV_K ** -0.5),
        "l1_sconv_conv_b": nrm(ks[15], (SCONV_WIDTH,), 0.02),
        "l1_sconv_w_out": nrm(ks[16], (SCONV_WIDTH, D_MODEL), SCONV_WIDTH ** -0.5),
        "l1_norm_ffn": gain(ks[17], (D_MODEL,)),
        "l1_ffn_w_up": nrm(ks[18], (D_MODEL, 2 * D_FF), D_MODEL ** -0.5),
        "l1_ffn_conv_w": nrm(ks[19], (CONV_K, 2 * D_FF), CONV_K ** -0.5),
        "l1_ffn_conv_b": nrm(ks[20], (2 * D_FF,), 0.02),
        "l1_ffn_w_down": nrm(ks[21], (D_FF, D_MODEL), D_FF ** -0.5),
        "final_norm": gain(ks[22], (D_MODEL,)),
    }

def first_block(x, l0_norm_mix, l0_mlstm_w_in, l0_mlstm_b_gates, l0_mlstm_head_norm, l0_mlstm_w_out,
              l0_norm_ffn, l0_ffn_w_up, l0_ffn_conv_w, l0_ffn_conv_b, l0_ffn_w_down,
              l1_norm_mix, l1_sconv_w_in, l1_sconv_conv_w, l1_sconv_conv_b, l1_sconv_w_out,
              l1_norm_ffn, l1_ffn_w_up, l1_ffn_conv_w, l1_ffn_conv_b, l1_ffn_w_down,
              final_norm):
    mix_norms = [l0_norm_mix, l1_norm_mix]
    mix_params = [(l0_mlstm_w_in, l0_mlstm_b_gates, l0_mlstm_head_norm, l0_mlstm_w_out),
                  (l1_sconv_w_in, l1_sconv_conv_w, l1_sconv_conv_b, l1_sconv_w_out)]
    ffn_norms = [l0_norm_ffn, l1_norm_ffn]
    ffn_params = [(l0_ffn_w_up, l0_ffn_conv_w, l0_ffn_conv_b, l0_ffn_w_down),
                  (l1_ffn_w_up, l1_ffn_conv_w, l1_ffn_conv_b, l1_ffn_w_down)]
    mixers = [mlstm_mixer, short_conv_mixer]
    for i in range(DEPTH):
        mixer = mixers[i % N_MIXERS]
        x = x + mixer(rmsnorm(x, mix_norms[i]), *mix_params[i])
        x = x + conv_ffn(rmsnorm(x, ffn_norms[i]), *ffn_params[i])
    return rmsnorm(x, final_norm)


DEPTH_2 = 2

QBLOCK = 128
WINDOW = 128
ROPE_THETA = 10000.0
MLA_HEADS = D_MODEL // 128
MLA_Q_RANK = D_MODEL // 4
MLA_KV_RANK = D_MODEL // 8
MLA_NOPE = 64
MLA_ROPE = 32
MLA_V = 64
SWA_HEADS = D_MODEL // 128
SWA_KV_HEADS = SWA_HEADS // 4
SWA_HEAD_DIM = 64
FOX_HEADS = D_MODEL // 64
FOX_HEAD_DIM = 64
FOX_WIDTH = FOX_HEADS * FOX_HEAD_DIM
FORGET_BIAS_INIT = 2.0

EVEN_WIDTH = MLA_HEADS * MLA_V + SWA_HEADS * SWA_HEAD_DIM
EVEN_SPLITS = (MLA_Q_RANK, MLA_KV_RANK, MLA_ROPE, SWA_HEADS * SWA_HEAD_DIM,
               SWA_KV_HEADS * SWA_HEAD_DIM, SWA_KV_HEADS * SWA_HEAD_DIM, EVEN_WIDTH)
ODD_SPLITS = (FOX_WIDTH, FOX_WIDTH, FOX_WIDTH, FOX_HEADS, FOX_WIDTH)
N_EVEN = (DEPTH_2 + 1) // 2
N_ODD = DEPTH_2 // 2


def rms_norm(x, g):
    xf = x.astype(jnp.float32)
    y = xf * lax.rsqrt(jnp.mean(xf * xf, axis=-1, keepdims=True) + EPS)
    return (y * g.astype(jnp.float32)).astype(x.dtype)

def split_cols(z, sizes):
    idx = [int(v) for v in np.cumsum(sizes)[:-1]]
    return jnp.split(z, idx, axis=-1)

def rope_angles(positions, dim):
    inv_freq = 1.0 / (ROPE_THETA ** (jnp.arange(0, dim, 2, dtype=jnp.float32) / dim))
    return positions.astype(jnp.float32)[..., None] * inv_freq

def apply_rope(x, ang):
    cos, sin = jnp.cos(ang), jnp.sin(ang)
    xf = x.astype(jnp.float32)
    x1, x2 = jnp.split(xf, 2, axis=-1)
    return jnp.concatenate([x1 * cos - x2 * sin, x2 * cos + x1 * sin], axis=-1).astype(x.dtype)

def alibi_slopes(n):
    return 2.0 ** (-8.0 * (jnp.arange(n, dtype=jnp.float32) + 1.0) / n)

def causal_block_attention(q, k, v, log_cum=None):
    B, S, H, Dk = q.shape
    Dv = v.shape[-1]
    nb = S // QBLOCK
    scale = Dk ** -0.5
    kpos = jnp.arange(S)
    lc_t = None if log_cum is None else jnp.transpose(log_cum, (0, 2, 1))

    def one_block(i):
        start = i * QBLOCK
        qi = lax.dynamic_slice_in_dim(q, start, QBLOCK, axis=1)
        s = jnp.einsum('bqhd,bkhd->bhqk', qi, k, preferred_element_type=jnp.float32) * scale
        if lc_t is not None:
            ci = lax.dynamic_slice_in_dim(lc_t, start, QBLOCK, axis=2)
            s = s + ci[..., :, None] - lc_t[..., None, :]
        qpos = start + jnp.arange(QBLOCK)
        mask = kpos[None, :] <= qpos[:, None]
        s = jnp.where(mask, s, -jnp.inf)
        p = jax.nn.softmax(s, axis=-1)
        return jnp.einsum('bhqk,bkhd->bqhd', p.astype(v.dtype), v)

    out = lax.map(one_block, jnp.arange(nb))
    return jnp.transpose(out, (1, 0, 2, 3, 4)).reshape(B, S, H, Dv)

def sliding_window_sink_attention(q, k, v, sinks, slopes):
    B, S, H, D = q.shape
    KV = k.shape[2]
    G = H // KV
    W = WINDOW
    nb = S // W
    qb = q.reshape(B, nb, W, KV, G, D)
    pad = ((0, 0), (W, 0), (0, 0), (0, 0))
    kp = jnp.pad(k, pad).reshape(B, nb + 1, W, KV, D)
    vp = jnp.pad(v, pad).reshape(B, nb + 1, W, KV, D)
    kb = jnp.concatenate([kp[:, :-1], kp[:, 1:]], axis=2)
    vb = jnp.concatenate([vp[:, :-1], vp[:, 1:]], axis=2)
    s = jnp.einsum('bnqkgd,bnckd->bnkgqc', qb, kb, preferred_element_type=jnp.float32) * (D ** -0.5)
    a = jnp.arange(W)[:, None]
    c = jnp.arange(2 * W)[None, :]
    dist = (W + a - c).astype(jnp.float32)
    blk = jnp.arange(nb)[:, None, None]
    valid = (dist >= 0) & (dist < W) & (blk * W + c[None] - W >= 0)
    s = s - slopes.reshape(KV, G)[:, :, None, None] * dist
    s = jnp.where(valid[None, :, None, None], s, -jnp.inf)
    sink = sinks.astype(jnp.float32).reshape(KV, G)[:, :, None, None]
    m = jnp.maximum(jnp.max(s, axis=-1, keepdims=True), sink)
    p = jnp.exp(s - m)
    p = p / (jnp.sum(p, axis=-1, keepdims=True) + jnp.exp(sink - m))
    o = jnp.einsum('bnkgqc,bnckd->bnqkgd', p.astype(v.dtype), vb)
    return o.reshape(B, S, H, D)

def mla_swa_layer(x, positions, g_in, w_in, g_q_a, w_q_up, g_kv_a, w_kv_up, sinks, w_out):
    B, S, _ = x.shape
    h = rms_norm(x, g_in)
    z = h @ w_in
    cq, ckv, kpe, q_s, k_s, v_s, gate = split_cols(z, EVEN_SPLITS)
    q = (rms_norm(cq, g_q_a) @ w_q_up).reshape(B, S, MLA_HEADS, MLA_NOPE + MLA_ROPE)
    q_nope, q_pe = q[..., :MLA_NOPE], q[..., MLA_NOPE:]
    kv = (rms_norm(ckv, g_kv_a) @ w_kv_up).reshape(B, S, MLA_HEADS, MLA_NOPE + MLA_V)
    k_nope, v_m = kv[..., :MLA_NOPE], kv[..., MLA_NOPE:]
    ang = rope_angles(positions, MLA_ROPE)
    q_pe = apply_rope(q_pe, ang[:, :, None, :])
    k_pe = apply_rope(kpe, ang)[:, :, None, :]
    qm = jnp.concatenate([q_nope, q_pe], axis=-1)
    km = jnp.concatenate([k_nope, jnp.broadcast_to(k_pe, (B, S, MLA_HEADS, MLA_ROPE))], axis=-1)
    o_mla = causal_block_attention(qm, km, v_m)
    o_swa = sliding_window_sink_attention(
        q_s.reshape(B, S, SWA_HEADS, SWA_HEAD_DIM),
        k_s.reshape(B, S, SWA_KV_HEADS, SWA_HEAD_DIM),
        v_s.reshape(B, S, SWA_KV_HEADS, SWA_HEAD_DIM),
        sinks, alibi_slopes(SWA_HEADS))
    o = jnp.concatenate([o_mla.reshape(B, S, -1), o_swa.reshape(B, S, -1)], axis=-1)
    return x + (o * jax.nn.silu(gate)) @ w_out

def fox_layer(x, g_in, w_in, b_f, w_out):
    B, S, _ = x.shape
    h = rms_norm(x, g_in)
    z = h @ w_in
    q, k, v, f_logit, gate = split_cols(z, ODD_SPLITS)
    log_f = jax.nn.log_sigmoid(f_logit.astype(jnp.float32) + b_f.astype(jnp.float32))
    log_cum = jnp.cumsum(log_f, axis=1)
    o = causal_block_attention(q.reshape(B, S, FOX_HEADS, FOX_HEAD_DIM),
                               k.reshape(B, S, FOX_HEADS, FOX_HEAD_DIM),
                               v.reshape(B, S, FOX_HEADS, FOX_HEAD_DIM), log_cum=log_cum)
    return x + (o.reshape(B, S, FOX_WIDTH) * jax.nn.silu(gate)) @ w_out

def second_inputs(seed: int = 0) -> dict:
    key = jax.random.key(seed)
    ks = jax.random.split(key, 16)
    f32 = jnp.float32

    def w(k, shape, fan_in):
        return jax.random.normal(k, shape, f32) * (fan_in ** -0.5)

    def gain(k, shape):
        return 1.0 + 0.05 * jax.random.normal(k, shape, f32)

    x = jax.random.normal(ks[0], (BATCH, SEQ, D_MODEL), f32)
    positions = jnp.broadcast_to(jnp.arange(SEQ, dtype=jnp.int32), (BATCH, SEQ))
    return {
        "x": x,
        "positions": positions,
        "e_g_in": gain(ks[1], (N_EVEN, D_MODEL)),
        "e_w_in": w(ks[2], (N_EVEN, D_MODEL, sum(EVEN_SPLITS)), D_MODEL),
        "e_g_q_a": gain(ks[3], (N_EVEN, MLA_Q_RANK)),
        "e_w_q_up": w(ks[4], (N_EVEN, MLA_Q_RANK, MLA_HEADS * (MLA_NOPE + MLA_ROPE)), MLA_Q_RANK),
        "e_g_kv_a": gain(ks[5], (N_EVEN, MLA_KV_RANK)),
        "e_w_kv_up": w(ks[6], (N_EVEN, MLA_KV_RANK, MLA_HEADS * (MLA_NOPE + MLA_V)), MLA_KV_RANK),
        "e_sinks": jax.random.normal(ks[7], (N_EVEN, SWA_HEADS), f32),
        "e_w_out": w(ks[8], (N_EVEN, EVEN_WIDTH, D_MODEL), EVEN_WIDTH),
        "o_g_in": gain(ks[9], (N_ODD, D_MODEL)),
        "o_w_in": w(ks[10], (N_ODD, D_MODEL, sum(ODD_SPLITS)), D_MODEL),
        "o_b_f": FORGET_BIAS_INIT + 0.5 * jax.random.normal(ks[11], (N_ODD, FOX_HEADS), f32),
        "o_w_out": w(ks[12], (N_ODD, FOX_WIDTH, D_MODEL), FOX_WIDTH),
        "g_final": gain(ks[13], (D_MODEL,)),
    }

def second_block(x, positions, e_g_in, e_w_in, e_g_q_a, e_w_q_up, e_g_kv_a, e_w_kv_up, e_sinks,
              e_w_out, o_g_in, o_w_in, o_b_f, o_w_out, g_final):
    for layer in range(DEPTH_2):
        j = layer // 2
        if layer % 2 == 0:
            x = mla_swa_layer(x, positions, e_g_in[j], e_w_in[j], e_g_q_a[j], e_w_q_up[j],
                              e_g_kv_a[j], e_w_kv_up[j], e_sinks[j], e_w_out[j])
        else:
            x = fox_layer(x, o_g_in[j], o_w_in[j], o_b_f[j], o_w_out[j])
    return rms_norm(x, g_final)


def setup_inputs(seed=0):
    out = dict(first_inputs(seed))
    for name, value in second_inputs(seed + 1).items():
        if name != "x":
            out[name + "_2"] = value
    return out


def reference(
    x, l0_norm_mix, l0_mlstm_w_in, l0_mlstm_b_gates, l0_mlstm_head_norm, l0_mlstm_w_out,
    l0_norm_ffn, l0_ffn_w_up, l0_ffn_conv_w, l0_ffn_conv_b, l0_ffn_w_down, l1_norm_mix,
    l1_sconv_w_in, l1_sconv_conv_w, l1_sconv_conv_b, l1_sconv_w_out, l1_norm_ffn, l1_ffn_w_up,
    l1_ffn_conv_w, l1_ffn_conv_b, l1_ffn_w_down, final_norm, positions_2, e_g_in_2, e_w_in_2,
    e_g_q_a_2, e_w_q_up_2, e_g_kv_a_2, e_w_kv_up_2, e_sinks_2, e_w_out_2, o_g_in_2, o_w_in_2,
    o_b_f_2, o_w_out_2, g_final_2,
):
    x = first_block(
        x, l0_norm_mix, l0_mlstm_w_in, l0_mlstm_b_gates, l0_mlstm_head_norm, l0_mlstm_w_out,
        l0_norm_ffn, l0_ffn_w_up, l0_ffn_conv_w, l0_ffn_conv_b, l0_ffn_w_down, l1_norm_mix,
        l1_sconv_w_in, l1_sconv_conv_w, l1_sconv_conv_b, l1_sconv_w_out, l1_norm_ffn,
        l1_ffn_w_up, l1_ffn_conv_w, l1_ffn_conv_b, l1_ffn_w_down, final_norm,
    )
    return second_block(
        x, positions_2, e_g_in_2, e_w_in_2, e_g_q_a_2, e_w_q_up_2, e_g_kv_a_2, e_w_kv_up_2,
        e_sinks_2, e_w_out_2, o_g_in_2, o_w_in_2, o_b_f_2, o_w_out_2, g_final_2,
    )


_drawn_inputs = setup_inputs


def setup_inputs(seed=0):
    import zlib

    import numpy as np

    out = dict(_drawn_inputs(seed))
    spreads = {}
    factors = {'l0_mlstm_head_norm': 4.737,
     'l0_norm_ffn': 3.901,
     'l0_ffn_conv_b': 3.933,
     'e_g_in_2': 4.518,
     'e_g_q_a_2': 8.0,
     'e_g_kv_a_2': 8.0,
     'e_sinks_2': 37.152,
     'o_g_in_2': 2.677}
    for name, (base, spread) in spreads.items():
        noise = np.random.default_rng([zlib.crc32(name.encode()), seed]).standard_normal(out[name].shape)
        drawn = base * np.exp(spread * noise) if base else spread * noise
        out[name] = __import__('jax').numpy.asarray(drawn.astype(out[name].dtype))
    for name, factor in factors.items():
        out[name] = (out[name] * factor).astype(out[name].dtype)
    return out
```

```python
from contextlib import ExitStack

import concourse.bass as bass
from concourse import mybir
import numpy as np

F32 = mybir.dt.float32
F32R = mybir.dt.float32r
I32 = mybir.dt.int32
ACT = mybir.ActivationFunctionType
ALU = mybir.AluOpType
AX = mybir.AxisListType

P = 128
TOK = 1024
D = 1024
KT = D // P
HALF = TOK // 2
NT = TOK // P
EPS = 1e-6
D_FF = 2816
FT = D_FF // P
BIG = 1e30

M_HEADS, M_DQK, M_DV = 4, 128, 256
M_QK, M_V = M_HEADS * M_DQK, M_HEADS * M_DV

MLA_HEADS, MLA_NOPE, MLA_ROPE, MLA_V = 8, 64, 32, 64
MLA_DK = MLA_NOPE + MLA_ROPE
Q_RANK, KV_RANK = 256, 128
SWA_HEADS, SWA_KV, SWA_D = 8, 2, 64
FOX_HEADS, FOX_D = 16, 64

E_CQ, E_CKV = 0, Q_RANK
E_KPE = E_CKV + KV_RANK
E_QS = E_KPE + MLA_ROPE
E_KS = E_QS + SWA_HEADS * SWA_D
E_VS = E_KS + SWA_KV * SWA_D
E_GATE = E_VS + SWA_KV * SWA_D

TWO_PI_1 = 6.28125
TWO_PI_2 = float(np.float32(0.0019350051879882812))
TWO_PI_3 = float(2 * np.pi - TWO_PI_1 - TWO_PI_2)
ROUND = 12582912.0
PI_BELOW = 3.1415925

ARENA_TILES = 28
X_AT = 18


C_IDENT, C_ONES, C_CAUSAL, C_LATER, C_SWA = 0, 128, 256, 384, 512
C_SLOPE = C_SWA + 512
C_ONEHOT = C_SLOPE + SWA_HEADS
C_FREQ = C_ONEHOT + 16
C_SIGN = C_FREQ + 1
C_TOTAL = C_SIGN + 1


def shape_constants():
    c = np.zeros((P, C_TOTAL), np.float32)
    r = np.arange(P)
    c[:, C_IDENT:C_IDENT + P] = np.eye(P)
    c[:, C_ONES:C_ONES + P] = 1
    c[:, C_CAUSAL:C_CAUSAL + P] = np.where(r[None, :] <= r[:, None], 0, -BIG)
    c[:, C_LATER:C_LATER + P] = np.where(r[:, None] <= r[None, :], 0, BIG)
    dist = P + r[:, None] - np.arange(2 * P)[None, :]
    inside = (dist >= 0) & (dist < P)
    first = inside & (np.arange(2 * P)[None, :] >= P)
    c[:, C_SWA:C_SWA + 2 * P] = np.where(first, -dist, -100 * BIG)
    c[:, C_SWA + 2 * P:C_SWA + 4 * P] = np.where(inside, -dist, -100 * BIG)
    c[:, C_SLOPE:C_SLOPE + SWA_HEADS] = 2.0 ** (-8.0 * (np.arange(SWA_HEADS) + 1.0) / SWA_HEADS)
    c[:, C_ONEHOT:C_ONEHOT + 16] = (r[:, None] % 32 == np.arange(16)[None, :]) & (r[:, None] % 32 < 16)
    inv = 1.0 / (np.float32(10000.0) ** (np.arange(0, MLA_ROPE, 2, dtype=np.float32) / MLA_ROPE))
    c[:, C_FREQ] = inv.astype(np.float32)[r % 16]
    c[:, C_SIGN] = np.where(r % 32 < 16, -1, 1)
    return c


COLS = {}
for _name, _n in (("l0_norm_mix", 8), ("l0_mlstm_head_norm", 8), ("l0_norm_ffn", 8), ("final_norm", 8),
                  ("e_g_in_2", 8), ("e_g_q_a_2", 2), ("e_g_kv_a_2", 1), ("o_g_in_2", 8), ("g_final_2", 8),
                  ("gates", 1), ("o_b_f", 1), ("sinks", 8)):
    COLS[_name] = (sum(n for _, n in COLS.values()), _n)
N_COLS = sum(n for _, n in COLS.values())


class Tally:

    def __init__(self, sem, credit=0):
        self.sem, self.base, self.credit = sem, 0, credit

    def at(self, n):
        return self.base + n

    def passed(self, n):
        self.base += n


class Plan:

    def __init__(self, *parts):
        self.parts, self.nb = parts, len(parts)

    def n(self, i, b):
        return i * self.nb + b

    def loads(self, i, b):
        s = b % 2
        return i * (16 * sum(self.parts[s::2])) + 16 * sum(self.parts[s:b + 1:2])


class Uses:

    def __init__(self, kernel, per_turn):
        self.per_turn = per_turn
        self.free = {**dict(enumerate(kernel.free)), "t0": kernel.tfree[0], "t1": kernel.tfree[1]}

    def clear(self, eng, pair, i, use):
        t = self.free[pair]
        eng.wait_ge(t.sem, t.at(i * self.per_turn[pair] + (use + 1)))

    def over(self, eng, pair, i, use):
        t = self.free[pair]
        eng.wait_ge(t.sem, t.at(i * self.per_turn[pair] + (use + 2)))

    def passed(self, turns):
        for pair, n in self.per_turn.items():
            self.free[pair].passed(n * turns)


class Kernel:
    def __init__(self, nc, dram, ctx):
        self.nc, self.dram = nc, dram

        def sb(name, shape, dt=F32):
            return ctx.enter_context(nc.sbuf_tensor(name, shape, dt))

        self.hhi = sb("hhi", [P, KT, TOK], F32R)
        self.hlo = sb("hlo", [P, KT, TOK], F32R)
        self.whi = sb("whi", [P, 2, KT * P], F32R)
        self.wlo = sb("wlo", [P, 2, KT * P], F32R)
        self.raw = sb("raw", [P, 2, KT * P])
        self.consts = sb("consts", [P, C_TOTAL])
        self.cols = sb("cols", [P, N_COLS])
        self.conv = sb("conv", [P, FT, 8])
        self.small = sb("small", [P, 128])
        self.arena = sb("arena", [P, ARENA_TILES, TOK])
        flat = self.arena[:, :, :].rearrange("p a t -> p (a t)")
        self.flat = flat
        self.x = flat[:, X_AT * TOK:(X_AT + 8) * TOK].rearrange("p (h k c) -> p h k c", h=2, k=KT)
        self.ps = [ctx.enter_context(nc.psum_tensor(f"ps{n}", [P, TOK], F32)) for n in range(4)]
        self.ident = self.consts[:, C_IDENT:C_IDENT + P]
        self.ones = self.consts[:, C_ONES:C_ONES + P]

        def tally(name, credit=0):
            return Tally(ctx.enter_context(nc.semaphore(name)), credit)

        self.loaded = [tally("weights_loaded0"), tally("weights_loaded1")]
        self.hi_done = tally("weights_hi_done")
        self.split = tally("weights_split", 2)
        self.used = tally("weights_used", 2)
        self.free = [tally(f"pair_free{n}", 1) for n in range(4)]
        self.tfree = [tally(f"transposed_free{n}", 1) for n in range(2)]
        self.dma = [tally(f"dma{n}") for n in range(4)]
        self.dve_step = tally("dve_step")
        self.act_step = tally("act_step")
        self.pool_step = tally("pool_step")
        self.pe_step = tally("pe_step")
        self.ev = {n: tally(n) for n in (
            "squared", "summed", "scaled", "h_hi", "h_split", "evacuated", "act_split", "stored",
            "q_ready", "k_ready", "v_ready", "vt_ready", "gate_ready", "vt_done", "t_done", "t_out",
            "scores_done", "max_ready", "exp_done", "p_ready", "pv_done", "o_ready", "decay_ready",
            "sk_ready", "rows_ready", "bcast_done")}

    def col(self, name, k=0, n=1, rows=slice(0, P)):
        at = COLS[name][0] + k
        return self.cols[rows, at:at + n]

    def start_credits(self):
        with self.nc.Block() as block:
            @block.sync
            def _(sp):
                for t in (self.split, self.used, *self.free, *self.tfree):
                    if t.credit:
                        sp.sem_inc(t.sem, t.credit)
                sp.dma_start(self.consts[:, :], self.dram["consts"]).then_inc(self.dma[0].sem, 16)
                sp.dma_start(self.cols[:, :], self.dram["cols"]).then_inc(self.dma[0].sem, 16)
                sp.dma_start(self.conv[:, :, :], self.dram["conv"]).then_inc(self.dma[0].sem, 16)
                sp.wait_ge(self.dma[0].sem, 48)
        self.dma[0].passed(48)

    def load_weights(self, sp, plan, i, b, parts):
        n, s = plan.n(i, b), b % 2
        sp.wait_ge(self.split.sem, self.split.at(n + 1))
        for dst, src in parts:
            sp.dma_start(dst, src).then_inc(self.loaded[s].sem, 16)

    def slot(self, b, kt, width=P):
        return self.raw[:, b % 2, 0:kt * width].rearrange("p (k c) -> p k c", k=kt)

    def weights_hi(self, act, plan, i, b, width=KT * P):
        n, s = plan.n(i, b), b % 2
        act.wait_ge(self.loaded[s].sem, self.loaded[s].at(plan.loads(i, b)))
        act.wait_ge(self.used.sem, self.used.at(n + 1))
        act.activation(self.whi[:, s, 0:width], self.raw[:, s, 0:width], ACT.Copy).then_inc(self.hi_done.sem, 1)

    def weights_lo(self, pool, plan, i, b, width=KT * P):
        n, s = plan.n(i, b), b % 2
        pool.wait_ge(self.hi_done.sem, self.hi_done.at(n + 1))
        pool.tensor_tensor(self.wlo[:, s, 0:width], self.raw[:, s, 0:width],
                           self.whi[:, s, 0:width].bitcast(F32), ALU.subtract).then_inc(self.split.sem, 1)

    def project(self, pe, plan, i, b, out, weight_tiles, moving, m=P, last=True):
        n, s = plan.n(i, b), b % 2
        pe.wait_ge(self.split.sem, self.split.at(n + 3))
        terms = [(w, k, part) for w, k in zip(weight_tiles, moving) for part in range(3)]
        for at, (w, k, part) in enumerate(terms):
            weights = (self.wlo if part == 2 else self.whi)[:, s, w * P:w * P + m]
            for h in range(2):
                mov = (self.hlo if part == 1 else self.hhi)[:, k, h * HALF:(h + 1) * HALF]
                mm = pe.matmul(out[0:m, h * HALF:(h + 1) * HALF], weights, mov,
                               start=at == 0, stop=at == len(terms) - 1)
        if last:
            mm.then_inc(self.used.sem, 1)
        return mm

    def passed_blocks(self, plan, turns):
        for s in range(2):
            self.loaded[s].passed(16 * turns * sum(plan.parts[s::2]))
        for t in (self.hi_done, self.split, self.used):
            t.passed(turns * plan.nb)

    def weights(self, name, rows=None):
        w = self.dram[name]
        return w.rearrange("(k p) n -> p k n", p=P)

    def load_x(self):
        nc, ps, x, raw = self.nc, self.ps, self.x, self.raw
        loaded, free, pe_step = self.loaded, self.free, self.pe_step
        with nc.Block() as block:
            @block.sync
            def _(sp):
                with sp.Fori(0, NT // 2) as i:
                    for s in range(2):
                        sp.wait_ge(free[s].sem, free[s].at(i + 1))
                        sp.dma_start(raw[:, s, :], self.dram["x"][bass.ds(i * (2 * P) + s * P, P), :])\
                          .then_inc(loaded[s].sem, 16)

            @block.tensor
            def _(pe):
                with pe.Fori(0, NT // 2) as i:
                    for s in range(2):
                        pe.wait_ge(loaded[s].sem, loaded[s].at(i * 16 + 16))
                        pe.wait_ge(free[s].sem, free[s].at(i + 1))
                        for k in range(KT):
                            mm = pe.transpose(ps[s][:, k * P:(k + 1) * P], raw[:, s, k * P:(k + 1) * P], self.ident)
                        mm.then_inc(pe_step.sem, 1)

            @block.vector
            def _(dve):
                for h in range(2):
                    with dve.Fori(0, NT // 4) as i:
                        for s in range(2):
                            dve.wait_ge(pe_step.sem, pe_step.at(i * 2 + (h * NT // 2 + s + 1)))
                            dve.tensor_scalar(x[:, h, :, bass.ds(i * (2 * P) + s * P, P)],
                                              ps[s][:, :].rearrange("p (k c) -> p k c", k=KT),
                                              1.0, None, ALU.mult).then_inc(free[s].sem, 1)
        for s in range(2):
            loaded[s].passed(16 * NT // 2)
            free[s].passed(NT // 2)
        pe_step.passed(NT)

    def norm(self, gain, into_h=True, spill=True):
        nc, x, ps = self.nc, self.x, self.ps
        sq = [self.arena[:, n, :] for n in (0, 1)]
        h = [self.arena[:, n, :] for n in (2, 3)]
        total, rstd = self.arena[:, 4, :], self.arena[:, 5, :]
        halves = lambda a: a.rearrange("p (h c) -> p h c", h=2)
        squared, summed, scaled = self.ev["squared"], self.ev["summed"], self.ev["scaled"]
        h_hi, h_split, stored = self.ev["h_hi"], self.ev["h_split"], self.ev["stored"]
        step, pe_step = self.dve_step, self.pe_step
        with nc.Block() as block:
            if spill:
                @block.sync
                def _(sp):
                    sp.dma_start(self.dram["x_kept"], x).then_inc(stored.sem, 16)
                    sp.wait_ge(stored.sem, stored.at(16))

            @block.scalar
            def _(act):
                for k in range(KT):
                    if k >= 2:
                        act.wait_ge(summed.sem, summed.at(k - 1))
                    act.activation(halves(sq[k % 2]), x[:, :, k, :], ACT.Square).then_inc(squared.sem, 1)
                act.wait_ge(step.sem, step.at(2))
                act.activation(rstd, rstd, ACT.Sqrt).then_inc(self.act_step.sem, 1)
                if into_h:
                    for k in range(KT):
                        act.wait_ge(scaled.sem, scaled.at(k + 1))
                        act.activation(self.hhi[:, k, :], h[k % 2], ACT.Copy).then_inc(h_hi.sem, 1)

            @block.gpsimd
            def _(pool):
                if into_h:
                    for k in range(KT):
                        pool.wait_ge(h_hi.sem, h_hi.at(k + 1))
                        pool.tensor_tensor(self.hlo[:, k, :], h[k % 2], self.hhi[:, k, :].bitcast(F32),
                                           ALU.subtract).then_inc(h_split.sem, 1)

            @block.tensor
            def _(pe):
                pe.wait_ge(summed.sem, summed.at(KT))
                for c in range(2):
                    mm = pe.matmul(ps[0][:, c * HALF:(c + 1) * HALF], self.ones,
                                   total[:, c * HALF:(c + 1) * HALF], start=True, stop=True)
                mm.then_inc(pe_step.sem, 1)

            @block.vector
            def _(dve):
                for k in range(KT):
                    dve.wait_ge(squared.sem, squared.at(k + 1))
                    if k:
                        dve.wait_ge(summed.sem, summed.at(k))
                        dve.tensor_tensor(total, total, sq[k % 2], ALU.add).then_inc(summed.sem, 1)
                    else:
                        dve.tensor_copy(total, sq[0]).then_inc(summed.sem, 1)
                dve.wait_ge(pe_step.sem, pe_step.at(1))
                dve.tensor_scalar(rstd, ps[0][:, :], 1.0 / D, EPS, ALU.mult, ALU.add).then_inc(step.sem, 1)
                dve.wait_ge(step.sem, step.at(1))
                dve.reciprocal(rstd, rstd).then_inc(step.sem, 1)
                dve.wait_ge(self.act_step.sem, self.act_step.at(1))
                if not into_h and spill:
                    dve.wait_ge(stored.sem, stored.at(16))
                for k in range(KT):
                    if into_h and k >= 2:
                        dve.wait_ge(h_split.sem, h_split.at(k - 1))
                    out = halves(h[k % 2]) if into_h else x[:, :, k, :]
                    dve.scalar_tensor_tensor(out, x[:, :, k, :], self.col(gain, k), halves(rstd),
                                             ALU.mult, ALU.mult).then_inc(scaled.sem, 1)
        squared.passed(KT)
        summed.passed(KT)
        scaled.passed(KT)
        step.passed(2)
        self.act_step.passed(1)
        pe_step.passed(1)
        if spill:
            stored.passed(16)
        if into_h:
            h_hi.passed(KT)
            h_split.passed(KT)

    def split_o(self, block_o=0):
        with self.nc.Block() as block:
            h_hi, h_split = self.ev["h_hi"], self.ev["h_split"]

            @block.scalar
            def _(act):
                for k in range(KT):
                    act.activation(self.hhi[:, k, :], self.arena[:, k, :], ACT.Copy).then_inc(h_hi.sem, 1)

            @block.gpsimd
            def _(pool):
                for k in range(0, KT, 2):
                    pool.wait_ge(h_hi.sem, h_hi.at(k + 1))
                    pool.tensor_tensor(self.hlo[:, k, :], self.arena[:, k, :], self.hhi[:, k, :].bitcast(F32),
                                       ALU.subtract).then_inc(h_split.sem, 1)

            @block.vector
            def _(dve):
                for k in range(1, KT, 2):
                    dve.wait_ge(h_hi.sem, h_hi.at(k + 1))
                    dve.tensor_tensor(self.hlo[:, k, :], self.arena[:, k, :], self.hhi[:, k, :].bitcast(F32),
                                      ALU.subtract).then_inc(h_split.sem, 1)
        h_hi.passed(KT)
        h_split.passed(KT)

    def out_projection(self, name):
        nc, ps, x = self.nc, self.ps, self.x
        plan, turns = Plan(1, 1), KT // 2
        w = self.weights(name)
        kept = [self.arena[:, n, :].rearrange("p (h c) -> p h c", h=2) for n in (26, 27)]
        used, free, dma = self.used, self.free, self.dma
        with nc.Block() as block:
            @block.sync
            def _(sp):
                with sp.Fori(0, turns) as i:
                    for b in range(2):
                        self.load_weights(sp, plan, i, b, [(self.slot(b, KT), w[:, :, bass.ds(i * (2 * P) + b * P, P)])])
                        sp.wait_ge(free[b].sem, free[b].at(i + 1))
                        sp.dma_start(kept[b], self.dram["x_kept"][:, :, bass.ds(i * 2 + b, 1), :])\
                          .then_inc(dma[b].sem, 16)

            @block.scalar
            def _(act):
                with act.Fori(0, turns) as i:
                    for b in range(2):
                        self.weights_hi(act, plan, i, b)

            @block.gpsimd
            def _(pool):
                with pool.Fori(0, turns) as i:
                    for b in range(2):
                        self.weights_lo(pool, plan, i, b)

            @block.tensor
            def _(pe):
                with pe.Fori(0, turns) as i:
                    for b in range(2):
                        pe.wait_ge(free[b].sem, free[b].at(i + 1))
                        self.project(pe, plan, i, b, ps[b], range(KT), range(KT))

            @block.vector
            def _(dve):
                with dve.Fori(0, turns) as i:
                    for b in range(2):
                        dve.wait_ge(used.sem, used.at(plan.n(i, b) + 3))
                        dve.wait_ge(dma[b].sem, dma[b].at(i * 16 + 16))
                        dve.tensor_tensor(x[:, :, bass.ds(i * 2 + b, 1), :].rearrange("p h k c -> p h (k c)"),
                                          ps[b][:, :].rearrange("p (h c) -> p h c", h=2), kept[b], ALU.add)\
                           .then_inc(free[b].sem, 1)
        self.passed_blocks(plan, turns)
        for b in range(2):
            free[b].passed(turns)
            dma[b].passed(16 * turns)

    def store(self):
        nc, ps, x, raw = self.nc, self.ps, self.x, self.raw
        free, pe_step, dma, evac = self.free, self.pe_step, self.dma, self.ev["evacuated"]
        with nc.Block() as block:
            @block.tensor
            def _(pe):
                for t in range(NT):
                    s = t % 2
                    pe.wait_ge(free[s].sem, free[s].at(t // 2 + 1))
                    for k in range(KT):
                        mm = pe.transpose(ps[s][:, k * P:(k + 1) * P],
                                          x[:, t // 4, k, (t % 4) * P:(t % 4 + 1) * P], self.ident)
                    mm.then_inc(pe_step.sem, 1)

            @block.scalar
            def _(act):
                with act.Fori(0, NT // 2) as i:
                    for s in range(2):
                        act.wait_ge(pe_step.sem, pe_step.at(i * 2 + s + 1))
                        act.wait_ge(evac.sem, evac.at(i * 2 + s + 1))
                        act.activation(raw[:, s, :], ps[s][:, :], ACT.Copy).then_inc(free[s].sem, 1)

            @block.sync
            def _(sp):
                sp.sem_inc(evac.sem, 2)
                with sp.Fori(0, NT // 2) as i:
                    for s in range(2):
                        sp.wait_ge(free[s].sem, free[s].at(i + 2))
                        sp.dma_start(self.dram["out"][bass.ds(i * (2 * P) + s * P, P), :], raw[:, s, :])\
                          .then_inc(dma[s].sem, 16)
                        sp.wait_ge(dma[s].sem, dma[s].at(i * 16 + 16))
                        sp.sem_inc(evac.sem, 1)
        for s in range(2):
            free[s].passed(NT // 2)
            dma[s].passed(16 * NT // 2)
        pe_step.passed(NT)
        evac.passed(NT + 2)

    def gates(self, name, parts, bias):
        nc, ps = self.nc, self.ps
        plan = Plan(len(parts))
        w = self.weights(name)
        cleared, out = self.pool_step, self.ev["evacuated"]
        with nc.Block() as block:
            @block.gpsimd
            def _(pool):
                pool.memset(self.raw[:, 0, :], 0.0).then_inc(cleared.sem, 1)
                self.weights_lo(pool, plan, 0, 0)

            @block.sync
            def _(sp):
                sp.wait_ge(cleared.sem, cleared.at(1))
                self.load_weights(sp, plan, 0, 0, [(self.slot(0, KT)[:, :, at:at + n], w[:, :, c:c + n])
                                                   for at, c, n in parts])

            @block.scalar
            def _(act):
                self.weights_hi(act, plan, 0, 0)
                act.wait_ge(self.used.sem, self.used.at(3))
                act.activation(self.arena[:, 10, :], ps[0][:, :], ACT.Identity, bias=self.col(bias))\
                   .then_inc(out.sem, 1)

            @block.tensor
            def _(pe):
                self.project(pe, plan, 0, 0, ps[0], range(KT), range(KT))
        self.passed_blocks(plan, 1)
        cleared.passed(1)
        out.passed(1)

    def log_forget(self, act, dve, z, tmp, out, n):
        a, d = self.act_step, self.dve_step
        if act is not None:
            act.activation(tmp, z, ACT.Abs).then_inc(a.sem, 1)
            act.wait_ge(a.sem, a.at(1))
            act.activation(tmp, tmp, ACT.Exp, scale=-1.0).then_inc(a.sem, 1)
            act.wait_ge(a.sem, a.at(2))
            act.activation(tmp, tmp, ACT.Ln, bias=self.ones[0:n, 0:1]).then_inc(a.sem, 1)
        else:
            dve.wait_ge(a.sem, a.at(3))
            dve.scalar_tensor_tensor(out, z, 0.0, tmp, ALU.min, ALU.subtract).then_inc(d.sem, 1)

    def mlstm_rows(self):
        nc, ps = self.nc, self.ps
        n = M_HEADS
        logits, z, tmp, lf, one, f, a = (self.arena[0:n, k, :] for k in (10, 11, 12, 13, 14, 15, 16))
        row = self.arena[:, 27, :]
        d, pl, pe_step = self.dve_step, self.pool_step, self.pe_step
        ready = self.ev["rows_ready"]
        with nc.Block() as block:
            @block.gpsimd
            def _(pool):
                pool.memset(one, 1.0).then_inc(pl.sem, 1)

            @block.scalar
            def _(act):
                act.wait_ge(d.sem, d.at(1))
                self.log_forget(act, None, z, tmp, lf, n)

            @block.vector
            def _(dve):
                dve.tensor_copy(z, self.arena[32:32 + n, 10, :]).then_inc(d.sem, 1)
                self.log_forget(None, dve, z, tmp, lf, n)
                dve.wait_ge(d.sem, d.at(2))
                dve.wait_ge(pl.sem, pl.at(1))
                dve.tensor_tensor_scan(f, one, lf, 0.0, ALU.mult, ALU.add).then_inc(d.sem, 1)
                dve.wait_ge(d.sem, d.at(3))
                dve.tensor_tensor(a, logits, f, ALU.subtract).then_inc(d.sem, 1)
                dve.wait_ge(d.sem, d.at(4))
                dve.tensor_tensor_scan(row[0:n, :], a, a, 0.0, ALU.max, ALU.max).then_inc(d.sem, 1)
                dve.wait_ge(d.sem, d.at(5))
                dve.scalar_tensor_tensor(row[96:96 + n, :], f, -1.0, row[0:n, :], ALU.mult, ALU.subtract)\
                   .then_inc(d.sem, 1)
                dve.wait_ge(pe_step.sem, pe_step.at(1))
                dve.tensor_copy(self.small[:, 8:8 + NT * n], ps[1][:, 0:NT * n]).then_inc(ready.sem, 1)

            @block.tensor
            def _(pe):
                pe.wait_ge(d.sem, d.at(4))
                for t in range(NT):
                    mm = pe.transpose(ps[1][:, t * n:(t + 1) * n], a[:, t * P:(t + 1) * P], self.ident[0:n, 0:n])
                mm.then_inc(pe_step.sem, 1)
        d.passed(6)
        self.act_step.passed(3)
        pl.passed(1)
        pe_step.passed(1)
        ready.passed(1)

    def mlstm_heads(self):
        nc, ps, A = self.nc, self.ps, self.arena
        w = self.weights("l0_mlstm_w_in")
        plan, turns = Plan(1, 1, 1, 1, 1, 1), M_HEADS
        used, free, tfree = self.used, self.free, self.tfree
        O = A[:, 0:8, :]
        SSQ = A[:, 8:12, :]
        q, k = A[:, 19, :], A[:, 20, :]
        E = [A[:, 21, :], A[:, 22, :]]
        VT = E
        OG = [A[:, 23, :], A[:, 24, :]]
        MB, EM = A[:, 25, :], A[:, 26, :]
        V = self.flat[:, 17 * TOK:19 * TOK].rearrange("p (t v) -> p t v", t=NT)
        rows = A[:, 27, :]
        AB = E[0]
        HT = [MB, E[1]]
        sk_at = [12 * TOK + sum(TOK - P * r for r in range(s)) - P * s for s in range(NT)]
        sk = [self.flat[:, at:at + TOK] for at in sk_at]
        masked = [self.flat[:, 16896 + n * P:16896 + (n + 1) * P] for n in range(2)]
        a_cols = self.small[:, 8:8 + NT * M_HEADS].rearrange("p (t h) -> p t h", h=M_HEADS)
        a_head, gain = self.small[:, 40:48], self.small[:, 48:50]
        ev = self.ev
        v_turned, picked, bcast = ev["vt_done"], ev["rows_ready"], ev["bcast_done"]
        scores, decay, masked_ready = ev["scores_done"], ev["exp_done"], ev["max_ready"]
        sums, absd, squared, head_done = ev["pv_done"], ev["p_ready"], ev["squared"], ev["o_ready"]
        step = self.dve_step
        STEPS = 9
        uses = Uses(self, {0: 8, 1: 7, 3: 3, "t0": 3, "t1": 3})
        columns = (lambda i: i * M_DQK, lambda i: i * M_DQK + M_QK,
                   lambda i: i * M_DV + 2 * M_QK, lambda i: i * M_DV + (2 * M_QK + P),
                   lambda i: i * M_DV + (2 * M_QK + M_V), lambda i: i * M_DV + (2 * M_QK + M_V + P))

        def num_bank(th, n):
            return (ps[2] if th == 0 else ps[0])[:, n * HALF:(n + 1) * HALF]

        with nc.Block() as block:
            @block.sync
            def _(sp):
                with sp.Fori(0, turns) as i:
                    for b in range(6):
                        self.load_weights(sp, plan, i, b, [(self.slot(b, KT), w[:, :, bass.ds(columns[b](i), P)])])

            @block.gpsimd
            def _(pool):
                with pool.Fori(0, turns) as i:
                    for b in range(6):
                        self.weights_lo(pool, plan, i, b)

            @block.tensor
            def _(pe):
                with pe.Fori(0, turns) as i:
                    for b in range(6):
                        uses.clear(pe, b % 2, i, b // 2)
                        self.project(pe, plan, i, b, ps[b % 2], range(KT), range(KT))
                        if b < 4:
                            continue
                        dv = b - 4
                        uses.over(pe, dv, i, 1)
                        for g in range(2):
                            uses.clear(pe, f"t{g}", i, dv)
                            for t in range(4):
                                mm = pe.transpose(ps[2][:, g * HALF + t * P:g * HALF + (t + 1) * P],
                                                  VT[dv][:, (g * 4 + t) * P:(g * 4 + t + 1) * P], self.ident)
                            mm.then_inc(v_turned.sem, 1)
                    for r in range(2):
                        pe.wait_ge(picked.sem, picked.at(i * 2 + (r + 1)))
                        uses.clear(pe, 3, i, r)
                        at = 64 if r else 32
                        for c in range(2):
                            mm = pe.matmul(ps[3][:, c * HALF:(c + 1) * HALF], self.ones[at:at + M_HEADS, :],
                                           rows[at:at + M_HEADS, c * HALF:(c + 1) * HALF], start=True, stop=True)
                        mm.then_inc(bcast.sem, 1)
                    uses.over(pe, 0, i, 0)
                    uses.over(pe, 1, i, 0)
                    for s in range(NT):
                        uses.clear(pe, s % 2, i, 3 + s // 2)
                        for lo, hi in ((s * P, HALF), (max(s * P, HALF), TOK)):
                            if lo < hi:
                                mm = pe.matmul(ps[s % 2][:, lo:hi], k[:, s * P:(s + 1) * P], q[:, lo:hi],
                                               start=True, stop=True)
                        mm.then_inc(scores.sem, 1)
                    for g in range(2):
                        uses.over(pe, f"t{g}", i, 1)
                    for th in range(2):
                        if th == 0:
                            for g in range(2):
                                uses.clear(pe, f"t{g}", i, 2)
                            uses.clear(pe, 3, i, 2)
                        else:
                            uses.clear(pe, 0, i, 7)
                        tiles = 4 * (th + 1)
                        for n in range(3):
                            for s in range(tiles):
                                if n == 0:
                                    uses.over(pe, s % 2, i, 3 + s // 2)
                                lo = max(s * P, th * HALF)
                                out = num_bank(th, n) if n < 2 else ps[3][:, th * HALF:(th + 1) * HALF]
                                mm = pe.matmul(out[:, lo - th * HALF:HALF],
                                               V[:, s, n * P:(n + 1) * P] if n < 2 else self.ones,
                                               sk[s][:, lo:(th + 1) * HALF], start=s == 0, stop=s == tiles - 1,
                                               skip_group_check=True)
                        mm.then_inc(sums.sem, 1)

            @block.scalar
            def _(act):
                act.sem_inc(head_done.sem, 1)
                with act.Fori(0, turns) as i:
                    self.weights_hi(act, plan, i, 0)
                    self.weights_hi(act, plan, i, 1)
                    for b in range(6):
                        if b == 2:
                            act.wait_ge(head_done.sem, head_done.at(i + 1))
                        act.wait_ge(used.sem, used.at(plan.n(i, b) + 3))
                        out, func = ((q, ACT.Copy), (k, ACT.Copy), (VT[0], ACT.Copy), (VT[1], ACT.Copy),
                                     (OG[0], ACT.Sigmoid), (OG[1], ACT.Sigmoid))[b]
                        act.activation(out, ps[b % 2][:, :], func, scale=M_DQK ** -0.5 if b == 0 else 1.0)\
                           .then_inc(free[b % 2].sem, 1)
                        if b + 2 < 6:
                            self.weights_hi(act, plan, i, b + 2)
                    for dv in range(2):
                        for g in range(2):
                            act.wait_ge(v_turned.sem, v_turned.at(i * 4 + (dv * 2 + g + 1)))
                            act.activation(V[:, g * 4:g * 4 + 4, dv * P:(dv + 1) * P],
                                           ps[2][:, g * HALF:(g + 1) * HALF].rearrange("p (t v) -> p t v", t=4),
                                           ACT.Copy).then_inc(tfree[g].sem, 1)
                    act.wait_ge(bcast.sem, bcast.at(i * 2 + 2))
                    act.activation(EM, ps[3][:, :], ACT.Exp).then_inc(free[3].sem, 1)
                    for s in range(NT):
                        act.wait_ge(masked_ready.sem, masked_ready.at(i * NT + (s + 1)))
                        if s >= 2:
                            uses.over(act, s % 2, i, 2 + s // 2)
                        if s < NT - 1:
                            act.activation(E[s % 2][:, (s + 1) * P:], MB[:, (s + 1) * P:], ACT.Exp, scale=-1.0,
                                           bias=a_head[:, s:s + 1])
                        act.activation(E[s % 2][:, s * P:(s + 1) * P], masked[s % 2], ACT.Exp, scale=-1.0,
                                       bias=a_head[:, s:s + 1]).then_inc(decay.sem, 1)
                    uses.over(act, 0, i, 6)
                    act.wait_ge(sums.sem, sums.at(i * 2 + 1))
                    act.activation(AB[:, 0:HALF], ps[3][:, 0:HALF], ACT.Abs).then_inc(absd.sem, 1)
                    act.wait_ge(sums.sem, sums.at(i * 2 + 2))
                    act.activation(AB[:, HALF:TOK], ps[3][:, HALF:TOK], ACT.Abs).then_inc(free[3].sem, 1)
                    uses.over(act, "t1", i, 2)
                    act.activation(EM[:, 0:HALF], HT[0][:, HALF:TOK], ACT.Square).then_inc(squared.sem, 1)
                    uses.over(act, 0, i, 7)
                    act.activation(EM[:, HALF:TOK], HT[1][:, HALF:TOK], ACT.Square).then_inc(squared.sem, 1)

            @block.vector
            def _(dve):
                with dve.Fori(0, turns) as i:
                    count = [0]

                    def done(ins):
                        count[0] += 1
                        ins.then_inc(step.sem, 1)
                        dve.wait_ge(step.sem, step.at(i * STEPS + count[0]))

                    done(dve.tensor_scalar(a_head, a_cols[:, :, bass.ds(i, 1)].rearrange("p t h -> p (t h)"),
                                           1.0, None, ALU.mult))
                    at = COLS["l0_mlstm_head_norm"][0]
                    done(dve.tensor_scalar(gain, self.cols[:, bass.ds(i * 2 + at, 2)], 1.0, None, ALU.mult))
                    for r in range(2):
                        to = 64 if r else 32
                        dve.tensor_scalar(rows[to:to + M_HEADS, :], rows[96 * r:96 * r + M_HEADS, :],
                                          self.consts[96 * r:96 * r + M_HEADS, bass.ds(i + C_ONEHOT, 1)], None,
                                          ALU.mult).then_inc(picked.sem, 1)
                    dve.wait_ge(bcast.sem, bcast.at(i * 2 + 1))
                    dve.tensor_copy(MB, ps[3][:, :]).then_inc(free[3].sem, 1)
                    uses.over(dve, 3, i, 0)

                    def mask(s):
                        dve.tensor_tensor(masked[s % 2], MB[:, s * P:(s + 1) * P],
                                          self.consts[:, C_LATER:C_LATER + P], ALU.add)\
                           .then_inc(masked_ready.sem, 1)

                    mask(0)
                    mask(1)
                    for s in range(NT):
                        dve.wait_ge(scores.sem, scores.at(i * NT + (s + 1)))
                        dve.wait_ge(decay.sem, decay.at(i * NT + (s + 1)))
                        dve.tensor_tensor(sk[s][:, s * P:], ps[s % 2][:, s * P:], E[s % 2][:, s * P:], ALU.mult)\
                           .then_inc(free[s % 2].sem, 1)
                        if s + 2 < NT:
                            mask(s + 2)
                    for th in range(2):
                        cols = slice(th * HALF, (th + 1) * HALF)
                        if th == 0:
                            dve.wait_ge(absd.sem, absd.at(i + 1))
                        else:
                            uses.over(dve, 3, i, 2)
                        done(dve.tensor_tensor(AB[:, cols], AB[:, cols], EM[:, cols], ALU.max))
                        done(dve.reciprocal(AB[:, cols], AB[:, cols]))
                        if th == 0:
                            dve.tensor_tensor(HT[0][:, 0:HALF], num_bank(0, 0), AB[:, cols], ALU.mult)\
                               .then_inc(tfree[0].sem, 1)
                            dve.tensor_tensor(HT[0][:, HALF:TOK], num_bank(0, 1), AB[:, cols], ALU.mult)\
                               .then_inc(tfree[1].sem, 1)
                            uses.over(dve, "t0", i, 2)
                            uses.over(dve, "t1", i, 2)
                        else:
                            done(dve.tensor_tensor(HT[1][:, 0:HALF], num_bank(1, 0), AB[:, cols], ALU.mult))
                            dve.tensor_tensor(HT[1][:, HALF:TOK], num_bank(1, 1), AB[:, cols], ALU.mult)\
                               .then_inc(free[0].sem, 1)
                            uses.over(dve, 0, i, 7)
                        for n in range(2):
                            out = O[:, bass.ds(i * 2 + n, 1), cols].rearrange("p f c -> p (f c)")
                            dve.scalar_tensor_tensor(out, HT[th][:, n * HALF:(n + 1) * HALF], gain[:, n:n + 1],
                                                     OG[n][:, cols], ALU.mult, ALU.mult)
                        ssq = SSQ[:, bass.ds(i, 1), cols].rearrange("p f c -> p (f c)")
                        done(dve.tensor_tensor(ssq, HT[th][:, 0:HALF], HT[th][:, 0:HALF], ALU.mult))
                        dve.wait_ge(squared.sem, squared.at(i * 2 + (th + 1)))
                        last = dve.tensor_tensor(ssq, ssq, EM[:, cols], ALU.add)
                    last.then_inc(head_done.sem, 1)
                    assert count[0] == STEPS, count
        self.passed_blocks(plan, turns)
        uses.passed(turns)
        for t, n in ((v_turned, 4), (picked, 2), (bcast, 2), (scores, NT), (decay, NT), (masked_ready, NT),
                     (sums, 2), (absd, 1), (squared, 2), (step, STEPS)):
            t.passed(turns * n)
        head_done.passed(turns + 1)

    def mlstm_norm(self):
        nc, ps, A = self.nc, self.ps, self.arena
        step, pe_step, act_step = self.dve_step, self.pe_step, self.act_step
        with nc.Block() as block:
            @block.tensor
            def _(pe):
                for h in range(M_HEADS):
                    for c in range(2):
                        mm = pe.matmul(ps[h][:, c * HALF:(c + 1) * HALF], self.ones,
                                       A[:, 8 + h, c * HALF:(c + 1) * HALF], start=True, stop=True)
                    mm.then_inc(pe_step.sem, 1)

            @block.scalar
            def _(act):
                for h in range(M_HEADS):
                    act.wait_ge(step.sem, step.at(2 * h + 2))
                    act.activation(A[:, 8 + h, :], A[:, 8 + h, :], ACT.Sqrt).then_inc(act_step.sem, 1)

            @block.vector
            def _(dve):
                for h in range(M_HEADS):
                    r = A[:, 8 + h, :]
                    dve.wait_ge(pe_step.sem, pe_step.at(h + 1))
                    dve.tensor_scalar(r, ps[h][:, :], 1.0 / M_DV, EPS, ALU.mult, ALU.add).then_inc(step.sem, 1)
                    dve.wait_ge(step.sem, step.at(2 * h + 1))
                    dve.reciprocal(r, r).then_inc(step.sem, 1)
                for h in range(M_HEADS):
                    dve.wait_ge(act_step.sem, act_step.at(h + 1))
                    for n in range(2):
                        dve.tensor_tensor(A[:, 2 * h + n, :], A[:, 2 * h + n, :], A[:, 8 + h, :], ALU.mult)
        step.passed(8)
        pe_step.passed(4)
        act_step.passed(4)

    def ffn_up(self):
        nc, ps = self.nc, self.ps
        plan, turns = Plan(1, 1), FT
        w = self.weights("l0_ffn_w_up")
        act_t = self.flat[:, 0:FT * TOK].rearrange("p (h f c) -> p h f c", h=2, f=FT)
        conv_out = [self.arena[:, FT + n, :] for n in range(2)]
        gate, prod = self.arena[:, FT + 2, :], self.arena[:, FT + 3, :]
        taps = self.small[:, 0:8]
        halves = lambda a: a.rearrange("p (h c) -> p h c", h=2)
        used, free = self.used, self.free
        start, gated, taps_ready = (self.ev[n] for n in ("squared", "scaled", "h_hi"))
        written, step = self.ev["act_split"], self.dve_step
        with nc.Block() as block:
            @block.sync
            def _(sp):
                with sp.Fori(0, turns) as i:
                    for b in range(2):
                        self.load_weights(sp, plan, i, b, [(self.slot(b, KT), w[:, :, bass.ds(i * P + b * D_FF, P)])])

            @block.gpsimd
            def _(pool):
                with pool.Fori(0, turns) as i:
                    for b in range(2):
                        self.weights_lo(pool, plan, i, b)

            @block.tensor
            def _(pe):
                with pe.Fori(0, turns) as i:
                    for b in range(2):
                        pe.wait_ge(free[b].sem, free[b].at(i + 1))
                        self.project(pe, plan, i, b, ps[b], range(KT), range(KT))

            @block.scalar
            def _(act):
                act.sem_inc(written.sem, 1)
                with act.Fori(0, turns) as i:
                    for b in range(2):
                        self.weights_hi(act, plan, i, b)
                    for b in range(2):
                        act.wait_ge(used.sem, used.at(plan.n(i, b) + 3))
                        act.wait_ge(taps_ready.sem, taps_ready.at(i + 1))
                        if b == 0:
                            act.wait_ge(written.sem, written.at(i + 1))
                        act.activation(conv_out[b], ps[b][:, :], ACT.Identity, scale=taps[:, b * 4 + 2:b * 4 + 3],
                                       bias=taps[:, b * 4 + 3:b * 4 + 4]).then_inc(start.sem, 1)
                    act.wait_ge(free[0].sem, free[0].at(i + 2))
                    act.activation(gate, conv_out[0], ACT.Sigmoid).then_inc(gated.sem, 1)

            @block.vector
            def _(dve):
                with dve.Fori(0, turns) as i:
                    dve.wait_ge(written.sem, written.at(i + 1))
                    dve.tensor_scalar(taps, self.conv[:, bass.ds(i, 1), :].rearrange("p f c -> p (f c)"),
                                      1.0, None, ALU.mult).then_inc(taps_ready.sem, 1)
                    dve.wait_ge(taps_ready.sem, taps_ready.at(i + 1))
                    for b in range(2):
                        dve.wait_ge(start.sem, start.at(i * 2 + b + 1))
                        dve.scalar_tensor_tensor(conv_out[b][:, 1:TOK], ps[b][:, 0:TOK - 1], taps[:, b * 4 + 1:b * 4 + 2],
                                                 conv_out[b][:, 1:TOK], ALU.mult, ALU.add).then_inc(step.sem, 1)
                        dve.wait_ge(step.sem, step.at(i * 3 + b + 1))
                        dve.scalar_tensor_tensor(conv_out[b][:, 2:TOK], ps[b][:, 0:TOK - 2], taps[:, b * 4:b * 4 + 1],
                                                 conv_out[b][:, 2:TOK], ALU.mult, ALU.add).then_inc(free[b].sem, 1)
                        dve.wait_ge(free[b].sem, free[b].at(i + 2))
                    dve.tensor_tensor(prod, conv_out[0], conv_out[1], ALU.mult).then_inc(step.sem, 1)
                    dve.wait_ge(step.sem, step.at(i * 3 + 3))
                    dve.wait_ge(gated.sem, gated.at(i + 1))
                    dve.tensor_tensor(act_t[:, :, bass.ds(i, 1), :].rearrange("p h f c -> p h (f c)"),
                                      halves(prod), halves(gate), ALU.mult).then_inc(written.sem, 1)
        self.passed_blocks(plan, turns)
        for b in range(2):
            free[b].passed(turns)
        start.passed(2 * turns)
        gated.passed(turns)
        taps_ready.passed(turns)
        written.passed(turns + 1)
        step.passed(3 * turns)

    def ffn_down(self):
        nc, ps, x = self.nc, self.ps, self.x
        plan = Plan(1, 1)
        w = self.dram["l0_ffn_w_down"].rearrange("(f p) n -> p f n", p=P)
        act_t = self.flat[:, 0:FT * TOK].rearrange("p (h f c) -> p h f c", h=2, f=FT)
        kept = self.flat[:, 26 * TOK:28 * TOK].rearrange("p (s c) -> p s c", s=4)
        ahi, alo = self.hhi[:, 0, :].rearrange("p (s c) -> p s c", s=2), self.hlo[:, 0, :].rearrange("p (s c) -> p s c", s=2)
        used, free, dma = self.used, self.free, self.dma
        a_hi, a_split = self.ev["h_hi"], self.ev["act_split"]
        PAIRS = FT // 2

        def bank(o):
            return ps[o // 2][:, (o % 2) * HALF:(o % 2 + 1) * HALF]

        for half in (1, 0):
            with nc.Block() as block:
                @block.sync
                def _(sp):
                    with sp.Fori(0, PAIRS) as i:
                        for b in range(2):
                            self.load_weights(sp, plan, i, b, [
                                (self.raw[:, b, :], w[:, bass.ds(i * 2 + b, 1), :].rearrange("p f n -> p (f n)"))])
                    for o in range(KT):
                        if o >= 4:
                            sp.wait_ge(free[(o - 4) // 2].sem, free[(o - 4) // 2].at((o - 4) % 2 + 2))
                        sp.dma_start(kept[:, o % 4, :], self.dram["x_kept"][:, half, o, :]).then_inc(dma[o % 4].sem, 16)

                @block.scalar
                def _(act):
                    with act.Fori(0, PAIRS) as i:
                        for b in range(2):
                            self.weights_hi(act, plan, i, b)

                @block.gpsimd
                def _(pool):
                    with pool.Fori(0, PAIRS) as i:
                        for b in range(2):
                            self.weights_lo(pool, plan, i, b)

                @block.tensor
                def _(pe):
                    def pair(i, first, last):
                        for b in range(2):
                            pe.wait_ge(self.split.sem, self.split.at(plan.n(i, b) + 3))
                            pe.wait_ge(a_split.sem, a_split.at(plan.n(i, b) + 1))
                            for o in range(KT):
                                for wt, mov in ((self.whi, ahi), (self.whi, alo), (self.wlo, ahi)):
                                    mm = pe.matmul(bank(o), wt[:, b, o * P:(o + 1) * P], mov[:, b, :],
                                                   start=first and b == 0 and wt is self.whi and mov is ahi,
                                                   stop=last and b == 1 and wt is self.wlo, skip_group_check=True)
                            mm.then_inc(used.sem, 1)
                    pair(0, True, False)
                    with pe.Fori(1, PAIRS - 1) as i:
                        pair(i, False, False)
                    pair(PAIRS - 1, False, True)

                @block.vector
                def _(dve):
                    with dve.Fori(0, PAIRS) as i:
                        for b in range(2):
                            n = plan.n(i, b)
                            tile = act_t[:, half, bass.ds(i * 2 + b, 1), :].rearrange("p f c -> p (f c)")
                            dve.wait_ge(used.sem, used.at(n + 1))
                            dve.tensor_scalar(ahi[:, b, :], tile, 1.0, None, ALU.mult).then_inc(a_hi.sem, 1)
                            dve.wait_ge(a_hi.sem, a_hi.at(n + 1))
                            dve.tensor_tensor(alo[:, b, :], tile, ahi[:, b, :].bitcast(F32), ALU.subtract)\
                               .then_inc(a_split.sem, 1)
                    dve.wait_ge(used.sem, used.at(FT + 2))
                    for o in range(KT):
                        dve.wait_ge(dma[o % 4].sem, dma[o % 4].at(16 * (o // 4) + 16))
                        dve.tensor_tensor(x[:, half, o, :], bank(o), kept[:, o % 4, :], ALU.add)\
                           .then_inc(free[o // 2].sem, 1)
            self.passed_blocks(plan, PAIRS)
            for n in range(4):
                free[n].passed(2)
                dma[n].passed(32)
            a_hi.passed(FT)
            a_split.passed(FT)

    STEPS = 2 * NT
    Q_AT, K_AT, VT_AT, V_AT, P_AT, PT_AT = 8, 10, 12, 13, 14, 16

    def attention_buffers(self):
        A = self.arena
        self.Q = [A[:, self.Q_AT + a, :] for a in range(2)]
        self.K = [A[:, self.K_AT + a, :] for a in range(2)]
        self.VT = A[:, self.VT_AT, :]
        self.V = A[:, self.V_AT, :].rearrange("p (t v) -> p t v", t=NT)
        self.probs = [A[:, self.P_AT + n, :] for n in range(2)]
        at = self.PT_AT * TOK
        self.probs_t = [self.flat[:, at:at + 4 * HALF].rearrange("p (t c) -> p t c", t=4),
                        self.flat[:, at + 4 * HALF:at + 12 * HALF].rearrange("p (t c) -> p t c", t=8)]
        self.neg_max = self.small[:, 52:54]
        self.total = self.small[:, 54:56]
        self.inverse = self.small[:, 56:58]

    ATTEND_USES = {0: 2 + NT, 1: 2 + NT, "t0": 13, "t1": 13, 3: 4}

    @staticmethod
    def turned_before(j):
        per_head = 4 + 2 * 4
        return j // NT * per_head + j % NT + max(j % NT - 4, 0)

    def turn_v(self, pe, uses, i):
        vt_done = self.ev["vt_done"]
        for g in range(2):
            uses.clear(pe, f"t{g}", i, 0)
            for t in range(4):
                mm = pe.transpose(self.ps[2][:, g * HALF + t * P:g * HALF + (t + 1) * P],
                                  self.VT[:, (g * 4 + t) * P:(g * 4 + t + 1) * P], self.ident)
            mm.then_inc(vt_done.sem, 1)

    def take_v(self, act, i):
        vt_done = self.ev["vt_done"]
        for g in range(2):
            act.wait_ge(vt_done.sem, vt_done.at(i * 2 + (g + 1)))
            act.activation(self.V[:, g * 4:g * 4 + 4, :],
                           self.ps[2][:, g * HALF:(g + 1) * HALF].rearrange("p (t v) -> p t v", t=4),
                           ACT.Copy).then_inc(self.tfree[g].sem, 1)

    def attend_pe(self, pe, uses, i, kdim):
        ev, ps = self.ev, self.ps
        scores, t_done, pv_done, p_ready = (ev[n] for n in ("scores_done", "t_done", "pv_done", "p_ready"))

        def score(j):
            a, qt = divmod(j, NT)
            uses.clear(pe, j % 2, i, 2 + j // 2)
            keys = (qt + 1) * P
            for lo in range(0, keys, HALF):
                hi = min(keys, lo + HALF)
                mm = pe.matmul(ps[j % 2][:, lo:hi], self.Q[a][0:kdim, qt * P:(qt + 1) * P],
                               self.K[a][0:kdim, lo:hi], start=True, stop=True)
            mm.then_inc(scores.sem, 1)

        def turn(j):
            qt = j % NT
            pe.wait_ge(p_ready.sem, p_ready.at(i * self.STEPS + (j + 1)))
            for c in range(qt // 4 + 1):
                n = self.turned_before(j) + c
                uses.clear(pe, f"t{n % 2}", i, 1 + n // 2)
                for t in range(c * 4, min(c * 4 + 4, qt + 1)):
                    mm = pe.transpose(ps[2][:, (n % 2) * HALF + (t % 4) * P:(n % 2) * HALF + (t % 4 + 1) * P],
                                      self.probs[j % 2][:, t * P:(t + 1) * P], self.ident)
                mm.then_inc(t_done.sem, 1)

        def outputs(a, g):
            n = 2 * a + g
            last = self.turned_before(a * NT + g * 4 + 4) - 1
            uses.over(pe, f"t{last % 2}", i, 1 + last // 2)
            pe.wait_ge(self.free[3].sem, self.free[3].at(i * 4 + n))
            for t in range(4 * g + 4):
                lo = max(t * P - g * HALF, 0)
                mm = pe.matmul(ps[3][a * 64:a * 64 + 64, g * HALF + lo:(g + 1) * HALF],
                               self.V[:, t, a * 64:a * 64 + 64], self.probs_t[g][:, t, lo:HALF],
                               start=t == 0, stop=t == 4 * g + 3, skip_group_check=True)
            mm.then_inc(pv_done.sem, 1)

        score(0)
        score(1)
        for j in range(self.STEPS):
            turn(j)
            if j + 2 < self.STEPS:
                score(j + 2)
            if j and (j - 1) % 4 == 3:
                outputs((j - 1) // NT, (j - 1) % NT // 4)
        outputs(1, 1)

    def attend_act(self, act, uses, i):
        ev, ps = self.ev, self.ps
        max_ready, t_done = ev["max_ready"], ev["t_done"]

        def exponentials(j):
            act.wait_ge(max_ready.sem, max_ready.at(i * self.STEPS + (j + 1)))
            keys = (j % NT + 1) * P
            act.activation(self.probs[j % 2][:, 0:keys], ps[j % 2][:, 0:keys], ACT.Exp,
                           bias=self.neg_max[:, j % 2:j % 2 + 1],
                           accum_out=self.total[:, j % 2:j % 2 + 1]).then_inc(self.free[j % 2].sem, 1)

        exponentials(0)
        for j in range(self.STEPS):
            if j + 1 < self.STEPS:
                exponentials(j + 1)
            qt = j % NT
            for c in range(qt // 4 + 1):
                n = self.turned_before(j) + c
                blocks = min(qt + 1 - 4 * c, 4)
                act.wait_ge(t_done.sem, t_done.at(i * 24 + (n + 1)))
                act.activation(self.probs_t[qt // 4][:, 4 * c:4 * c + blocks, (qt % 4) * P:(qt % 4 + 1) * P],
                               ps[2][:, (n % 2) * HALF:(n % 2) * HALF + blocks * P]
                               .rearrange("p (t c) -> p t c", t=blocks), ACT.Copy)\
                   .then_inc(self.tfree[n % 2].sem, 1)

    def attend_dve(self, dve, uses, i, gates):
        ev, ps, step = self.ev, self.ps, self.dve_step
        scores, max_ready, p_ready, pv_done = (ev[n] for n in ("scores_done", "max_ready", "p_ready", "pv_done"))
        masked, inverted = ev["exp_done"], ev["sk_ready"]
        O = self.arena[:, 0:8, :]

        def maximum(j):
            qt = j % NT
            s = ps[j % 2]
            dve.wait_ge(scores.sem, scores.at(i * self.STEPS + (j + 1)))
            dve.tensor_tensor(s[:, qt * P:(qt + 1) * P], s[:, qt * P:(qt + 1) * P],
                              self.consts[:, C_CAUSAL:C_CAUSAL + P], ALU.add).then_inc(masked.sem, 1)
            dve.wait_ge(masked.sem, masked.at(i * self.STEPS + (j + 1)))
            dve.tensor_reduce(self.neg_max[:, j % 2:j % 2 + 1], s[:, 0:(qt + 1) * P], AX.X, ALU.max,
                              negate=True).then_inc(max_ready.sem, 1)

        def normalise(j):
            r = self.inverse[:, j % 2:j % 2 + 1]
            uses.over(dve, j % 2, i, 2 + j // 2)
            dve.reciprocal(r, self.total[:, j % 2:j % 2 + 1]).then_inc(inverted.sem, 1)
            dve.wait_ge(inverted.sem, inverted.at(i * self.STEPS + (j + 1)))
            p = self.probs[j % 2][:, 0:(j % NT + 1) * P]
            dve.tensor_scalar(p, p, r, None, ALU.mult).then_inc(p_ready.sem, 1)

        def outputs(a, g):
            rows, cols = slice(a * 64, a * 64 + 64), slice(g * HALF, (g + 1) * HALF)
            dve.wait_ge(pv_done.sem, pv_done.at(i * 4 + (2 * a + g + 1)))
            dve.tensor_tensor(O[rows, bass.ds(i, 1), cols].rearrange("p f c -> p (f c)"), ps[3][rows, cols],
                              gates(rows, cols), ALU.mult).then_inc(self.free[3].sem, 1)

        maximum(0)
        for j in range(self.STEPS):
            if j + 1 < self.STEPS:
                maximum(j + 1)
            normalise(j)
            if j >= 2 and (j - 2) % 4 == 3:
                outputs((j - 2) // NT, (j - 2) % NT // 4)
        outputs(1, 1)

    def attend_passed(self, turns):
        for name, n in (("vt_done", 2), ("scores_done", self.STEPS), ("max_ready", self.STEPS), ("exp_done", self.STEPS),
                        ("sk_ready", self.STEPS), ("p_ready", self.STEPS), ("t_done", 24), ("pv_done", 4)):
            self.ev[name].passed(turns * n)

    def dense(self, name, column, turns, tile):
        nc, ps = self.nc, self.ps
        plan = Plan(1, 1)
        w = self.weights(name)
        free, used = self.free, self.used
        with nc.Block() as block:
            @block.sync
            def _(sp):
                with sp.Fori(0, turns) as i:
                    for b in range(2):
                        self.load_weights(sp, plan, i, b, [
                            (self.slot(b, KT), w[:, :, bass.ds(i * (2 * P) + (column + b * P), P)])])

            @block.scalar
            def _(act):
                with act.Fori(0, turns) as i:
                    for b in range(2):
                        self.weights_hi(act, plan, i, b)

            @block.gpsimd
            def _(pool):
                with pool.Fori(0, turns) as i:
                    for b in range(2):
                        self.weights_lo(pool, plan, i, b)

            @block.tensor
            def _(pe):
                with pe.Fori(0, turns) as i:
                    for b in range(2):
                        pe.wait_ge(free[b].sem, free[b].at(i + 1))
                        self.project(pe, plan, i, b, ps[b], range(KT), range(KT))

            @block.vector
            def _(dve):
                with dve.Fori(0, turns) as i:
                    for b in range(2):
                        dve.wait_ge(used.sem, used.at(plan.n(i, b) + 3))
                        dve.tensor_scalar(self.arena[:, bass.ds(i * 2 + (tile + b), 1), :].rearrange("p f c -> p (f c)"),
                                          ps[b][:, :], 1.0, None, ALU.mult).then_inc(free[b].sem, 1)
        self.passed_blocks(plan, turns)
        for b in range(2):
            free[b].passed(turns)

    def rotate(self, dve, tile, tmp, step, at):
        cos, sin = self.arena[64:96, self.ROPE_AT, :], self.arena[96:128, self.ROPE_AT, :]
        dve.tensor_tensor(tmp[64:96, :], tile[96:128, :], sin, ALU.mult).then_inc(step.sem, 1)
        dve.tensor_tensor(tile[64:96, :], tile[64:96, :], cos, ALU.mult).then_inc(step.sem, 1)
        dve.wait_ge(step.sem, at(2))
        return dve.tensor_tensor(tile[64:96, :], tile[64:96, :], tmp[64:96, :], ALU.add)

    ROPE_AT, KPE_AT, TMP_AT = 24, 25, 26

    def angles(self):
        A = self.arena
        rows = slice(64, 128)
        pos, ang, turns_, r = (A[rows, n, :] for n in (26, 27, 20, 21))
        out = A[:, self.ROPE_AT, :]
        ints = self.raw[rows, 0, :].bitcast(I32)
        d, act_step, loaded = self.dve_step, self.act_step, self.dma[0]
        half_pi = self.small[:, 60:61]
        with self.nc.Block() as block:
            @block.sync
            def _(sp):
                sp.dma_start(ints, self.dram["positions"].partition_broadcast(64)).then_inc(loaded.sem, 16)

            @block.vector
            def _(dve):
                count = [0]

                def done(ins):
                    count[0] += 1
                    ins.then_inc(d.sem, 1)
                    dve.wait_ge(d.sem, d.at(count[0]))

                done(dve.memset(half_pi, float(np.pi / 2)))
                dve.wait_ge(loaded.sem, loaded.at(16))
                done(dve.tensor_copy(pos, ints))
                done(dve.tensor_scalar(ang, pos, self.consts[rows, C_FREQ:C_FREQ + 1], None, ALU.mult))
                done(dve.tensor_scalar(turns_, ang, float(1 / (2 * np.pi)), ROUND, ALU.mult, ALU.add))
                done(dve.tensor_scalar(turns_, turns_, -ROUND, None, ALU.add))
                done(dve.scalar_tensor_tensor(r, turns_, -TWO_PI_1, ang, ALU.mult, ALU.add))
                done(dve.scalar_tensor_tensor(r, turns_, -TWO_PI_2, r, ALU.mult, ALU.add))
                done(dve.scalar_tensor_tensor(r, turns_, -TWO_PI_3, r, ALU.mult, ALU.add))
                done(dve.tensor_scalar(r, r, PI_BELOW, -PI_BELOW, ALU.min, ALU.max))
                dve.wait_ge(act_step.sem, act_step.at(3))
                dve.tensor_scalar(out[96:128, :], out[96:128, :], self.consts[96:128, C_SIGN:C_SIGN + 1], None, ALU.mult)
                assert count[0] == 9

            @block.scalar
            def _(act):
                act.wait_ge(d.sem, d.at(9))
                act.activation(out[64:96, :], r[0:32, :], ACT.Abs).then_inc(act_step.sem, 1)
                act.wait_ge(act_step.sem, act_step.at(1))
                act.activation(out[64:96, :], out[64:96, :], ACT.Sin, scale=-1.0, bias=half_pi[64:96, :])\
                   .then_inc(act_step.sem, 1)
                act.activation(out[96:128, :], r[32:64, :], ACT.Sin).then_inc(act_step.sem, 1)
        d.passed(9)
        act_step.passed(3)
        loaded.passed(16)

    def low_rank(self):
        nc, ps, A = self.nc, self.ps, self.arena
        w = self.weights("e_w_in_2")
        plan = Plan(1, 1, 1, 3)
        latent = [A[:, n, :] for n in (14, 15, 16)]
        squares = [A[:, n, :] for n in (17, 18, 19)]
        rstd = [A[:, n, :] for n in (20, 21)]
        h = latent
        kpe, tmp = A[:, self.KPE_AT, :], A[:, self.TMP_AT, :]
        used, free, step, act_step, pe_step = self.used, self.free, self.dve_step, self.act_step, self.pe_step
        out, squared, scaled = self.ev["evacuated"], self.ev["squared"], self.ev["scaled"]
        h_hi = self.ev["h_hi"]
        groups = ((0, 1), (2,))
        swap = E_KPE + MLA_ROPE // 2
        columns = [[(0, P, E_CQ)], [(0, P, E_CQ + P)], [(0, P, E_CKV)],
                   [(64, MLA_ROPE, E_KPE), (96, MLA_ROPE // 2, swap), (96 + MLA_ROPE // 2, MLA_ROPE // 2, E_KPE)]]
        with nc.Block() as block:
            @block.sync
            def _(sp):
                for b in range(4):
                    self.load_weights(sp, plan, 0, b, [(self.slot(b, KT)[:, :, at:at + n], w[:, :, c:c + n])
                                                       for at, n, c in columns[b]])

            @block.gpsimd
            def _(pool):
                for b in range(4):
                    self.weights_lo(pool, plan, 0, b)
                for k in range(3):
                    pool.wait_ge(h_hi.sem, h_hi.at(k + 1))
                    pool.tensor_tensor(self.hlo[:, k, :], h[k], self.hhi[:, k, :].bitcast(F32), ALU.subtract)

            @block.tensor
            def _(pe):
                for b in range(4):
                    if b >= 2:
                        pe.wait_ge(out.sem, out.at(b - 1))
                    self.project(pe, plan, 0, b, ps[b % 2], range(KT), range(KT))
                for g, tiles in enumerate(groups):
                    pe.wait_ge(squared.sem, squared.at(tiles[-1] + 1))
                    for c in range(2):
                        for t in tiles:
                            mm = pe.matmul(ps[2 + g][:, c * HALF:(c + 1) * HALF], self.ones,
                                           squares[t][:, c * HALF:(c + 1) * HALF],
                                           start=t == tiles[0], stop=t == tiles[-1])
                    mm.then_inc(pe_step.sem, 1)

            @block.scalar
            def _(act):
                self.weights_hi(act, plan, 0, 0)
                self.weights_hi(act, plan, 0, 1)
                for b in range(4):
                    act.wait_ge(used.sem, used.at(b + 3))
                    act.activation((latent + [kpe])[b], ps[b % 2][:, :], ACT.Copy).then_inc(out.sem, 1)
                    if b < 2:
                        self.weights_hi(act, plan, 0, b + 2)
                for t in range(3):
                    act.wait_ge(out.sem, out.at(t + 1))
                    act.activation(squares[t], latent[t], ACT.Square).then_inc(squared.sem, 1)
                for g in range(2):
                    act.wait_ge(step.sem, step.at(2 * g + 2))
                    act.activation(rstd[g], rstd[g], ACT.Sqrt).then_inc(act_step.sem, 1)
                for k in range(3):
                    act.wait_ge(scaled.sem, scaled.at(k + 1))
                    act.activation(self.hhi[:, k, :], h[k], ACT.Copy).then_inc(h_hi.sem, 1)

            @block.vector
            def _(dve):
                for g, tiles in enumerate(groups):
                    dve.wait_ge(pe_step.sem, pe_step.at(g + 1))
                    dve.tensor_scalar(rstd[g], ps[2 + g][:, :], 1.0 / (P * len(tiles)), EPS, ALU.mult, ALU.add)\
                       .then_inc(step.sem, 1)
                    dve.wait_ge(step.sem, step.at(2 * g + 1))
                    dve.reciprocal(rstd[g], rstd[g]).then_inc(step.sem, 1)
                for g, tiles in enumerate(groups):
                    dve.wait_ge(act_step.sem, act_step.at(g + 1))
                    for t in tiles:
                        gain = self.col("e_g_q_a_2", t) if g == 0 else self.col("e_g_kv_a_2")
                        dve.wait_ge(squared.sem, squared.at(t + 1))
                        dve.scalar_tensor_tensor(h[t], latent[t], gain, rstd[g], ALU.mult, ALU.mult)\
                           .then_inc(scaled.sem, 1)
                dve.wait_ge(out.sem, out.at(4))
                self.rotate(dve, kpe, tmp, step, lambda n: step.at(4 + n)).then_inc(step.sem, 1)
        self.passed_blocks(plan, 1)
        out.passed(4)
        squared.passed(3)
        scaled.passed(3)
        h_hi.passed(3)
        step.passed(7)
        act_step.passed(2)
        pe_step.passed(2)

    def silu_gates(self):
        nc, ps, A = self.nc, self.ps, self.arena
        sig = [A[:, n, :] for n in (14, 15)]
        gated, used = self.ev["scaled"], self.ev["squared"]
        keys, v_tok = self.swa_buffers()
        cleared, turned, pe_step = self.pool_step, self.ev["vt_done"], self.pe_step
        with nc.Block() as block:
            @block.scalar
            def _(act):
                for k in range(KT):
                    if k >= 2:
                        act.wait_ge(used.sem, used.at(k - 1))
                    act.activation(sig[k % 2], A[:, k, :], ACT.Sigmoid).then_inc(gated.sem, 1)
                act.wait_ge(pe_step.sem, pe_step.at(1))
                act.activation(v_tok[:, 1:1 + NT, :], ps[0][:, :].rearrange("p (t v) -> p t v", t=NT), ACT.Copy)
                for g in range(SWA_KV):
                    act.activation(keys[g][:, P:P + TOK], A[g * 64:g * 64 + 64, 12, :], ACT.Copy)

            @block.gpsimd
            def _(pool):
                pool.memset(v_tok[:, 0, :], 0.0)
                for g in range(SWA_KV):
                    pool.memset(keys[g][:, 0:P], 0.0)

            @block.tensor
            def _(pe):
                for t in range(NT):
                    mm = pe.transpose(ps[0][:, t * P:(t + 1) * P], A[:, 13, t * P:(t + 1) * P], self.ident)
                mm.then_inc(pe_step.sem, 1)

            @block.vector
            def _(dve):
                for k in range(KT):
                    dve.wait_ge(gated.sem, gated.at(k + 1))
                    dve.tensor_tensor(A[:, k, :], A[:, k, :], sig[k % 2], ALU.mult).then_inc(used.sem, 1)
        gated.passed(KT)
        used.passed(KT)
        pe_step.passed(1)

    def swa_buffers(self):
        at = 16 * TOK
        keys = [self.flat[0:64, at + g * (P + TOK):at + (g + 1) * (P + TOK)] for g in range(SWA_KV)]
        at += SWA_KV * (P + TOK)
        return keys, self.flat[:, at:at + (NT + 1) * P].rearrange("p (t v) -> p t v", t=NT + 1)

    def sliding_window(self):
        nc, ps, A, ev = self.nc, self.ps, self.arena, self.ev
        keys, v_tok = self.swa_buffers()
        H = SWA_HEADS
        q_tiles = A[:, 8:12, :]
        q = self.flat[0:64, 20 * TOK:20 * TOK + H * P].rearrange("p (f a c) -> p f a c", f=H // 2, a=2)
        v = self.flat[:, 20 * TOK - 2 * P:20 * TOK].rearrange("p (t c) -> p t c", t=2)
        s = self.flat[:, 21 * TOK:23 * TOK].rearrange("p (h k) -> p h k", h=H)
        p_t = self.flat[:, 26 * TOK:28 * TOK].rearrange("p (t h q) -> p t h q", t=2, h=H)
        sinks = self.col("sinks", 0, H)
        top, total, sink = (self.small[:, 64 + n * H:64 + (n + 1) * H] for n in range(3))
        free, step = self.free, self.dve_step
        staged, scores, shifted, exp_done = (ev[n] for n in ("q_ready", "scores_done", "max_ready", "exp_done"))
        p_ready, t_done, t_out, pv_done = (ev[n] for n in ("p_ready", "t_done", "t_out", "pv_done"))
        turned = ev["o_ready"]
        STEPS, SCORED = 6, 4
        wide = lambda a: a.unsqueeze(2).broadcast_to((P, H, 2 * P))

        def tensor_turn(pe, i):
            pe.wait_ge(staged.sem, staged.at(i * 3 + 3))
            for h in range(H):
                if h % SCORED == 0:
                    pe.wait_ge(free[h // SCORED].sem, free[h // SCORED].at(i * (h // SCORED + 1) + 1))
                mm = pe.matmul(ps[h // SCORED][:, h % SCORED * 256:(h % SCORED + 1) * 256], q[:, h // 2, h % 2, :],
                               keys[h // SCORED][:, bass.ds(i * P, 2 * P)], start=True, stop=True)
                if h % SCORED == SCORED - 1:
                    mm.then_inc(scores.sem, 1)
            pe.wait_ge(p_ready.sem, p_ready.at(i + 1))
            for t in range(2):
                pe.wait_ge(free[2 + t].sem, free[2 + t].at(i + 1))
                for h in range(H):
                    mm = pe.transpose(ps[2 + t][:, h * P:(h + 1) * P], s[:, h, t * P:(t + 1) * P], self.ident)
                mm.then_inc(t_done.sem, 1)
            for t in range(2):
                pe.wait_ge(free[2 + t].sem, free[2 + t].at(i + 2))
            pe.wait_ge(free[1].sem, free[1].at(i * 2 + 2))
            for h in range(H):
                g = h // SCORED
                for t in range(2):
                    mm = pe.matmul(ps[1][h % 2 * 64:h % 2 * 64 + 64, h // 2 * P:(h // 2 + 1) * P],
                                   v[:, t, g * 64:g * 64 + 64], p_t[:, t, h, :], start=t == 0, stop=t == 1,
                                   skip_group_check=True)
            mm.then_inc(pv_done.sem, 1)

        def vector_turn(dve, i):
            count = [0]

            def done(ins):
                count[0] += 1
                ins.then_inc(step.sem, 1)
                dve.wait_ge(step.sem, step.at(i * STEPS + count[0]))

            for a in range(2):
                dve.tensor_scalar(q[:, :, a, :], q_tiles[a * 64:a * 64 + 64, :, bass.ds(i * P, P)], SWA_D ** -0.5, None,
                                  ALU.mult).then_inc(staged.sem, 1)
            dve.tensor_scalar(v, v_tok[:, bass.ds(i, 2), :], 1.0, None, ALU.mult).then_inc(staged.sem, 1)
            table = C_SWA + (0 if isinstance(i, int) else 2 * P)
            for h in range(H):
                if h % SCORED == 0:
                    dve.wait_ge(scores.sem, scores.at(i * 2 + (h // SCORED + 1)))
                ins = dve.scalar_tensor_tensor(s[:, h, :], self.consts[:, table:table + 2 * P],
                                               self.consts[:, C_SLOPE + h:C_SLOPE + h + 1],
                                               ps[h // SCORED][:, h % SCORED * 256:(h % SCORED + 1) * 256],
                                               ALU.mult, ALU.add)
                if h % SCORED == SCORED - 1:
                    ins.then_inc(free[h // SCORED].sem, 1)
                    dve.wait_ge(free[h // SCORED].sem, free[h // SCORED].at(i * (h // SCORED + 1) + 2))
            done(dve.tensor_reduce(top, s, AX.X, ALU.max))
            done(dve.tensor_tensor(top, top, sinks, ALU.max))
            done(dve.tensor_tensor(sink, sinks, top, ALU.subtract))
            dve.tensor_tensor(s, s, wide(top), ALU.subtract).then_inc(shifted.sem, 1)
            dve.wait_ge(exp_done.sem, exp_done.at(i * 2 + 2))
            done(dve.tensor_reduce(total, s, AX.X, ALU.add))
            done(dve.tensor_tensor(total, total, sink, ALU.add))
            done(dve.reciprocal(total, total))
            dve.tensor_tensor(s, s, wide(total), ALU.mult).then_inc(p_ready.sem, 1)
            dve.wait_ge(pv_done.sem, pv_done.at(i + 1))
            out = A[:, 4:8, bass.ds(i * P, P)]
            dve.tensor_tensor(out, ps[1][:, 0:4 * P].rearrange("p (f c) -> p f c", f=4), out, ALU.mult)\
               .then_inc(free[1].sem, 1)
            assert count[0] == STEPS

        def scalar_turn(act, i):
            act.wait_ge(shifted.sem, shifted.at(i + 1))
            act.activation(s, s, ACT.Exp).then_inc(exp_done.sem, 1)
            act.activation(sink, sink, ACT.Exp).then_inc(exp_done.sem, 1)
            for t in range(2):
                act.wait_ge(t_done.sem, t_done.at(i * 2 + (t + 1)))
                act.activation(p_t[:, t, :, :], ps[2 + t][:, :].rearrange("p (h q) -> p h q", h=H), ACT.Copy)\
                   .then_inc(free[2 + t].sem, 1)

        with nc.Block() as block:
            for program, engine in ((tensor_turn, block.tensor), (vector_turn, block.vector),
                                    (scalar_turn, block.scalar)):
                @engine
                def _(eng, program=program):
                    program(eng, 0)
                    with eng.Fori(1, NT) as i:
                        program(eng, i)
        for t, n in ((staged, 3), (scores, 2), (shifted, 1), (exp_done, 2), (p_ready, 1), (t_done, 2), (pv_done, 1),
                     (step, STEPS), (free[0], 1), (free[1], 2), (free[2], 1), (free[3], 1)):
            t.passed(n * NT)

    def mla_heads(self):
        nc, ps, ev, A = self.nc, self.ps, self.ev, self.arena
        self.attention_buffers()
        Q, K, VT = self.Q, self.K, self.VT
        wq, wkv = self.weights("e_w_q_up_2"), self.weights("e_w_kv_up_2")
        plan, turns = Plan(3, 1, 3, 1), MLA_HEADS // 2
        uses = Uses(self, self.ATTEND_USES)
        used, free = self.used, self.free
        kpe, tmp = A[:, self.KPE_AT, :], A[:, self.TMP_AT, :]
        rotated, kpe_there, step = ev["q_ready"], ev["k_ready"], ev["rows_ready"]
        swap = MLA_ROPE // 2
        KV = MLA_NOPE + MLA_V
        with nc.Block() as block:
            @block.sync
            def _(sp):
                with sp.Fori(0, turns) as i:
                    for a in range(2):
                        at = i * (2 * MLA_DK) + a * MLA_DK
                        slot = self.slot(2 * a, 2)
                        self.load_weights(sp, plan, i, 2 * a, [
                            (slot[:, :, 0:MLA_DK], wq[:, :, bass.ds(at, MLA_DK)]),
                            (slot[:, :, MLA_DK:MLA_DK + swap], wq[:, :, bass.ds(at + (MLA_NOPE + swap), swap)]),
                            (slot[:, :, MLA_DK + swap:P], wq[:, :, bass.ds(at + MLA_NOPE, swap)])])
                        self.load_weights(sp, plan, i, 2 * a + 1, [
                            (self.slot(1, 1), wkv[:, :, bass.ds(i * (2 * KV) + a * KV, KV)])])

            @block.gpsimd
            def _(pool):
                with pool.Fori(0, turns) as i:
                    for b in range(4):
                        self.weights_lo(pool, plan, i, b, P if b % 2 else 2 * P)

            @block.tensor
            def _(pe):
                with pe.Fori(0, turns) as i:
                    for b in range(4):
                        uses.clear(pe, b % 2, i, b // 2)
                        self.project(pe, plan, i, b, ps[b % 2], (0,) if b % 2 else (0, 1), (2,) if b % 2 else (0, 1))
                    uses.over(pe, 1, i, 1)
                    self.turn_v(pe, uses, i)
                    pe.wait_ge(kpe_there.sem, kpe_there.at(2))
                    pe.wait_ge(rotated.sem, rotated.at(i * 2 + 2))
                    self.attend_pe(pe, uses, i, MLA_DK)

            @block.scalar
            def _(act):
                for a in range(2):
                    act.activation(K[a][64:96, :], kpe[64:96, :], ACT.Copy).then_inc(kpe_there.sem, 1)
                with act.Fori(0, turns) as i:
                    self.weights_hi(act, plan, i, 0, 2 * P)
                    self.weights_hi(act, plan, i, 1, P)
                    for b in range(4):
                        a = b // 2
                        act.wait_ge(used.sem, used.at(plan.n(i, b) + 3))
                        if b % 2 == 0:
                            act.activation(Q[a], ps[0][:, :], ACT.Copy, scale=MLA_DK ** -0.5).then_inc(free[0].sem, 1)
                        else:
                            act.activation(K[a][0:64, :], ps[1][0:64, :], ACT.Copy)
                            act.activation(VT[a * 64:a * 64 + 64, :], ps[1][64:128, :], ACT.Copy)\
                               .then_inc(free[1].sem, 1)
                        if b < 2:
                            self.weights_hi(act, plan, i, b + 2, P if b % 2 else 2 * P)
                    self.take_v(act, i)
                    self.attend_act(act, uses, i)

            @block.vector
            def _(dve):
                O = A[:, 0:8, :]
                with dve.Fori(0, turns) as i:
                    for a in range(2):
                        uses.over(dve, 0, i, a)
                        self.rotate(dve, Q[a], tmp, step, lambda n: step.at(i * 4 + (a * 2 + n)))\
                            .then_inc(rotated.sem, 1)
                        dve.wait_ge(rotated.sem, rotated.at(i * 2 + (a + 1)))
                    self.attend_dve(dve, uses, i, lambda rows, cols: O[rows, bass.ds(i, 1), cols]
                                    .rearrange("p f c -> p (f c)"))
        self.passed_blocks(plan, turns)
        uses.passed(turns)
        self.attend_passed(turns)
        kpe_there.passed(2)
        rotated.passed(2 * turns)
        step.passed(4 * turns)

    def fox_rows(self):
        n = FOX_HEADS
        z, tmp, lf, one, lc, nlc = (self.arena[0:n, k, :] for k in (10, 11, 12, 13, 14, 15))
        d, pl, stored = self.dve_step, self.pool_step, self.ev["stored"]
        with self.nc.Block() as block:
            @block.gpsimd
            def _(pool):
                pool.memset(one, 1.0).then_inc(pl.sem, 1)

            @block.scalar
            def _(act):
                self.log_forget(act, None, z, tmp, lf, n)

            @block.vector
            def _(dve):
                self.log_forget(None, dve, z, tmp, lf, n)
                dve.wait_ge(d.sem, d.at(1))
                dve.wait_ge(pl.sem, pl.at(1))
                dve.tensor_tensor_scan(lc, one, lf, 0.0, ALU.mult, ALU.add).then_inc(d.sem, 1)
                dve.wait_ge(d.sem, d.at(2))
                dve.tensor_scalar(nlc, lc, -1.0, None, ALU.mult).then_inc(d.sem, 1)

            @block.sync
            def _(sp):
                sp.wait_ge(d.sem, d.at(2))
                sp.dma_start(self.dram["log_cum"][0], lc).then_inc(stored.sem, 16)
                sp.wait_ge(d.sem, d.at(3))
                sp.dma_start(self.dram["log_cum"][1], nlc).then_inc(stored.sem, 16)
                sp.wait_ge(stored.sem, stored.at(32))
        d.passed(3)
        pl.passed(1)
        self.act_step.passed(3)
        stored.passed(32)

    def fox_heads(self):
        nc, ps, ev = self.nc, self.ps, self.ev
        self.attention_buffers()
        Q, K, VT = self.Q, self.K, self.VT
        w = self.weights("o_w_in_2")
        plan, turns = Plan(1, 1, 1, 1), FOX_HEADS // 2
        kdim = FOX_D + 2
        gate, sig = self.arena[:, 22, :], self.arena[:, 23, :]
        starts = (0, D, 2 * D, 3 * D + FOX_HEADS)
        uses = Uses(self, self.ATTEND_USES)
        used, free, dma = self.used, self.free, self.dma
        ones_set, gated, scores = self.pool_step, ev["decay_ready"], ev["scores_done"]
        with nc.Block() as block:
            @block.sync
            def _(sp):
                sp.wait_ge(ones_set.sem, ones_set.at(4))
                with sp.Fori(0, turns) as i:
                    for b in range(4):
                        self.load_weights(sp, plan, i, b, [(self.slot(b, KT), w[:, :, bass.ds(i * P + starts[b], P)])])
                        if b == 1:
                            sp.wait_ge(scores.sem, scores.at(i * self.STEPS))
                            for a in range(2):
                                for side, tile, row in ((0, Q[a], 65), (1, K[a], 64)):
                                    sp.dma_start(tile[row:row + 1, :],
                                                 self.dram["log_cum"][side][bass.ds(i * 2 + a, 1), :])\
                                      .then_inc(dma[a].sem, 16)

            @block.gpsimd
            def _(pool):
                for tile in (*Q, *K):
                    pool.memset(tile[64:66, :], 1.0).then_inc(ones_set.sem, 1)
                with pool.Fori(0, turns) as i:
                    for b in range(4):
                        self.weights_lo(pool, plan, i, b)

            @block.tensor
            def _(pe):
                with pe.Fori(0, turns) as i:
                    for b in range(4):
                        uses.clear(pe, b % 2, i, b // 2)
                        self.project(pe, plan, i, b, ps[b % 2], range(KT), range(KT))
                    uses.over(pe, 0, i, 1)
                    self.turn_v(pe, uses, i)
                    uses.over(pe, 0, i, 0)
                    uses.over(pe, 1, i, 0)
                    for a in range(2):
                        pe.wait_ge(dma[a].sem, dma[a].at(i * 32 + 32))
                    self.attend_pe(pe, uses, i, kdim)

            @block.scalar
            def _(act):
                with act.Fori(0, turns) as i:
                    self.weights_hi(act, plan, i, 0)
                    self.weights_hi(act, plan, i, 1)
                    for b in range(4):
                        act.wait_ge(used.sem, used.at(plan.n(i, b) + 3))
                        if b == 0:
                            act.activation(Q[0][0:64, :], ps[0][0:64, :], ACT.Copy, scale=FOX_D ** -0.5)
                            act.activation(Q[1][0:64, :], ps[0][64:128, :], ACT.Copy, scale=FOX_D ** -0.5)\
                               .then_inc(free[0].sem, 1)
                        elif b == 1:
                            act.activation(K[0][0:64, :], ps[1][0:64, :], ACT.Copy)
                            act.activation(K[1][0:64, :], ps[1][64:128, :], ACT.Copy).then_inc(free[1].sem, 1)
                        elif b == 2:
                            act.activation(VT, ps[0][:, :], ACT.Copy).then_inc(free[0].sem, 1)
                        else:
                            act.activation(sig, ps[1][:, :], ACT.Sigmoid).then_inc(gated.sem, 1)
                        if b < 2:
                            self.weights_hi(act, plan, i, b + 2)
                    self.take_v(act, i)
                    self.attend_act(act, uses, i)

            @block.vector
            def _(dve):
                with dve.Fori(0, turns) as i:
                    dve.wait_ge(gated.sem, gated.at(i + 1))
                    uses.clear(dve, 3, i, 0)
                    dve.tensor_tensor(gate, ps[1][:, :], sig, ALU.mult).then_inc(free[1].sem, 1)
                    uses.over(dve, 1, i, 1)
                    self.attend_dve(dve, uses, i, lambda rows, cols: gate[rows, cols])
        self.passed_blocks(plan, turns)
        uses.passed(turns)
        self.attend_passed(turns)
        ones_set.passed(4)
        gated.passed(turns)
        for a in range(2):
            dma[a].passed(32 * turns)


def program(nc, dram):
    with ExitStack() as ctx:
        k = Kernel(nc, dram, ctx)
        k.start_credits()
        k.load_x()

        k.norm("l0_norm_mix")
        i_gate, f_gate = 2 * M_QK + 2 * M_V, 2 * M_QK + 2 * M_V + M_HEADS
        k.gates("l0_mlstm_w_in", ((0, i_gate, M_HEADS), (32, f_gate, M_HEADS)), "gates")
        k.mlstm_rows()
        k.mlstm_heads()
        k.mlstm_norm()
        k.split_o()
        k.out_projection("l0_mlstm_w_out")

        k.norm("l0_norm_ffn")
        k.ffn_up()
        k.ffn_down()
        k.norm("final_norm", into_h=False, spill=False)

        k.norm("e_g_in_2")
        k.dense("e_w_in_2", E_QS, 3, 8)
        k.dense("e_w_in_2", E_GATE, 4, 0)
        k.silu_gates()
        k.sliding_window()
        k.angles()
        k.low_rank()
        k.mla_heads()
        k.split_o()
        k.out_projection("e_w_out_2")

        k.norm("o_g_in_2")
        k.gates("o_w_in_2", ((0, 3 * D, FOX_HEADS),), "o_b_f")
        k.fox_rows()
        k.fox_heads()
        k.split_o()
        k.out_projection("o_w_out_2")

        k.norm("g_final_2", into_h=False, spill=False)
        k.store()


WEIGHTS = ["l0_mlstm_w_in", "l0_mlstm_w_out", "l0_ffn_w_up", "l0_ffn_w_down",
           "e_w_in_2", "e_w_q_up_2", "e_w_kv_up_2", "e_w_out_2", "o_w_in_2", "o_w_out_2"]


def column_layout(inputs):
    cols = np.zeros((P, N_COLS), np.float32)
    for name, (at, n) in COLS.items():
        if name in inputs and name != "o_b_f":
            cols[:, at:at + n] = np.asarray(inputs[name]).reshape(n, P).T
    gates = np.asarray(inputs["l0_mlstm_b_gates"])
    cols[0:M_HEADS, COLS["gates"][0]] = gates[:M_HEADS]
    cols[32:32 + M_HEADS, COLS["gates"][0]] = gates[M_HEADS:]
    cols[0:FOX_HEADS, COLS["o_b_f"][0]] = np.asarray(inputs["o_b_f_2"])[0]
    cols[:, COLS["sinks"][0]:COLS["sinks"][0] + SWA_HEADS] = np.asarray(inputs["e_sinks_2"])
    taps = np.concatenate([np.asarray(inputs["l0_ffn_conv_w"]), np.asarray(inputs["l0_ffn_conv_b"])[None]])
    conv = taps.reshape(4, 2, FT, P).transpose(3, 2, 1, 0).reshape(P, FT, 8)
    return cols, np.ascontiguousarray(conv)


def kernel(**inputs):
    import concourse.bacc as bacc
    from concourse.bass_utils import run_bass_kernel_spmd

    nc = bacc.Bacc("TRN2", target_bir_lowering=False, num_devices=1)
    cols, conv = column_layout(inputs)
    arrays = {"consts": shape_constants(), "cols": cols, "conv": conv,
              "x": np.asarray(inputs["x"]).reshape(TOK, D),
              "positions": np.asarray(inputs["positions_2"]).reshape(1, TOK)}
    for name in WEIGHTS:
        w = np.asarray(inputs[name])
        arrays[name] = w.reshape(w.shape[-2:])
    arrays = {name: np.ascontiguousarray(a) for name, a in arrays.items()}
    dram = {name: nc.dram_tensor(f"in_{name}", a.shape, mybir.dt.from_np(a.dtype), kind="ExternalInput").ap()
            for name, a in arrays.items()}
    dram["x_kept"] = nc.dram_tensor("x_kept", (P, 2, KT, HALF), F32, kind="Internal").ap()
    dram["log_cum"] = nc.dram_tensor("log_cum", (2, FOX_HEADS, TOK), F32, kind="Internal").ap()
    dram["out"] = nc.dram_tensor("out", (TOK, D), F32, kind="ExternalOutput").ap()
    program(nc, dram)
    done = run_bass_kernel_spmd(nc, [{f"in_{name}": a for name, a in arrays.items()}], core_ids=[0])
    return done.results[0]["out"].reshape(1, TOK, D)
```

```python
from contextlib import ExitStack

import concourse.bass as bass
from concourse import mybir
import numpy as np

F32 = mybir.dt.float32
F32R = mybir.dt.float32r
I32 = mybir.dt.int32
ACT = mybir.ActivationFunctionType
ALU = mybir.AluOpType
AX = mybir.AxisListType

P = 128
TOK = 1024
D = 1024
KT = D // P
HALF = TOK // 2
NT = TOK // P
EPS = 1e-6
D_FF = 2816
FT = D_FF // P
BIG = 1e30

M_HEADS, M_DQK, M_DV = 4, 128, 256
M_QK, M_V = M_HEADS * M_DQK, M_HEADS * M_DV

MLA_HEADS, MLA_NOPE, MLA_ROPE, MLA_V = 8, 64, 32, 64
MLA_DK = MLA_NOPE + MLA_ROPE
Q_RANK, KV_RANK = 256, 128
SWA_HEADS, SWA_KV, SWA_D = 8, 2, 64
FOX_HEADS, FOX_D = 16, 64

E_CQ, E_CKV = 0, Q_RANK
E_KPE = E_CKV + KV_RANK
E_QS = E_KPE + MLA_ROPE
E_KS = E_QS + SWA_HEADS * SWA_D
E_VS = E_KS + SWA_KV * SWA_D
E_GATE = E_VS + SWA_KV * SWA_D

TWO_PI_1 = 6.28125
TWO_PI_2 = float(np.float32(0.0019350051879882812))
TWO_PI_3 = float(2 * np.pi - TWO_PI_1 - TWO_PI_2)
ROUND = 12582912.0
PI_BELOW = 3.1415925

ORDER = [(a, qt) for a in range(2) for g in (1, 0) for qt in range(4 * g, 4 * g + 4)]
STEPS = len(ORDER)
GROUPS = STEPS // 4
TURNED = [0]
for _, _qt in ORDER:
    TURNED.append(TURNED[-1] + _qt // 4 + 1)

ARENA_TILES = 28
X_AT = 18


C_IDENT, C_ONES, C_CAUSAL, C_LATER, C_SWA = 0, 128, 256, 384, 512
C_SLOPE = C_SWA + 512
C_ONEHOT = C_SLOPE + SWA_HEADS
C_FREQ = C_ONEHOT + 16
C_SIGN = C_FREQ + 1
C_TOTAL = C_SIGN + 1


def shape_constants():
    c = np.zeros((P, C_TOTAL), np.float32)
    r = np.arange(P)
    c[:, C_IDENT:C_IDENT + P] = np.eye(P)
    c[:, C_ONES:C_ONES + P] = 1
    c[:, C_CAUSAL:C_CAUSAL + P] = np.where(r[None, :] <= r[:, None], 0, -BIG)
    c[:, C_LATER:C_LATER + P] = np.where(r[:, None] <= r[None, :], 0, BIG)
    dist = P + r[:, None] - np.arange(2 * P)[None, :]
    inside = (dist >= 0) & (dist < P)
    first = inside & (np.arange(2 * P)[None, :] >= P)
    c[:, C_SWA:C_SWA + 2 * P] = np.where(first, -dist, -100 * BIG)
    c[:, C_SWA + 2 * P:C_SWA + 4 * P] = np.where(inside, -dist, -100 * BIG)
    c[:, C_SLOPE:C_SLOPE + SWA_HEADS] = 2.0 ** (-8.0 * (np.arange(SWA_HEADS) + 1.0) / SWA_HEADS)
    c[:, C_ONEHOT:C_ONEHOT + 16] = (r[:, None] % 32 == np.arange(16)[None, :]) & (r[:, None] % 32 < 16)
    inv = 1.0 / (np.float32(10000.0) ** (np.arange(0, MLA_ROPE, 2, dtype=np.float32) / MLA_ROPE))
    c[:, C_FREQ] = inv.astype(np.float32)[r % 16]
    c[:, C_SIGN] = np.where(r % 32 < 16, -1, 1)
    return c


COLS = {}
for _name, _n in (("l0_norm_mix", 8), ("l0_mlstm_head_norm", 8), ("l0_norm_ffn", 8), ("final_norm", 8),
                  ("e_g_in_2", 8), ("e_g_q_a_2", 2), ("e_g_kv_a_2", 1), ("o_g_in_2", 8), ("g_final_2", 8),
                  ("gates", 1), ("o_b_f", 1), ("sinks", 8)):
    COLS[_name] = (sum(n for _, n in COLS.values()), _n)
N_COLS = sum(n for _, n in COLS.values())


class Tally:

    def __init__(self, sem, credit=0):
        self.sem, self.base, self.credit = sem, 0, credit

    def at(self, n):
        return self.base + n

    def passed(self, n):
        self.base += n


class Plan:

    def __init__(self, *parts):
        self.parts, self.nb = parts, len(parts)

    def n(self, i, b):
        return i * self.nb + b

    def loads(self, i, b):
        s = b % 2
        return i * (16 * sum(self.parts[s::2])) + 16 * sum(self.parts[s:b + 1:2])


class Uses:

    def __init__(self, kernel, per_turn):
        self.per_turn = per_turn
        self.free = {**dict(enumerate(kernel.free)), "t0": kernel.tfree[0], "t1": kernel.tfree[1]}

    def clear(self, eng, pair, i, use):
        t = self.free[pair]
        eng.wait_ge(t.sem, t.at(i * self.per_turn[pair] + (use + 1)))

    def over(self, eng, pair, i, use):
        t = self.free[pair]
        eng.wait_ge(t.sem, t.at(i * self.per_turn[pair] + (use + 2)))

    def passed(self, turns):
        for pair, n in self.per_turn.items():
            self.free[pair].passed(n * turns)


class Kernel:
    def __init__(self, nc, dram, ctx):
        self.nc, self.dram = nc, dram

        def sb(name, shape, dt=F32):
            return ctx.enter_context(nc.sbuf_tensor(name, shape, dt))

        self.hhi = sb("hhi", [P, KT, TOK], F32R)
        self.hlo = sb("hlo", [P, KT, TOK], F32R)
        self.whi = sb("whi", [P, 2, KT * P], F32R)
        self.wlo = sb("wlo", [P, 2, KT * P], F32R)
        self.raw = sb("raw", [P, 2, KT * P])
        self.consts = sb("consts", [P, C_TOTAL])
        self.cols = sb("cols", [P, N_COLS])
        self.conv = sb("conv", [P, FT, 8])
        self.small = sb("small", [P, 192])
        self.arena = sb("arena", [P, ARENA_TILES, TOK])
        flat = self.arena[:, :, :].rearrange("p a t -> p (a t)")
        self.flat = flat
        self.x = flat[:, X_AT * TOK:(X_AT + 8) * TOK].rearrange("p (h k c) -> p h k c", h=2, k=KT)
        self.ps = [ctx.enter_context(nc.psum_tensor(f"ps{n}", [P, TOK], F32)) for n in range(4)]
        self.ident = self.consts[:, C_IDENT:C_IDENT + P]
        self.ones = self.consts[:, C_ONES:C_ONES + P]

        def tally(name, credit=0):
            return Tally(ctx.enter_context(nc.semaphore(name)), credit)

        self.loaded = [tally("weights_loaded0"), tally("weights_loaded1")]
        self.hi_done = tally("weights_hi_done")
        self.split = tally("weights_split", 2)
        self.used = tally("weights_used", 2)
        self.free = [tally(f"pair_free{n}", 1) for n in range(4)]
        self.tfree = [tally(f"transposed_free{n}", 1) for n in range(2)]
        self.dma = [tally(f"dma{n}") for n in range(4)]
        self.dve_step = tally("dve_step")
        self.act_step = tally("act_step")
        self.pool_step = tally("pool_step")
        self.pe_step = tally("pe_step")
        self.norm_step, self.norm_root, self.norm_pe_step = (tally(n) for n in ("norm_step", "norm_root", "norm_pe_step"))
        self.ev = {n: tally(n) for n in (
            "squared", "summed", "scaled", "h_hi", "h_split", "evacuated", "act_split", "stored",
            "q_ready", "k_ready", "h_split_vector", "gated", "vt_done", "t_done", "t_out",
            "scores_done", "max_ready", "exp_done", "p_ready", "pv_done", "o_ready", "decay_ready",
            "sk_ready", "rows_ready", "bcast_done")}

    def col(self, name, k=0, n=1, rows=slice(0, P)):
        at = COLS[name][0] + k
        return self.cols[rows, at:at + n]

    def start_credits(self):
        with self.nc.Block() as block:
            @block.sync
            def _(sp):
                for t in (self.split, self.used, *self.free, *self.tfree):
                    if t.credit:
                        sp.sem_inc(t.sem, t.credit)
                sp.dma_start(self.consts[:, :], self.dram["consts"]).then_inc(self.dma[0].sem, 16)
                sp.dma_start(self.cols[:, :], self.dram["cols"]).then_inc(self.dma[0].sem, 16)
                sp.dma_start(self.conv[:, :, :], self.dram["conv"]).then_inc(self.dma[0].sem, 16)
                sp.wait_ge(self.dma[0].sem, 48)
        self.dma[0].passed(48)

    def load_weights(self, sp, plan, i, b, parts):
        n, s = plan.n(i, b), b % 2
        sp.wait_ge(self.split.sem, self.split.at(n + 1))
        for dst, src in parts:
            sp.dma_start(dst, src).then_inc(self.loaded[s].sem, 16)

    def slot(self, b, kt, width=P):
        return self.raw[:, b % 2, 0:kt * width].rearrange("p (k c) -> p k c", k=kt)

    def weights_hi(self, act, plan, i, b, width=KT * P):
        n, s = plan.n(i, b), b % 2
        act.wait_ge(self.loaded[s].sem, self.loaded[s].at(plan.loads(i, b)))
        act.wait_ge(self.used.sem, self.used.at(n + 1))
        act.activation(self.whi[:, s, 0:width], self.raw[:, s, 0:width], ACT.Copy).then_inc(self.hi_done.sem, 1)

    def weights_lo(self, pool, plan, i, b, width=KT * P):
        n, s = plan.n(i, b), b % 2
        pool.wait_ge(self.hi_done.sem, self.hi_done.at(n + 1))
        pool.tensor_tensor(self.wlo[:, s, 0:width], self.raw[:, s, 0:width],
                           self.whi[:, s, 0:width].bitcast(F32), ALU.subtract).then_inc(self.split.sem, 1)

    def project(self, pe, plan, i, b, out, weight_tiles, moving, new_h=False, kept=False):
        n, s = plan.n(i, b), b % 2
        pe.wait_ge(self.split.sem, self.split.at(n + 3))
        terms = [(w, k, part) for w, k in zip(weight_tiles, moving) for part in range(3)]
        for at, (w, k, part) in enumerate(terms):
            weights = (self.wlo if part == 2 else self.whi)[:, s, w * P:(w + 1) * P]
            if new_h and part == 0:
                self.h_tile_ready(pe, k)
            if kept and at == len(terms) - 3:
                pe.wait_ge(self.ev["stored"].sem, self.ev["stored"].at(16))
            for h in range(2):
                mov = (self.hlo if part == 1 else self.hhi)[:, k, h * HALF:(h + 1) * HALF]
                mm = pe.matmul(out[:, h * HALF:(h + 1) * HALF], weights, mov,
                               start=at == 0, stop=at == len(terms) - 1)
        mm.then_inc(self.used.sem, 1)

    def passed_blocks(self, plan, turns):
        for s in range(2):
            self.loaded[s].passed(16 * turns * sum(plan.parts[s::2]))
        for t in (self.hi_done, self.split, self.used):
            t.passed(turns * plan.nb)

    def weights(self, name, rows=None):
        w = self.dram[name]
        return w.rearrange("(k p) n -> p k n", p=P)

    def load_x(self):
        nc, ps, x, raw = self.nc, self.ps, self.x, self.raw
        loaded, free, pe_step = self.loaded, self.free, self.pe_step
        with nc.Block() as block:
            @block.sync
            def _(sp):
                with sp.Fori(0, NT // 2) as i:
                    for s in range(2):
                        sp.wait_ge(free[s].sem, free[s].at(i + 1))
                        sp.dma_start(raw[:, s, :], self.dram["x"][bass.ds(i * (2 * P) + s * P, P), :])\
                          .then_inc(loaded[s].sem, 16)

            @block.tensor
            def _(pe):
                with pe.Fori(0, NT // 2) as i:
                    for s in range(2):
                        pe.wait_ge(loaded[s].sem, loaded[s].at(i * 16 + 16))
                        pe.wait_ge(free[s].sem, free[s].at(i + 1))
                        for k in range(KT):
                            mm = pe.transpose(ps[s][:, k * P:(k + 1) * P], raw[:, s, k * P:(k + 1) * P], self.ident)
                        mm.then_inc(pe_step.sem, 1)

            @block.vector
            def _(dve):
                for h in range(2):
                    with dve.Fori(0, NT // 4) as i:
                        for s in range(2):
                            dve.wait_ge(pe_step.sem, pe_step.at(i * 2 + (h * NT // 2 + s + 1)))
                            dve.tensor_scalar(x[:, h, :, bass.ds(i * (2 * P) + s * P, P)],
                                              ps[s][:, :].rearrange("p (k c) -> p k c", k=KT),
                                              1.0, None, ALU.mult).then_inc(free[s].sem, 1)
        for s in range(2):
            loaded[s].passed(16 * NT // 2)
            free[s].passed(NT // 2)
        pe_step.passed(NT)

    def h_part(self, eng, k, source):
        h_hi, by_pool, by_vector = self.ev["h_hi"], self.ev["h_split"], self.ev["h_split_vector"]
        eng.wait_ge(h_hi.sem, h_hi.at(k + 1))
        eng.tensor_tensor(self.hlo[:, k, :], source, self.hhi[:, k, :].bitcast(F32), ALU.subtract)\
           .then_inc((by_vector if k % 2 else by_pool).sem, 1)

    def h_tile_ready(self, pe, k):
        t = self.ev["h_split_vector" if k % 2 else "h_split"]
        pe.wait_ge(t.sem, t.at(k // 2 + 1))

    def h_passed(self):
        self.ev["h_hi"].passed(KT)
        self.ev["h_split"].passed(KT // 2)
        self.ev["h_split_vector"].passed(KT // 2)

    def norm_act(self, act, into_h=True):
        squared, summed, scaled, h_hi = (self.ev[n] for n in ("squared", "summed", "scaled", "h_hi"))
        for k in range(KT):
            if k >= 2:
                act.wait_ge(summed.sem, summed.at(k - 1))
            act.activation(self.arena[:, k % 2, :].rearrange("p (h c) -> p h c", h=2), self.x[:, :, k, :], ACT.Square)\
               .then_inc(squared.sem, 1)
        r = self.small[:, 88:88 + NT]
        act.wait_ge(self.norm_step.sem, self.norm_step.at(2))
        act.activation(r, r, ACT.Sqrt).then_inc(self.norm_root.sem, 1)
        if into_h:
            for k in range(KT):
                act.wait_ge(scaled.sem, scaled.at(k + 1))
                act.activation(self.hhi[:, k, :], self.arena[:, 6 + k, :], ACT.Copy).then_inc(h_hi.sem, 1)

    def norm_pool(self, pool):
        for k in range(0, KT, 2):
            self.h_part(pool, k, self.arena[:, 6 + k, :])

    def norm_pe(self, pe):
        ps, summed, pe_step, step = self.ps, self.ev["summed"], self.norm_pe_step, self.norm_step
        total, diagonals = self.arena[:, 4, :], self.arena[:, 5, :]
        pe.wait_ge(summed.sem, summed.at(KT))
        for t in range(NT):
            mm = pe.matmul(ps[2][:, t:t + 1], total[:, t * P:(t + 1) * P], self.ones[:, 0:1], start=True, stop=True)
        mm.then_inc(pe_step.sem, 1)
        pe.wait_ge(step.sem, step.at(3))
        for c in range(2):
            mm = pe.matmul(ps[3][:, c * HALF:(c + 1) * HALF], self.ones, diagonals[:, c * HALF:(c + 1) * HALF],
                           start=True, stop=True)
        mm.then_inc(pe_step.sem, 1)

    def norm_dve(self, dve, gain, into_h=True):
        x, ps, step, pe_step = self.x, self.ps, self.norm_step, self.norm_pe_step
        squared, summed, scaled = self.ev["squared"], self.ev["summed"], self.ev["scaled"]
        total = self.arena[:, 4, :]
        r = self.small[:, 88:88 + NT]
        halves = lambda a: a.rearrange("p (h c) -> p h c", h=2)
        for k in range(KT):
            dve.wait_ge(squared.sem, squared.at(k + 1))
            if k:
                dve.wait_ge(summed.sem, summed.at(k))
                dve.tensor_tensor(total, total, self.arena[:, k % 2, :], ALU.add).then_inc(summed.sem, 1)
            else:
                dve.tensor_copy(total, self.arena[:, 0, :]).then_inc(summed.sem, 1)
        dve.wait_ge(pe_step.sem, pe_step.at(1))
        dve.tensor_scalar(r, ps[2][:, 0:NT], 1.0 / D, EPS, ALU.mult, ALU.add).then_inc(step.sem, 1)
        dve.wait_ge(step.sem, step.at(1))
        dve.reciprocal(r, r).then_inc(step.sem, 1)
        dve.wait_ge(self.norm_root.sem, self.norm_root.at(1))
        dve.tensor_tensor(self.arena[:, 5, :].rearrange("p (t c) -> p t c", t=NT),
                          self.ident.unsqueeze(1).broadcast_to((P, NT, P)),
                          r.unsqueeze(2).broadcast_to((P, NT, P)), ALU.mult).then_inc(step.sem, 1)
        dve.wait_ge(pe_step.sem, pe_step.at(2))
        for k in range(KT):
            out = halves(self.arena[:, 6 + k, :]) if into_h else x[:, :, k, :]
            dve.scalar_tensor_tensor(out, x[:, :, k, :], self.col(gain, k), halves(ps[3][:, :]),
                                     ALU.mult, ALU.mult).then_inc(scaled.sem, 1)
            if into_h and k >= 2 and k % 2 == 0:
                self.h_part(dve, k - 1, self.arena[:, 5 + k, :])
        if into_h:
            self.h_part(dve, KT - 1, self.arena[:, 5 + KT, :])

    def norm_passed(self, into_h=True):
        for name in ("squared", "summed", "scaled"):
            self.ev[name].passed(KT)
        self.norm_step.passed(3)
        self.norm_root.passed(1)
        self.norm_pe_step.passed(2)
        if into_h:
            self.h_passed()
            self.ev["stored"].passed(16)

    def keep_x(self, sp):
        sp.dma_start(self.dram["x_kept"], self.x).then_inc(self.ev["stored"].sem, 16)

    def norm(self, gain):
        with self.nc.Block() as block:
            @block.scalar
            def _(act):
                self.norm_act(act, into_h=False)

            @block.tensor
            def _(pe):
                self.norm_pe(pe)

            @block.vector
            def _(dve):
                self.norm_dve(dve, gain, into_h=False)
        self.norm_passed(into_h=False)

    def out_projection(self, name):
        nc, ps, x = self.nc, self.ps, self.x
        plan, turns = Plan(1, 1), KT // 2
        w = self.weights(name)
        kept = [self.arena[:, n, :].rearrange("p (h c) -> p h c", h=2) for n in (26, 27)]
        used, free, dma = self.used, self.free, self.dma
        with nc.Block() as block:
            @block.sync
            def _(sp):
                with sp.Fori(0, turns) as i:
                    for b in range(2):
                        self.load_weights(sp, plan, i, b, [(self.slot(b, KT), w[:, :, bass.ds(i * (2 * P) + b * P, P)])])
                        sp.wait_ge(free[b].sem, free[b].at(i + 1))
                        sp.dma_start(kept[b], self.dram["x_kept"][:, :, bass.ds(i * 2 + b, 1), :])\
                          .then_inc(dma[b].sem, 16)

            @block.scalar
            def _(act):
                for k in range(KT):
                    act.activation(self.hhi[:, k, :], self.arena[:, k, :], ACT.Copy).then_inc(self.ev["h_hi"].sem, 1)
                    if k in (2, 4):
                        self.weights_hi(act, plan, 0, k // 2 - 1)
                with act.Fori(1, turns) as i:
                    for b in range(2):
                        self.weights_hi(act, plan, i, b)

            @block.gpsimd
            def _(pool):
                for k in range(0, KT, 2):
                    self.h_part(pool, k, self.arena[:, k, :])
                    if k in (2, 4):
                        self.weights_lo(pool, plan, 0, k // 2 - 1)
                with pool.Fori(1, turns) as i:
                    for b in range(2):
                        self.weights_lo(pool, plan, i, b)

            @block.tensor
            def _(pe):
                for b in range(2):
                    self.project(pe, plan, 0, b, ps[b], range(KT), range(KT), new_h=b == 0)
                with pe.Fori(1, turns) as i:
                    for b in range(2):
                        pe.wait_ge(free[b].sem, free[b].at(i + 1))
                        self.project(pe, plan, i, b, ps[b], range(KT), range(KT))

            @block.vector
            def _(dve):
                for k in range(1, KT, 2):
                    self.h_part(dve, k, self.arena[:, k, :])
                with dve.Fori(0, turns) as i:
                    for b in range(2):
                        dve.wait_ge(used.sem, used.at(plan.n(i, b) + 3))
                        dve.wait_ge(dma[b].sem, dma[b].at(i * 16 + 16))
                        dve.tensor_tensor(x[:, :, bass.ds(i * 2 + b, 1), :].rearrange("p h k c -> p h (k c)"),
                                          ps[b][:, :].rearrange("p (h c) -> p h c", h=2), kept[b], ALU.add)\
                           .then_inc(free[b].sem, 1)
        self.passed_blocks(plan, turns)
        self.h_passed()
        for b in range(2):
            free[b].passed(turns)
            dma[b].passed(16 * turns)

    def store(self):
        nc, ps, x, raw = self.nc, self.ps, self.x, self.raw
        free, pe_step, dma, evac = self.free, self.pe_step, self.dma, self.ev["evacuated"]
        with nc.Block() as block:
            @block.tensor
            def _(pe):
                for t in range(NT):
                    s = t % 2
                    pe.wait_ge(free[s].sem, free[s].at(t // 2 + 1))
                    for k in range(KT):
                        mm = pe.transpose(ps[s][:, k * P:(k + 1) * P],
                                          x[:, t // 4, k, (t % 4) * P:(t % 4 + 1) * P], self.ident)
                    mm.then_inc(pe_step.sem, 1)

            @block.scalar
            def _(act):
                with act.Fori(0, NT // 2) as i:
                    for s in range(2):
                        act.wait_ge(pe_step.sem, pe_step.at(i * 2 + s + 1))
                        act.wait_ge(evac.sem, evac.at(i * 2 + s + 1))
                        act.activation(raw[:, s, :], ps[s][:, :], ACT.Copy).then_inc(free[s].sem, 1)

            @block.sync
            def _(sp):
                sp.sem_inc(evac.sem, 2)
                with sp.Fori(0, NT // 2) as i:
                    for s in range(2):
                        sp.wait_ge(free[s].sem, free[s].at(i + 2))
                        sp.dma_start(self.dram["out"][bass.ds(i * (2 * P) + s * P, P), :], raw[:, s, :])\
                          .then_inc(dma[s].sem, 16)
                        sp.wait_ge(dma[s].sem, dma[s].at(i * 16 + 16))
                        sp.sem_inc(evac.sem, 1)
        for s in range(2):
            free[s].passed(NT // 2)
            dma[s].passed(16 * NT // 2)
        pe_step.passed(NT)
        evac.passed(NT + 2)

    def gates(self, gain, name, parts, bias):
        nc, ps = self.nc, self.ps
        plan = Plan(len(parts))
        w = self.weights(name)
        cleared, out = self.pool_step, self.ev["evacuated"]
        with nc.Block() as block:
            @block.gpsimd
            def _(pool):
                pool.memset(self.raw[:, 0, :], 0.0).then_inc(cleared.sem, 1)
                self.weights_lo(pool, plan, 0, 0)
                self.norm_pool(pool)

            @block.sync
            def _(sp):
                self.keep_x(sp)
                sp.wait_ge(cleared.sem, cleared.at(1))
                self.load_weights(sp, plan, 0, 0, [(self.slot(0, KT)[:, :, at:at + n], w[:, :, c:c + n])
                                                   for at, c, n in parts])

            @block.scalar
            def _(act):
                self.weights_hi(act, plan, 0, 0)
                self.norm_act(act)
                act.wait_ge(self.used.sem, self.used.at(3))
                act.activation(self.arena[:, 10, :], ps[0][:, :], ACT.Identity, bias=self.col(bias))\
                   .then_inc(out.sem, 1)

            @block.tensor
            def _(pe):
                self.norm_pe(pe)
                self.project(pe, plan, 0, 0, ps[0], range(KT), range(KT), new_h=True, kept=True)

            @block.vector
            def _(dve):
                self.norm_dve(dve, gain)
        self.norm_passed()
        self.passed_blocks(plan, 1)
        cleared.passed(1)
        out.passed(1)

    def log_forget(self, act, dve, z, tmp, out, n):
        a, d = self.act_step, self.dve_step
        if act is not None:
            act.activation(tmp, z, ACT.Abs).then_inc(a.sem, 1)
            act.wait_ge(a.sem, a.at(1))
            act.activation(tmp, tmp, ACT.Exp, scale=-1.0).then_inc(a.sem, 1)
            act.wait_ge(a.sem, a.at(2))
            act.activation(tmp, tmp, ACT.Ln, bias=self.ones[0:n, 0:1]).then_inc(a.sem, 1)
        else:
            dve.wait_ge(a.sem, a.at(3))
            dve.scalar_tensor_tensor(out, z, 0.0, tmp, ALU.min, ALU.subtract).then_inc(d.sem, 1)

    def mlstm_rows(self):
        nc, ps = self.nc, self.ps
        n = M_HEADS
        logits, z, tmp, lf, one, f, a = (self.arena[0:n, k, :] for k in (10, 11, 12, 13, 14, 15, 16))
        row = self.arena[:, 27, :]
        d, pl, pe_step = self.dve_step, self.pool_step, self.pe_step
        ready = self.ev["rows_ready"]
        with nc.Block() as block:
            @block.gpsimd
            def _(pool):
                pool.memset(one, 1.0).then_inc(pl.sem, 1)

            @block.scalar
            def _(act):
                act.wait_ge(d.sem, d.at(1))
                self.log_forget(act, None, z, tmp, lf, n)

            @block.vector
            def _(dve):
                dve.tensor_copy(z, self.arena[32:32 + n, 10, :]).then_inc(d.sem, 1)
                self.log_forget(None, dve, z, tmp, lf, n)
                dve.wait_ge(d.sem, d.at(2))
                dve.wait_ge(pl.sem, pl.at(1))
                dve.tensor_tensor_scan(f, one, lf, 0.0, ALU.mult, ALU.add).then_inc(d.sem, 1)
                dve.wait_ge(d.sem, d.at(3))
                dve.tensor_tensor(a, logits, f, ALU.subtract).then_inc(d.sem, 1)
                dve.wait_ge(d.sem, d.at(4))
                dve.tensor_tensor_scan(row[0:n, :], a, a, 0.0, ALU.max, ALU.max).then_inc(d.sem, 1)
                dve.wait_ge(d.sem, d.at(5))
                dve.scalar_tensor_tensor(row[96:96 + n, :], f, -1.0, row[0:n, :], ALU.mult, ALU.subtract)\
                   .then_inc(d.sem, 1)
                dve.wait_ge(pe_step.sem, pe_step.at(1))
                dve.tensor_copy(self.small[:, 8:8 + NT * n], ps[1][:, 0:NT * n]).then_inc(ready.sem, 1)

            @block.tensor
            def _(pe):
                pe.wait_ge(d.sem, d.at(4))
                for t in range(NT):
                    mm = pe.transpose(ps[1][:, t * n:(t + 1) * n], a[:, t * P:(t + 1) * P], self.ident[0:n, 0:n])
                mm.then_inc(pe_step.sem, 1)
        d.passed(6)
        self.act_step.passed(3)
        pl.passed(1)
        pe_step.passed(1)
        ready.passed(1)

    def mlstm_heads(self):
        nc, ps, A = self.nc, self.ps, self.arena
        w = self.weights("l0_mlstm_w_in")
        plan, turns = Plan(1, 1, 1, 1, 1, 1), M_HEADS
        used, free, tfree = self.used, self.free, self.tfree
        O = A[:, 0:8, :]
        SSQ = A[:, 8:12, :]
        q, k = A[:, 19, :], A[:, 20, :]
        E = [A[:, 21, :], A[:, 22, :]]
        VT = E
        OG = [A[:, 23, :], A[:, 24, :]]
        MB, EM = A[:, 25, :], A[:, 26, :]
        V = self.flat[:, 17 * TOK:19 * TOK].rearrange("p (t v) -> p t v", t=NT)
        rows = A[:, 27, :]
        AB = E[0]
        HT = [MB, E[1]]
        sk_at = [12 * TOK + sum(TOK - P * r for r in range(s)) - P * s for s in range(NT)]
        sk = [self.flat[:, at:at + TOK] for at in sk_at]
        masked = [self.flat[:, 16896 + n * P:16896 + (n + 1) * P] for n in range(2)]
        a_cols = self.small[:, 8:8 + NT * M_HEADS].rearrange("p (t h) -> p t h", h=M_HEADS)
        a_head, gain = self.small[:, 40:48], self.small[:, 48:50]
        ev = self.ev
        v_turned, picked, bcast = ev["vt_done"], ev["rows_ready"], ev["bcast_done"]
        scores, decay, masked_ready = ev["scores_done"], ev["exp_done"], ev["max_ready"]
        sums, absd, squared, head_done = ev["pv_done"], ev["p_ready"], ev["squared"], ev["o_ready"]
        step = self.dve_step
        STEPS = 9
        uses = Uses(self, {0: 8, 1: 7, 3: 3, "t0": 3, "t1": 3})
        columns = (lambda i: i * M_DQK, lambda i: i * M_DQK + M_QK,
                   lambda i: i * M_DV + 2 * M_QK, lambda i: i * M_DV + (2 * M_QK + P),
                   lambda i: i * M_DV + (2 * M_QK + M_V), lambda i: i * M_DV + (2 * M_QK + M_V + P))

        def num_bank(th, n):
            return (ps[2] if th == 0 else ps[0])[:, n * HALF:(n + 1) * HALF]

        with nc.Block() as block:
            @block.sync
            def _(sp):
                with sp.Fori(0, turns) as i:
                    for b in range(6):
                        self.load_weights(sp, plan, i, b, [(self.slot(b, KT), w[:, :, bass.ds(columns[b](i), P)])])

            @block.gpsimd
            def _(pool):
                with pool.Fori(0, turns) as i:
                    for b in range(6):
                        self.weights_lo(pool, plan, i, b)

            @block.tensor
            def _(pe):
                with pe.Fori(0, turns) as i:
                    for b in range(6):
                        uses.clear(pe, b % 2, i, b // 2)
                        self.project(pe, plan, i, b, ps[b % 2], range(KT), range(KT))
                        if b < 4:
                            continue
                        dv = b - 4
                        uses.over(pe, dv, i, 1)
                        for g in range(2):
                            uses.clear(pe, f"t{g}", i, dv)
                            for t in range(4):
                                mm = pe.transpose(ps[2][:, g * HALF + t * P:g * HALF + (t + 1) * P],
                                                  VT[dv][:, (g * 4 + t) * P:(g * 4 + t + 1) * P], self.ident)
                            mm.then_inc(v_turned.sem, 1)
                    for r in range(2):
                        pe.wait_ge(picked.sem, picked.at(i * 2 + (r + 1)))
                        uses.clear(pe, 3, i, r)
                        at = 64 if r else 32
                        for c in range(2):
                            mm = pe.matmul(ps[3][:, c * HALF:(c + 1) * HALF], self.ones[at:at + M_HEADS, :],
                                           rows[at:at + M_HEADS, c * HALF:(c + 1) * HALF], start=True, stop=True)
                        mm.then_inc(bcast.sem, 1)
                    uses.over(pe, 0, i, 0)
                    uses.over(pe, 1, i, 0)
                    for s in range(NT):
                        uses.clear(pe, s % 2, i, 3 + s // 2)
                        for lo, hi in ((s * P, HALF), (max(s * P, HALF), TOK)):
                            if lo < hi:
                                mm = pe.matmul(ps[s % 2][:, lo:hi], k[:, s * P:(s + 1) * P], q[:, lo:hi],
                                               start=True, stop=True)
                        mm.then_inc(scores.sem, 1)
                    for g in range(2):
                        uses.over(pe, f"t{g}", i, 1)
                    for th in range(2):
                        if th == 0:
                            for g in range(2):
                                uses.clear(pe, f"t{g}", i, 2)
                            uses.clear(pe, 3, i, 2)
                        else:
                            uses.clear(pe, 0, i, 7)
                        tiles = 4 * (th + 1)
                        for n in range(3):
                            for s in range(tiles):
                                if n == 0:
                                    uses.over(pe, s % 2, i, 3 + s // 2)
                                lo = max(s * P, th * HALF)
                                out = num_bank(th, n) if n < 2 else ps[3][:, th * HALF:(th + 1) * HALF]
                                mm = pe.matmul(out[:, lo - th * HALF:HALF],
                                               V[:, s, n * P:(n + 1) * P] if n < 2 else self.ones,
                                               sk[s][:, lo:(th + 1) * HALF], start=s == 0, stop=s == tiles - 1,
                                               skip_group_check=True)
                        mm.then_inc(sums.sem, 1)

            @block.scalar
            def _(act):
                act.sem_inc(head_done.sem, 1)
                with act.Fori(0, turns) as i:
                    self.weights_hi(act, plan, i, 0)
                    self.weights_hi(act, plan, i, 1)
                    for b in range(6):
                        if b == 2:
                            act.wait_ge(head_done.sem, head_done.at(i + 1))
                        act.wait_ge(used.sem, used.at(plan.n(i, b) + 3))
                        out, func = ((q, ACT.Copy), (k, ACT.Copy), (VT[0], ACT.Copy), (VT[1], ACT.Copy),
                                     (OG[0], ACT.Sigmoid), (OG[1], ACT.Sigmoid))[b]
                        act.activation(out, ps[b % 2][:, :], func, scale=M_DQK ** -0.5 if b == 0 else 1.0)\
                           .then_inc(free[b % 2].sem, 1)
                        if b + 2 < 6:
                            self.weights_hi(act, plan, i, b + 2)
                    for dv in range(2):
                        for g in range(2):
                            act.wait_ge(v_turned.sem, v_turned.at(i * 4 + (dv * 2 + g + 1)))
                            act.activation(V[:, g * 4:g * 4 + 4, dv * P:(dv + 1) * P],
                                           ps[2][:, g * HALF:(g + 1) * HALF].rearrange("p (t v) -> p t v", t=4),
                                           ACT.Copy).then_inc(tfree[g].sem, 1)
                    act.wait_ge(bcast.sem, bcast.at(i * 2 + 2))
                    act.activation(EM, ps[3][:, :], ACT.Exp).then_inc(free[3].sem, 1)
                    for s in range(NT):
                        act.wait_ge(masked_ready.sem, masked_ready.at(i * NT + (s + 1)))
                        if s >= 2:
                            uses.over(act, s % 2, i, 2 + s // 2)
                        if s < NT - 1:
                            act.activation(E[s % 2][:, (s + 1) * P:], MB[:, (s + 1) * P:], ACT.Exp, scale=-1.0,
                                           bias=a_head[:, s:s + 1])
                        act.activation(E[s % 2][:, s * P:(s + 1) * P], masked[s % 2], ACT.Exp, scale=-1.0,
                                       bias=a_head[:, s:s + 1]).then_inc(decay.sem, 1)
                    uses.over(act, 0, i, 6)
                    act.wait_ge(sums.sem, sums.at(i * 2 + 1))
                    act.activation(AB[:, 0:HALF], ps[3][:, 0:HALF], ACT.Abs).then_inc(absd.sem, 1)
                    act.wait_ge(sums.sem, sums.at(i * 2 + 2))
                    act.activation(AB[:, HALF:TOK], ps[3][:, HALF:TOK], ACT.Abs).then_inc(free[3].sem, 1)
                    uses.over(act, "t1", i, 2)
                    act.activation(EM[:, 0:HALF], HT[0][:, HALF:TOK], ACT.Square).then_inc(squared.sem, 1)
                    uses.over(act, 0, i, 7)
                    act.activation(EM[:, HALF:TOK], HT[1][:, HALF:TOK], ACT.Square).then_inc(squared.sem, 1)

            @block.vector
            def _(dve):
                with dve.Fori(0, turns) as i:
                    count = [0]

                    def done(ins):
                        count[0] += 1
                        ins.then_inc(step.sem, 1)
                        dve.wait_ge(step.sem, step.at(i * STEPS + count[0]))

                    done(dve.tensor_scalar(a_head, a_cols[:, :, bass.ds(i, 1)].rearrange("p t h -> p (t h)"),
                                           1.0, None, ALU.mult))
                    at = COLS["l0_mlstm_head_norm"][0]
                    done(dve.tensor_scalar(gain, self.cols[:, bass.ds(i * 2 + at, 2)], 1.0, None, ALU.mult))
                    for r in range(2):
                        to = 64 if r else 32
                        dve.tensor_scalar(rows[to:to + M_HEADS, :], rows[96 * r:96 * r + M_HEADS, :],
                                          self.consts[96 * r:96 * r + M_HEADS, bass.ds(i + C_ONEHOT, 1)], None,
                                          ALU.mult).then_inc(picked.sem, 1)
                    dve.wait_ge(bcast.sem, bcast.at(i * 2 + 1))
                    dve.tensor_copy(MB, ps[3][:, :]).then_inc(free[3].sem, 1)
                    uses.over(dve, 3, i, 0)

                    def mask(s):
                        dve.tensor_tensor(masked[s % 2], MB[:, s * P:(s + 1) * P],
                                          self.consts[:, C_LATER:C_LATER + P], ALU.add)\
                           .then_inc(masked_ready.sem, 1)

                    mask(0)
                    mask(1)
                    for s in range(NT):
                        dve.wait_ge(scores.sem, scores.at(i * NT + (s + 1)))
                        dve.wait_ge(decay.sem, decay.at(i * NT + (s + 1)))
                        dve.tensor_tensor(sk[s][:, s * P:], ps[s % 2][:, s * P:], E[s % 2][:, s * P:], ALU.mult)\
                           .then_inc(free[s % 2].sem, 1)
                        if s + 2 < NT:
                            mask(s + 2)
                    for th in range(2):
                        cols = slice(th * HALF, (th + 1) * HALF)
                        if th == 0:
                            dve.wait_ge(absd.sem, absd.at(i + 1))
                        else:
                            uses.over(dve, 3, i, 2)
                        done(dve.tensor_tensor(AB[:, cols], AB[:, cols], EM[:, cols], ALU.max))
                        done(dve.reciprocal(AB[:, cols], AB[:, cols]))
                        if th == 0:
                            dve.tensor_tensor(HT[0][:, 0:HALF], num_bank(0, 0), AB[:, cols], ALU.mult)\
                               .then_inc(tfree[0].sem, 1)
                            dve.tensor_tensor(HT[0][:, HALF:TOK], num_bank(0, 1), AB[:, cols], ALU.mult)\
                               .then_inc(tfree[1].sem, 1)
                            uses.over(dve, "t0", i, 2)
                            uses.over(dve, "t1", i, 2)
                        else:
                            done(dve.tensor_tensor(HT[1][:, 0:HALF], num_bank(1, 0), AB[:, cols], ALU.mult))
                            dve.tensor_tensor(HT[1][:, HALF:TOK], num_bank(1, 1), AB[:, cols], ALU.mult)\
                               .then_inc(free[0].sem, 1)
                            uses.over(dve, 0, i, 7)
                        for n in range(2):
                            out = O[:, bass.ds(i * 2 + n, 1), cols].rearrange("p f c -> p (f c)")
                            dve.scalar_tensor_tensor(out, HT[th][:, n * HALF:(n + 1) * HALF], gain[:, n:n + 1],
                                                     OG[n][:, cols], ALU.mult, ALU.mult)
                        ssq = SSQ[:, bass.ds(i, 1), cols].rearrange("p f c -> p (f c)")
                        done(dve.tensor_tensor(ssq, HT[th][:, 0:HALF], HT[th][:, 0:HALF], ALU.mult))
                        dve.wait_ge(squared.sem, squared.at(i * 2 + (th + 1)))
                        last = dve.tensor_tensor(ssq, ssq, EM[:, cols], ALU.add)
                    last.then_inc(head_done.sem, 1)
                    assert count[0] == STEPS, count
        self.passed_blocks(plan, turns)
        uses.passed(turns)
        for t, n in ((v_turned, 4), (picked, 2), (bcast, 2), (scores, NT), (decay, NT), (masked_ready, NT),
                     (sums, 2), (absd, 1), (squared, 2), (step, STEPS)):
            t.passed(turns * n)
        head_done.passed(turns + 1)

    def mlstm_norm(self):
        nc, ps, A = self.nc, self.ps, self.arena
        step, pe_step, act_step = self.dve_step, self.pe_step, self.act_step
        r = self.small[:, 88:88 + M_HEADS * NT]
        diagonals = [A[:, 12 + h, :] for h in range(M_HEADS)]
        with nc.Block() as block:
            @block.tensor
            def _(pe):
                for h in range(M_HEADS):
                    for t in range(NT):
                        mm = pe.matmul(ps[0][:, h * NT + t:h * NT + t + 1], A[:, 8 + h, t * P:(t + 1) * P],
                                       self.ones[:, 0:1], start=True, stop=True)
                mm.then_inc(pe_step.sem, 1)
                for h in range(M_HEADS):
                    pe.wait_ge(step.sem, step.at(3 + h))
                    for c in range(2):
                        mm = pe.matmul(ps[h][:, c * HALF:(c + 1) * HALF], self.ones,
                                       diagonals[h][:, c * HALF:(c + 1) * HALF], start=True, stop=True)
                    mm.then_inc(pe_step.sem, 1)

            @block.scalar
            def _(act):
                act.wait_ge(step.sem, step.at(2))
                act.activation(r, r, ACT.Sqrt).then_inc(act_step.sem, 1)

            @block.vector
            def _(dve):
                dve.wait_ge(pe_step.sem, pe_step.at(1))
                dve.tensor_scalar(r, ps[0][:, 0:M_HEADS * NT], 1.0 / M_DV, EPS, ALU.mult, ALU.add).then_inc(step.sem, 1)
                dve.wait_ge(step.sem, step.at(1))
                dve.reciprocal(r, r).then_inc(step.sem, 1)
                dve.wait_ge(act_step.sem, act_step.at(1))

                def diagonal(h):
                    dve.tensor_tensor(diagonals[h].rearrange("p (t c) -> p t c", t=NT),
                                      self.ident.unsqueeze(1).broadcast_to((P, NT, P)),
                                      r[:, h * NT:(h + 1) * NT].unsqueeze(2).broadcast_to((P, NT, P)), ALU.mult)\
                       .then_inc(step.sem, 1)

                diagonal(0)
                for h in range(M_HEADS):
                    if h + 1 < M_HEADS:
                        diagonal(h + 1)
                    dve.wait_ge(pe_step.sem, pe_step.at(h + 2))
                    for n in range(2):
                        dve.tensor_tensor(A[:, 2 * h + n, :], A[:, 2 * h + n, :], ps[h][:, :], ALU.mult)
        step.passed(2 + M_HEADS)
        pe_step.passed(1 + M_HEADS)
        act_step.passed(1)

    def ffn_up(self, gain):
        nc, ps = self.nc, self.ps
        plan, turns = Plan(1, 1), FT
        w = self.weights("l0_ffn_w_up")
        act_t = self.flat[:, 0:FT * TOK].rearrange("p (h f c) -> p h f c", h=2, f=FT)
        conv_out = [self.arena[:, FT + n, :] for n in range(2)]
        gate, prod = self.arena[:, FT + 2, :], self.arena[:, FT + 3, :]
        taps = self.small[:, 0:8]
        halves = lambda a: a.rearrange("p (h c) -> p h c", h=2)
        used, free = self.used, self.free
        start, gated, taps_ready = (self.ev[n] for n in ("exp_done", "max_ready", "q_ready"))
        written, step = self.ev["act_split"], self.dve_step
        with nc.Block() as block:
            @block.sync
            def _(sp):
                self.keep_x(sp)
                with sp.Fori(0, turns) as i:
                    for b in range(2):
                        self.load_weights(sp, plan, i, b, [(self.slot(b, KT), w[:, :, bass.ds(i * P + b * D_FF, P)])])

            @block.gpsimd
            def _(pool):
                for b in range(2):
                    self.weights_lo(pool, plan, 0, b)
                self.norm_pool(pool)
                with pool.Fori(1, turns) as i:
                    for b in range(2):
                        self.weights_lo(pool, plan, i, b)

            @block.tensor
            def _(pe):
                self.norm_pe(pe)
                for b in range(2):
                    self.project(pe, plan, 0, b, ps[b], range(KT), range(KT), new_h=b == 0, kept=b == 0)
                with pe.Fori(1, turns) as i:
                    for b in range(2):
                        pe.wait_ge(free[b].sem, free[b].at(i + 1))
                        self.project(pe, plan, i, b, ps[b], range(KT), range(KT))

            @block.scalar
            def _(act):
                def turn(i, last=False):
                    for b in range(2):
                        if not last:
                            self.weights_hi(act, plan, i + 1, b)
                        act.wait_ge(used.sem, used.at(plan.n(i, b) + 3))
                        act.wait_ge(taps_ready.sem, taps_ready.at(i + 1))
                        if b == 0:
                            act.wait_ge(written.sem, written.at(i + 1))
                        act.activation(conv_out[b], ps[b][:, :], ACT.Identity, scale=taps[:, b * 4 + 2:b * 4 + 3],
                                       bias=taps[:, b * 4 + 3:b * 4 + 4]).then_inc(start.sem, 1)
                    act.wait_ge(free[0].sem, free[0].at(i + 2))
                    act.activation(gate, conv_out[0], ACT.Sigmoid).then_inc(gated.sem, 1)

                act.sem_inc(written.sem, 1)
                for b in range(2):
                    self.weights_hi(act, plan, 0, b)
                self.norm_act(act)
                with act.Fori(0, turns - 1) as i:
                    turn(i)
                turn(turns - 1, last=True)

            @block.vector
            def _(dve):
                self.norm_dve(dve, gain)
                with dve.Fori(0, turns) as i:
                    dve.wait_ge(written.sem, written.at(i + 1))
                    dve.tensor_scalar(taps, self.conv[:, bass.ds(i, 1), :].rearrange("p f c -> p (f c)"),
                                      1.0, None, ALU.mult).then_inc(taps_ready.sem, 1)
                    dve.wait_ge(taps_ready.sem, taps_ready.at(i + 1))
                    for b in range(2):
                        dve.wait_ge(start.sem, start.at(i * 2 + b + 1))
                        dve.scalar_tensor_tensor(conv_out[b][:, 1:TOK], ps[b][:, 0:TOK - 1], taps[:, b * 4 + 1:b * 4 + 2],
                                                 conv_out[b][:, 1:TOK], ALU.mult, ALU.add).then_inc(step.sem, 1)
                        dve.wait_ge(step.sem, step.at(i * 3 + b + 1))
                        dve.scalar_tensor_tensor(conv_out[b][:, 2:TOK], ps[b][:, 0:TOK - 2], taps[:, b * 4:b * 4 + 1],
                                                 conv_out[b][:, 2:TOK], ALU.mult, ALU.add).then_inc(free[b].sem, 1)
                        dve.wait_ge(free[b].sem, free[b].at(i + 2))
                    dve.tensor_tensor(prod, conv_out[0], conv_out[1], ALU.mult).then_inc(step.sem, 1)
                    dve.wait_ge(step.sem, step.at(i * 3 + 3))
                    dve.wait_ge(gated.sem, gated.at(i + 1))
                    dve.tensor_tensor(act_t[:, :, bass.ds(i, 1), :].rearrange("p h f c -> p h (f c)"),
                                      halves(prod), halves(gate), ALU.mult).then_inc(written.sem, 1)
        self.norm_passed()
        self.passed_blocks(plan, turns)
        for b in range(2):
            free[b].passed(turns)
        start.passed(2 * turns)
        gated.passed(turns)
        taps_ready.passed(turns)
        written.passed(turns + 1)
        step.passed(3 * turns)

    def ffn_down(self):
        nc, ps, x = self.nc, self.ps, self.x
        plan = Plan(1, 1)
        w = self.dram["l0_ffn_w_down"].rearrange("(f p) n -> p f n", p=P)
        act_t = self.flat[:, 0:FT * TOK].rearrange("p (h f c) -> p h f c", h=2, f=FT)
        kept = self.flat[:, 26 * TOK:28 * TOK].rearrange("p (s c) -> p s c", s=4)
        ahi, alo = self.hhi[:, 0, :].rearrange("p (s c) -> p s c", s=2), self.hlo[:, 0, :].rearrange("p (s c) -> p s c", s=2)
        used, free, dma = self.used, self.free, self.dma
        a_hi, a_split = self.ev["h_hi"], self.ev["act_split"]
        PAIRS = FT // 2

        def bank(o):
            return ps[o // 2][:, (o % 2) * HALF:(o % 2 + 1) * HALF]

        for half in (1, 0):
            with nc.Block() as block:
                @block.sync
                def _(sp):
                    with sp.Fori(0, PAIRS) as i:
                        for b in range(2):
                            self.load_weights(sp, plan, i, b, [
                                (self.raw[:, b, :], w[:, bass.ds(i * 2 + b, 1), :].rearrange("p f n -> p (f n)"))])
                    for o in range(KT):
                        if o >= 4:
                            sp.wait_ge(free[(o - 4) // 2].sem, free[(o - 4) // 2].at((o - 4) % 2 + 2))
                        sp.dma_start(kept[:, o % 4, :], self.dram["x_kept"][:, half, o, :]).then_inc(dma[o % 4].sem, 16)

                @block.scalar
                def _(act):
                    with act.Fori(0, PAIRS) as i:
                        for b in range(2):
                            self.weights_hi(act, plan, i, b)

                @block.gpsimd
                def _(pool):
                    with pool.Fori(0, PAIRS) as i:
                        for b in range(2):
                            self.weights_lo(pool, plan, i, b)

                @block.tensor
                def _(pe):
                    def pair(i, first, last):
                        for b in range(2):
                            pe.wait_ge(self.split.sem, self.split.at(plan.n(i, b) + 3))
                            pe.wait_ge(a_split.sem, a_split.at(plan.n(i, b) + 1))
                            for o in range(KT):
                                for wt, mov in ((self.whi, ahi), (self.whi, alo), (self.wlo, ahi)):
                                    mm = pe.matmul(bank(o), wt[:, b, o * P:(o + 1) * P], mov[:, b, :],
                                                   start=first and b == 0 and wt is self.whi and mov is ahi,
                                                   stop=last and b == 1 and wt is self.wlo, skip_group_check=True)
                            mm.then_inc(used.sem, 1)
                    pair(0, True, False)
                    with pe.Fori(1, PAIRS - 1) as i:
                        pair(i, False, False)
                    pair(PAIRS - 1, False, True)

                @block.vector
                def _(dve):
                    with dve.Fori(0, PAIRS) as i:
                        for b in range(2):
                            n = plan.n(i, b)
                            tile = act_t[:, half, bass.ds(i * 2 + b, 1), :].rearrange("p f c -> p (f c)")
                            dve.wait_ge(used.sem, used.at(n + 1))
                            dve.tensor_scalar(ahi[:, b, :], tile, 1.0, None, ALU.mult).then_inc(a_hi.sem, 1)
                            dve.wait_ge(a_hi.sem, a_hi.at(n + 1))
                            dve.tensor_tensor(alo[:, b, :], tile, ahi[:, b, :].bitcast(F32), ALU.subtract)\
                               .then_inc(a_split.sem, 1)
                    dve.wait_ge(used.sem, used.at(FT + 2))
                    for o in range(KT):
                        dve.wait_ge(dma[o % 4].sem, dma[o % 4].at(16 * (o // 4) + 16))
                        dve.tensor_tensor(x[:, half, o, :], bank(o), kept[:, o % 4, :], ALU.add)\
                           .then_inc(free[o // 2].sem, 1)
            self.passed_blocks(plan, PAIRS)
            for n in range(4):
                free[n].passed(2)
                dma[n].passed(32)
            a_hi.passed(FT)
            a_split.passed(FT)

    Q_AT, K_AT, VT_AT, V_AT, P_AT, PT_AT = 8, 10, 12, 13, 14, 16

    def attention_buffers(self):
        A = self.arena
        self.Q = [A[:, self.Q_AT + a, :] for a in range(2)]
        self.K = [A[:, self.K_AT + a, :] for a in range(2)]
        self.VT = A[:, self.VT_AT, :]
        self.V = A[:, self.V_AT, :].rearrange("p (t v) -> p t v", t=NT)
        self.probs = [A[:, self.P_AT + n, :] for n in range(2)]
        at = self.PT_AT * TOK
        self.probs_t = [self.flat[:, at:at + 4 * HALF].rearrange("p (t c) -> p t c", t=4),
                        self.flat[:, at + 4 * HALF:at + 12 * HALF].rearrange("p (t c) -> p t c", t=8)]
        self.neg_max = self.small[:, 52:54]
        self.total = self.small[:, 54:56]
        self.inverse = self.small[:, 56:58]

    def attend_uses(self, gates):
        self.first_step = {0: 2, 1: 1 if gates else 2}
        self.first_output = 1 if gates else 0
        turned = TURNED[-1] // 2 + 1
        return Uses(self, {0: self.first_step[0] + NT, 1: self.first_step[1] + NT, "t0": turned, "t1": turned,
                           3: self.first_output + GROUPS})

    def turn_v(self, pe, uses, i):
        vt_done = self.ev["vt_done"]
        for g in range(2):
            uses.clear(pe, f"t{g}", i, 0)
            for t in range(4):
                mm = pe.transpose(self.ps[2][:, g * HALF + t * P:g * HALF + (t + 1) * P],
                                  self.VT[:, (g * 4 + t) * P:(g * 4 + t + 1) * P], self.ident)
            mm.then_inc(vt_done.sem, 1)

    def take_v(self, act, i):
        vt_done = self.ev["vt_done"]
        for g in range(2):
            act.wait_ge(vt_done.sem, vt_done.at(i * 2 + (g + 1)))
            act.activation(self.V[:, g * 4:g * 4 + 4, :],
                           self.ps[2][:, g * HALF:(g + 1) * HALF].rearrange("p (t v) -> p t v", t=4),
                           ACT.Copy).then_inc(self.tfree[g].sem, 1)

    def score(self, pe, uses, i, j, kdim):
        ps, scores = self.ps, self.ev["scores_done"]
        a, qt = ORDER[j]
        uses.clear(pe, j % 2, i, self.first_step[j % 2] + j // 2)
        keys = (qt + 1) * P
        for lo in range(0, keys, HALF):
            hi = min(keys, lo + HALF)
            mm = pe.matmul(ps[j % 2][:, lo:hi], self.Q[a][0:kdim, qt * P:(qt + 1) * P],
                           self.K[a][0:kdim, lo:hi], start=True, stop=True)
        mm.then_inc(scores.sem, 1)

    def attend_pe(self, pe, uses, i, kdim):
        ps, t_done, pv_done, p_ready = self.ps, self.ev["t_done"], self.ev["pv_done"], self.ev["p_ready"]

        def turn(j):
            qt = ORDER[j][1]
            pe.wait_ge(p_ready.sem, p_ready.at(i * STEPS + (j + 1)))
            for c in range(qt // 4 + 1):
                n = TURNED[j] + c
                uses.clear(pe, f"t{n % 2}", i, 1 + n // 2)
                for t in range(c * 4, min(c * 4 + 4, qt + 1)):
                    mm = pe.transpose(ps[2][:, (n % 2) * HALF + (t % 4) * P:(n % 2) * HALF + (t % 4 + 1) * P],
                                      self.probs[j % 2][:, t * P:(t + 1) * P], self.ident)
                mm.then_inc(t_done.sem, 1)

        def outputs(m, part):
            a, last_qt = ORDER[4 * m + 3]
            g = last_qt // 4
            if part == 0:
                last = TURNED[4 * m + 4] - 1
                uses.over(pe, f"t{last % 2}", i, 1 + last // 2)
                uses.clear(pe, 3, i, self.first_output + m - 1)
            for t in range(part * (g + 1), (part + 1) * (g + 1)):
                lo = max(t * P - g * HALF, 0)
                bank = (m % 2) * HALF
                mm = pe.matmul(ps[3][a * 64:a * 64 + 64, bank + lo:bank + HALF],
                               self.V[:, t, a * 64:a * 64 + 64], self.probs_t[g][:, t, lo:HALF],
                               start=t == 0, stop=t == 4 * g + 3, skip_group_check=True)
            if part == 3:
                mm.then_inc(pv_done.sem, 1)

        for j in range(STEPS):
            turn(j)
            if j + 2 < STEPS:
                self.score(pe, uses, i, j + 2, kdim)
            if j >= 4:
                outputs(j // 4 - 1, j % 4)
        for part in range(4):
            outputs(GROUPS - 1, part)

    def exponentials(self, act, i, j):
        max_ready = self.ev["max_ready"]
        act.wait_ge(max_ready.sem, max_ready.at(i * STEPS + (j + 1)))
        keys = (ORDER[j][1] + 1) * P
        act.activation(self.probs[j % 2][:, 0:keys], self.ps[j % 2][:, 0:keys], ACT.Exp,
                       bias=self.neg_max[:, j % 2:j % 2 + 1],
                       accum_out=self.total[:, j % 2:j % 2 + 1]).then_inc(self.free[j % 2].sem, 1)

    def take_turned(self, act, i, j):
        t_done, qt = self.ev["t_done"], ORDER[j][1]
        for c in range(qt // 4 + 1):
            n = TURNED[j] + c
            blocks = min(qt + 1 - 4 * c, 4)
            act.wait_ge(t_done.sem, t_done.at(i * TURNED[-1] + (n + 1)))
            act.activation(self.probs_t[qt // 4][:, 4 * c:4 * c + blocks, (qt % 4) * P:(qt % 4 + 1) * P],
                           self.ps[2][:, (n % 2) * HALF:(n % 2) * HALF + blocks * P]
                           .rearrange("p (t c) -> p t c", t=blocks), ACT.Copy).then_inc(self.tfree[n % 2].sem, 1)

    def attend_act(self, act, i, next_weights):
        for j in range(STEPS):
            if j and j + 1 < STEPS:
                self.exponentials(act, i, j + 1)
            self.take_turned(act, i, j)
            if next_weights and j in (8, 10):
                next_weights(act, (j - 8) // 2)

    def maximum(self, dve, i, j):
        scores, masked, max_ready = (self.ev[n] for n in ("scores_done", "exp_done", "max_ready"))
        qt, s = ORDER[j][1], self.ps[j % 2]
        dve.wait_ge(scores.sem, scores.at(i * STEPS + (j + 1)))
        dve.tensor_tensor(s[:, qt * P:(qt + 1) * P], s[:, qt * P:(qt + 1) * P],
                          self.consts[:, C_CAUSAL:C_CAUSAL + P], ALU.add).then_inc(masked.sem, 1)
        dve.wait_ge(masked.sem, masked.at(i * STEPS + (j + 1)))
        dve.tensor_reduce(self.neg_max[:, j % 2:j % 2 + 1], s[:, 0:(qt + 1) * P], AX.X, ALU.max,
                          negate=True).then_inc(max_ready.sem, 1)

    def normalise(self, dve, uses, i, j):
        inverted, p_ready = self.ev["sk_ready"], self.ev["p_ready"]
        r = self.inverse[:, j % 2:j % 2 + 1]
        uses.over(dve, j % 2, i, self.first_step[j % 2] + j // 2)
        dve.reciprocal(r, self.total[:, j % 2:j % 2 + 1]).then_inc(inverted.sem, 1)
        dve.wait_ge(inverted.sem, inverted.at(i * STEPS + (j + 1)))
        p = self.probs[j % 2][:, 0:(ORDER[j][1] + 1) * P]
        dve.tensor_scalar(p, p, r, None, ALU.mult).then_inc(p_ready.sem, 1)

    def attend_dve(self, dve, uses, i, gates):
        pv_done = self.ev["pv_done"]

        def outputs(m):
            a, last_qt = ORDER[4 * m + 3]
            g, bank = last_qt // 4, (m % 2) * HALF
            rows, cols = slice(a * 64, a * 64 + 64), slice(g * HALF, (g + 1) * HALF)
            dve.wait_ge(pv_done.sem, pv_done.at(i * GROUPS + (m + 1)))
            dve.tensor_tensor(self.arena[rows, bass.ds(i, 1), cols].rearrange("p f c -> p (f c)"),
                              self.ps[3][rows, bank:bank + HALF], gates(rows, cols), ALU.mult)\
               .then_inc(self.free[3].sem, 1)

        for j in range(1, STEPS):
            self.normalise(dve, uses, i, j)
            if j + 1 < STEPS:
                self.maximum(dve, i, j + 1)
            if j >= 8 and j % 4 == 0:
                outputs(j // 4 - 2)
        outputs(GROUPS - 2)
        outputs(GROUPS - 1)

    def attend_passed(self, turns):
        for name, n in (("vt_done", 2), ("scores_done", STEPS), ("max_ready", STEPS),
                        ("exp_done", STEPS), ("sk_ready", STEPS), ("p_ready", STEPS),
                        ("t_done", TURNED[-1]), ("pv_done", GROUPS)):
            self.ev[name].passed(turns * n)

    def dense(self, name, column, turns, tile, gain=None):
        nc, ps = self.nc, self.ps
        plan = Plan(1, 1)
        w = self.weights(name)
        free, used = self.free, self.used
        with nc.Block() as block:
            @block.sync
            def _(sp):
                if gain:
                    self.keep_x(sp)
                with sp.Fori(0, turns) as i:
                    for b in range(2):
                        self.load_weights(sp, plan, i, b, [
                            (self.slot(b, KT), w[:, :, bass.ds(i * (2 * P) + (column + b * P), P)])])

            @block.scalar
            def _(act):
                for b in range(2):
                    self.weights_hi(act, plan, 0, b)
                if gain:
                    self.norm_act(act)
                with act.Fori(1, turns) as i:
                    for b in range(2):
                        self.weights_hi(act, plan, i, b)

            @block.gpsimd
            def _(pool):
                for b in range(2):
                    self.weights_lo(pool, plan, 0, b)
                if gain:
                    self.norm_pool(pool)
                with pool.Fori(1, turns) as i:
                    for b in range(2):
                        self.weights_lo(pool, plan, i, b)

            @block.tensor
            def _(pe):
                if gain:
                    self.norm_pe(pe)
                for b in range(2):
                    self.project(pe, plan, 0, b, ps[b], range(KT), range(KT), new_h=gain and b == 0, kept=gain and b == 0)
                with pe.Fori(1, turns) as i:
                    for b in range(2):
                        pe.wait_ge(free[b].sem, free[b].at(i + 1))
                        self.project(pe, plan, i, b, ps[b], range(KT), range(KT))

            @block.vector
            def _(dve):
                if gain:
                    self.norm_dve(dve, gain)
                with dve.Fori(0, turns) as i:
                    for b in range(2):
                        dve.wait_ge(used.sem, used.at(plan.n(i, b) + 3))
                        dve.tensor_scalar(self.arena[:, bass.ds(i * 2 + (tile + b), 1), :].rearrange("p f c -> p (f c)"),
                                          ps[b][:, :], 1.0, None, ALU.mult).then_inc(free[b].sem, 1)
        if gain:
            self.norm_passed()
        self.passed_blocks(plan, turns)
        for b in range(2):
            free[b].passed(turns)

    def rotate(self, dve, tile, tmp, step, at):
        cos, sin = self.arena[64:96, self.ROPE_AT, :], self.arena[96:128, self.ROPE_AT, :]
        dve.tensor_tensor(tmp[64:96, :], tile[96:128, :], sin, ALU.mult).then_inc(step.sem, 1)
        dve.tensor_tensor(tile[64:96, :], tile[64:96, :], cos, ALU.mult).then_inc(step.sem, 1)
        dve.wait_ge(step.sem, at(2))
        return dve.tensor_tensor(tile[64:96, :], tile[64:96, :], tmp[64:96, :], ALU.add)

    ROPE_AT, KPE_AT, TMP_AT = 24, 25, 26

    def angles(self):
        A = self.arena
        rows = slice(64, 128)
        pos, ang, turns_, r = (A[rows, n, :] for n in (26, 27, 20, 21))
        out = A[:, self.ROPE_AT, :]
        ints = self.raw[rows, 0, :].bitcast(I32)
        d, act_step, loaded = self.dve_step, self.act_step, self.dma[0]
        half_pi = self.small[:, 60:61]
        with self.nc.Block() as block:
            @block.sync
            def _(sp):
                sp.dma_start(ints, self.dram["positions"].partition_broadcast(64)).then_inc(loaded.sem, 16)

            @block.vector
            def _(dve):
                count = [0]

                def done(ins):
                    count[0] += 1
                    ins.then_inc(d.sem, 1)
                    dve.wait_ge(d.sem, d.at(count[0]))

                done(dve.memset(half_pi, float(np.pi / 2)))
                dve.wait_ge(loaded.sem, loaded.at(16))
                done(dve.tensor_copy(pos, ints))
                done(dve.tensor_scalar(ang, pos, self.consts[rows, C_FREQ:C_FREQ + 1], None, ALU.mult))
                done(dve.tensor_scalar(turns_, ang, float(1 / (2 * np.pi)), ROUND, ALU.mult, ALU.add))
                done(dve.tensor_scalar(turns_, turns_, -ROUND, None, ALU.add))
                done(dve.scalar_tensor_tensor(r, turns_, -TWO_PI_1, ang, ALU.mult, ALU.add))
                done(dve.scalar_tensor_tensor(r, turns_, -TWO_PI_2, r, ALU.mult, ALU.add))
                done(dve.scalar_tensor_tensor(r, turns_, -TWO_PI_3, r, ALU.mult, ALU.add))
                done(dve.tensor_scalar(r, r, PI_BELOW, -PI_BELOW, ALU.min, ALU.max))
                dve.wait_ge(act_step.sem, act_step.at(3))
                dve.tensor_scalar(out[96:128, :], out[96:128, :], self.consts[96:128, C_SIGN:C_SIGN + 1], None, ALU.mult)
                assert count[0] == 9

            @block.scalar
            def _(act):
                act.wait_ge(d.sem, d.at(9))
                act.activation(out[64:96, :], r[0:32, :], ACT.Abs).then_inc(act_step.sem, 1)
                act.wait_ge(act_step.sem, act_step.at(1))
                act.activation(out[64:96, :], out[64:96, :], ACT.Sin, scale=-1.0, bias=half_pi[64:96, :])\
                   .then_inc(act_step.sem, 1)
                act.activation(out[96:128, :], r[32:64, :], ACT.Sin).then_inc(act_step.sem, 1)
        d.passed(9)
        act_step.passed(3)
        loaded.passed(16)

    def low_rank(self):
        nc, ps, A = self.nc, self.ps, self.arena
        w = self.weights("e_w_in_2")
        plan = Plan(1, 1, 1, 3)
        latent = [A[:, n, :] for n in (14, 15, 16)]
        squares = [A[:, n, :] for n in (17, 18, 19)]
        rstd = [A[:, n, :] for n in (20, 21)]
        h = latent
        kpe, tmp = A[:, self.KPE_AT, :], A[:, self.TMP_AT, :]
        used, free, step, act_step, pe_step = self.used, self.free, self.dve_step, self.act_step, self.pe_step
        out, squared, scaled = self.ev["evacuated"], self.ev["squared"], self.ev["scaled"]
        h_hi = self.ev["h_hi"]
        groups = ((0, 1), (2,))
        swap = E_KPE + MLA_ROPE // 2
        columns = [[(0, P, E_CQ)], [(0, P, E_CQ + P)], [(0, P, E_CKV)],
                   [(64, MLA_ROPE, E_KPE), (96, MLA_ROPE // 2, swap), (96 + MLA_ROPE // 2, MLA_ROPE // 2, E_KPE)]]
        with nc.Block() as block:
            @block.sync
            def _(sp):
                for b in range(4):
                    self.load_weights(sp, plan, 0, b, [(self.slot(b, KT)[:, :, at:at + n], w[:, :, c:c + n])
                                                       for at, n, c in columns[b]])

            @block.gpsimd
            def _(pool):
                for b in range(4):
                    self.weights_lo(pool, plan, 0, b)
                for k in range(3):
                    pool.wait_ge(h_hi.sem, h_hi.at(k + 1))
                    pool.tensor_tensor(self.hlo[:, k, :], h[k], self.hhi[:, k, :].bitcast(F32), ALU.subtract)

            @block.tensor
            def _(pe):
                for b in range(4):
                    if b >= 2:
                        pe.wait_ge(out.sem, out.at(b - 1))
                    self.project(pe, plan, 0, b, ps[b % 2], range(KT), range(KT))
                for g, tiles in enumerate(groups):
                    pe.wait_ge(squared.sem, squared.at(tiles[-1] + 1))
                    for c in range(2):
                        for t in tiles:
                            mm = pe.matmul(ps[2 + g][:, c * HALF:(c + 1) * HALF], self.ones,
                                           squares[t][:, c * HALF:(c + 1) * HALF],
                                           start=t == tiles[0], stop=t == tiles[-1])
                    mm.then_inc(pe_step.sem, 1)

            @block.scalar
            def _(act):
                self.weights_hi(act, plan, 0, 0)
                self.weights_hi(act, plan, 0, 1)
                for b in range(4):
                    act.wait_ge(used.sem, used.at(b + 3))
                    act.activation((latent + [kpe])[b], ps[b % 2][:, :], ACT.Copy).then_inc(out.sem, 1)
                    if b < 2:
                        self.weights_hi(act, plan, 0, b + 2)
                for t in range(3):
                    act.wait_ge(out.sem, out.at(t + 1))
                    act.activation(squares[t], latent[t], ACT.Square).then_inc(squared.sem, 1)
                for g in range(2):
                    act.wait_ge(step.sem, step.at(2 * g + 2))
                    act.activation(rstd[g], rstd[g], ACT.Sqrt).then_inc(act_step.sem, 1)
                for k in range(3):
                    act.wait_ge(scaled.sem, scaled.at(k + 1))
                    act.activation(self.hhi[:, k, :], h[k], ACT.Copy).then_inc(h_hi.sem, 1)

            @block.vector
            def _(dve):
                for g, tiles in enumerate(groups):
                    dve.wait_ge(pe_step.sem, pe_step.at(g + 1))
                    dve.tensor_scalar(rstd[g], ps[2 + g][:, :], 1.0 / (P * len(tiles)), EPS, ALU.mult, ALU.add)\
                       .then_inc(step.sem, 1)
                    dve.wait_ge(step.sem, step.at(2 * g + 1))
                    dve.reciprocal(rstd[g], rstd[g]).then_inc(step.sem, 1)
                for g, tiles in enumerate(groups):
                    dve.wait_ge(act_step.sem, act_step.at(g + 1))
                    for t in tiles:
                        gain = self.col("e_g_q_a_2", t) if g == 0 else self.col("e_g_kv_a_2")
                        dve.wait_ge(squared.sem, squared.at(t + 1))
                        dve.scalar_tensor_tensor(h[t], latent[t], gain, rstd[g], ALU.mult, ALU.mult)\
                           .then_inc(scaled.sem, 1)
                dve.wait_ge(out.sem, out.at(4))
                self.rotate(dve, kpe, tmp, step, lambda n: step.at(4 + n)).then_inc(step.sem, 1)
        self.passed_blocks(plan, 1)
        out.passed(4)
        squared.passed(3)
        scaled.passed(3)
        h_hi.passed(3)
        step.passed(7)
        act_step.passed(2)
        pe_step.passed(2)

    def silu_gates(self):
        nc, ps, A = self.nc, self.ps, self.arena
        sig = [A[:, n, :] for n in (14, 15)]
        gated, used = self.ev["scaled"], self.ev["squared"]
        keys, v_tok = self.swa_buffers()
        cleared, turned, pe_step = self.pool_step, self.ev["vt_done"], self.pe_step
        with nc.Block() as block:
            @block.scalar
            def _(act):
                for k in range(KT):
                    if k >= 2:
                        act.wait_ge(used.sem, used.at(k - 1))
                    act.activation(sig[k % 2], A[:, k, :], ACT.Sigmoid).then_inc(gated.sem, 1)
                act.wait_ge(pe_step.sem, pe_step.at(1))
                act.activation(v_tok[:, 1:1 + NT, :], ps[0][:, :].rearrange("p (t v) -> p t v", t=NT), ACT.Copy)
                for g in range(SWA_KV):
                    act.activation(keys[g][:, P:P + TOK], A[g * 64:g * 64 + 64, 12, :], ACT.Copy)

            @block.gpsimd
            def _(pool):
                pool.memset(v_tok[:, 0, :], 0.0)
                for g in range(SWA_KV):
                    pool.memset(keys[g][:, 0:P], 0.0)

            @block.tensor
            def _(pe):
                for t in range(NT):
                    mm = pe.transpose(ps[0][:, t * P:(t + 1) * P], A[:, 13, t * P:(t + 1) * P], self.ident)
                mm.then_inc(pe_step.sem, 1)

            @block.vector
            def _(dve):
                for k in range(KT):
                    dve.wait_ge(gated.sem, gated.at(k + 1))
                    dve.tensor_tensor(A[:, k, :], A[:, k, :], sig[k % 2], ALU.mult).then_inc(used.sem, 1)
        gated.passed(KT)
        used.passed(KT)
        pe_step.passed(1)

    def swa_buffers(self):
        at = 16 * TOK
        keys = [self.flat[0:64, at + g * (P + TOK):at + (g + 1) * (P + TOK)] for g in range(SWA_KV)]
        at += SWA_KV * (P + TOK)
        return keys, self.flat[:, at:at + (NT + 1) * P].rearrange("p (t v) -> p t v", t=NT + 1)

    def sliding_window(self):
        nc, ps, A, ev = self.nc, self.ps, self.arena, self.ev
        keys, v_tok = self.swa_buffers()
        H, G = SWA_HEADS, SWA_HEADS // SWA_KV
        q_tiles = A[:, 8:12, :]
        q = [self.flat[0:64, at * TOK:at * TOK + H * P].rearrange("p (f a c) -> p f a c", f=H // 2, a=2) for at in (20, 23)]
        v = [self.flat[:, 15 * TOK + n * 2 * P:15 * TOK + (n + 1) * 2 * P].rearrange("p (t c) -> p t c", t=2)
             for n in range(2)]
        s = [self.flat[:, at * TOK:(at + 2) * TOK].rearrange("p (h k) -> p h k", h=H) for at in (21, 24)]
        p_t = self.flat[:, 26 * TOK:28 * TOK].rearrange("p (t h q) -> p t h q", t=2, h=H)
        sinks = self.col("sinks", 0, H)
        neg_sinks = self.small[:, 64:64 + H]
        neg_max, total, sink = ([self.small[:, 72 + (2 * n + u) * H:72 + (2 * n + u + 1) * H] for u in range(2)]
                                for n in range(3))
        free, step, small = self.free, self.dve_step, ev["q_ready"]
        q_staged, v_staged, scores, max_ready = (ev[n] for n in ("k_ready", "vt_done", "scores_done", "max_ready"))
        exp_done, p_ready, t_done, pv_done = (ev[n] for n in ("exp_done", "p_ready", "t_done", "pv_done"))
        STEPS = 2

        def score(pe, i, u):
            pe.wait_ge(q_staged.sem, q_staged.at(i * 2 + 2))
            for h in range(H):
                if h % G == 0:
                    pe.wait_ge(free[h // G].sem, free[h // G].at(i + 1))
                mm = pe.matmul(ps[h // G][:, h % G * 2 * P:(h % G + 1) * 2 * P], q[u][:, h // 2, h % 2, :],
                               keys[h // G][:, bass.ds(i * P, 2 * P)], start=True, stop=True)
                if h % G == G - 1:
                    mm.then_inc(scores.sem, 1)

        def turn(pe, i, u):
            pe.wait_ge(p_ready.sem, p_ready.at(i + 1))
            for t in range(2):
                pe.wait_ge(free[2 + t].sem, free[2 + t].at(i * (2 - t) + 1))
                for h in range(H):
                    mm = pe.transpose(ps[2 + t][:, h * P:(h + 1) * P], s[u][:, h, t * P:(t + 1) * P], self.ident)
                mm.then_inc(t_done.sem, 1)

        def outputs(pe, i, u):
            pe.wait_ge(v_staged.sem, v_staged.at(i + 1))
            for t in range(2):
                pe.wait_ge(free[2 + t].sem, free[2 + t].at(i * (2 - t) + 2))
            for h in range(H):
                g = h // G
                for t in range(2):
                    mm = pe.matmul(ps[2][h % 2 * 64:h % 2 * 64 + 64, h // 2 * P:(h // 2 + 1) * P],
                                   v[u][:, t, g * 64:g * 64 + 64], p_t[:, t, h, :], start=t == 0, stop=t == 1,
                                   skip_group_check=True)
            mm.then_inc(pv_done.sem, 1)

        def stage_q(dve, i, u):
            for a in range(2):
                dve.tensor_scalar(q[u][:, :, a, :], q_tiles[a * 64:a * 64 + 64, :, bass.ds(i * P, P)], SWA_D ** -0.5, None,
                                  ALU.mult).then_inc(q_staged.sem, 1)

        def stage_v(dve, i, u):
            dve.tensor_scalar(v[u], v_tok[:, bass.ds(i, 2), :], 1.0, None, ALU.mult).then_inc(v_staged.sem, 1)

        def maximum(dve, i, u, first=False):
            table = C_SWA + (0 if first else 2 * P)
            for h in range(H):
                if h % G == 0:
                    dve.wait_ge(scores.sem, scores.at(i * 2 + (h // G + 1)))
                ins = dve.scalar_tensor_tensor(s[u][:, h, :], self.consts[:, table:table + 2 * P],
                                               self.consts[:, C_SLOPE + h:C_SLOPE + h + 1],
                                               ps[h // G][:, h % G * 2 * P:(h % G + 1) * 2 * P], ALU.mult, ALU.add)
                if h % G == G - 1:
                    ins.then_inc(free[h // G].sem, 1)
                    dve.wait_ge(free[h // G].sem, free[h // G].at(i + 2))
            dve.tensor_reduce(neg_max[u], s[u], AX.X, ALU.max, negate=True).then_inc(step.sem, 1)
            dve.wait_ge(step.sem, step.at(i * STEPS + 1))
            dve.tensor_tensor(neg_max[u], neg_max[u], neg_sinks, ALU.min).then_inc(step.sem, 1)
            dve.wait_ge(step.sem, step.at(i * STEPS + 2))
            dve.tensor_tensor(sink[u], sinks, neg_max[u], ALU.add).then_inc(max_ready.sem, 1)

        def normalise(dve, i, u):
            dve.wait_ge(exp_done.sem, exp_done.at(i + 1))
            dve.tensor_tensor(total[u], total[u], sink[u], ALU.add).then_inc(small.sem, 1)
            dve.wait_ge(small.sem, small.at(i * 2 + 1))
            dve.reciprocal(total[u], total[u]).then_inc(small.sem, 1)
            dve.wait_ge(small.sem, small.at(i * 2 + 2))
            dve.tensor_tensor(s[u], s[u], total[u].unsqueeze(2).broadcast_to((P, H, 2 * P)), ALU.mult)\
               .then_inc(p_ready.sem, 1)

        def gate_outputs(dve, i):
            dve.wait_ge(pv_done.sem, pv_done.at(i + 1))
            out = A[:, 4:8, bass.ds(i * P, P)]
            dve.tensor_tensor(out, ps[2][:, 0:4 * P].rearrange("p (f c) -> p f c", f=4), out, ALU.mult)\
               .then_inc(free[2].sem, 1)

        def exponentials(act, i, u):
            act.wait_ge(max_ready.sem, max_ready.at(i + 1))
            for h in range(H):
                act.activation(s[u][:, h, :], s[u][:, h, :], ACT.Exp, bias=neg_max[u][:, h:h + 1],
                               accum_out=total[u][:, h:h + 1])
            act.activation(sink[u], sink[u], ACT.Exp).then_inc(exp_done.sem, 1)

        def take_transposed(act, i):
            for t in range(2):
                act.wait_ge(t_done.sem, t_done.at(i * 2 + (t + 1)))
                act.activation(p_t[:, t, :, :], ps[2 + t][:, :].rearrange("p (h q) -> p h q", h=H), ACT.Copy)\
                   .then_inc(free[2 + t].sem, 1)

        def tensor_turn(pe, i, u, ahead=True):
            turn(pe, i, u)
            if ahead:
                score(pe, i + 2, u)
            outputs(pe, i, u)

        def vector_turn(dve, i, u, first=False, ahead=True, last=False):
            normalise(dve, i, u)
            if ahead:
                stage_q(dve, i + 2, u)
            if not first:
                if not last:
                    maximum(dve, i + 1, 1 - u)
                gate_outputs(dve, i - 1)
                if not last:
                    stage_v(dve, i + 1, 1 - u)

        def scalar_turn(act, i, u, last=False):
            if not last:
                exponentials(act, i + 1, 1 - u)
            take_transposed(act, i)

        PAIRED = (NT - 4) // 2
        with nc.Block() as block:
            @block.tensor
            def _(pe):
                score(pe, 0, 0)
                score(pe, 1, 1)
                tensor_turn(pe, 0, 0)
                with pe.Fori(0, PAIRED) as n:
                    tensor_turn(pe, n * 2 + 1, 1)
                    tensor_turn(pe, n * 2 + 2, 0)
                tensor_turn(pe, NT - 3, 1)
                tensor_turn(pe, NT - 2, 0, ahead=False)
                tensor_turn(pe, NT - 1, 1, ahead=False)

            @block.vector
            def _(dve):
                dve.tensor_scalar(neg_sinks, sinks, -1.0, None, ALU.mult)
                for u in range(2):
                    stage_q(dve, u, u)
                    stage_v(dve, u, u)
                maximum(dve, 0, 0, first=True)
                maximum(dve, 1, 1)
                vector_turn(dve, 0, 0, first=True)
                with dve.Fori(0, PAIRED) as n:
                    vector_turn(dve, n * 2 + 1, 1)
                    vector_turn(dve, n * 2 + 2, 0)
                vector_turn(dve, NT - 3, 1)
                vector_turn(dve, NT - 2, 0, ahead=False)
                vector_turn(dve, NT - 1, 1, ahead=False, last=True)
                gate_outputs(dve, NT - 1)

            @block.scalar
            def _(act):
                exponentials(act, 0, 0)
                with act.Fori(0, NT // 2 - 1) as n:
                    scalar_turn(act, n * 2, 0)
                    scalar_turn(act, n * 2 + 1, 1)
                scalar_turn(act, NT - 2, 0)
                scalar_turn(act, NT - 1, 1, last=True)
        for t, n in ((q_staged, 2), (v_staged, 1), (scores, 2), (max_ready, 1), (exp_done, 1), (p_ready, 1),
                     (t_done, 2), (pv_done, 1), (step, STEPS), (small, 2), (free[0], 1), (free[1], 1), (free[2], 2),
                     (free[3], 1)):
            t.passed(n * NT)

    def mla_heads(self):
        nc, ps, ev, A = self.nc, self.ps, self.ev, self.arena
        self.attention_buffers()
        Q, K, VT = self.Q, self.K, self.VT
        wq, wkv = self.weights("e_w_q_up_2"), self.weights("e_w_kv_up_2")
        plan, turns = Plan(3, 1, 3, 1), MLA_HEADS // 2
        uses = self.attend_uses(gates=False)
        used, free = self.used, self.free
        kpe, tmp = A[:, self.KPE_AT, :], A[:, self.TMP_AT, :]
        rotated, kpe_there, step = ev["q_ready"], ev["k_ready"], ev["rows_ready"]
        swap = MLA_ROPE // 2
        KV = MLA_NOPE + MLA_V
        with nc.Block() as block:
            @block.sync
            def _(sp):
                with sp.Fori(0, turns) as i:
                    for a in range(2):
                        at = i * (2 * MLA_DK) + a * MLA_DK
                        slot = self.slot(2 * a, 2)
                        self.load_weights(sp, plan, i, 2 * a, [
                            (slot[:, :, 0:MLA_DK], wq[:, :, bass.ds(at, MLA_DK)]),
                            (slot[:, :, MLA_DK:MLA_DK + swap], wq[:, :, bass.ds(at + (MLA_NOPE + swap), swap)]),
                            (slot[:, :, MLA_DK + swap:P], wq[:, :, bass.ds(at + MLA_NOPE, swap)])])
                        self.load_weights(sp, plan, i, 2 * a + 1, [
                            (self.slot(1, 1), wkv[:, :, bass.ds(i * (2 * KV) + a * KV, KV)])])

            @block.gpsimd
            def _(pool):
                with pool.Fori(0, turns) as i:
                    for b in range(4):
                        self.weights_lo(pool, plan, i, b, P if b % 2 else 2 * P)

            @block.tensor
            def _(pe):
                with pe.Fori(0, turns) as i:
                    for b in range(4):
                        uses.clear(pe, b % 2, i, b // 2)
                        self.project(pe, plan, i, b, ps[b % 2], (0,) if b % 2 else (0, 1), (2,) if b % 2 else (0, 1))
                    pe.wait_ge(kpe_there.sem, kpe_there.at(2))
                    pe.wait_ge(rotated.sem, rotated.at(i * 2 + 1))
                    for j in range(2):
                        self.score(pe, uses, i, j, MLA_DK)
                    self.turn_v(pe, uses, i)
                    self.attend_pe(pe, uses, i, MLA_DK)

            @block.scalar
            def _(act):
                def turn(i, last=False):
                    for b in range(4):
                        a = b // 2
                        act.wait_ge(used.sem, used.at(plan.n(i, b) + 3))
                        if b % 2 == 0:
                            act.activation(Q[a], ps[0][:, :], ACT.Copy, scale=MLA_DK ** -0.5).then_inc(free[0].sem, 1)
                        else:
                            act.activation(K[a][0:64, :], ps[1][0:64, :], ACT.Copy)
                            act.activation(VT[a * 64:a * 64 + 64, :], ps[1][64:128, :], ACT.Copy)\
                               .then_inc(free[1].sem, 1)
                        if b < 2:
                            self.weights_hi(act, plan, i, b + 2, P if b % 2 else 2 * P)
                    self.exponentials(act, i, 0)
                    self.take_v(act, i)
                    self.exponentials(act, i, 1)
                    self.attend_act(act, i, None if last else
                                    lambda eng, b: self.weights_hi(eng, plan, i + 1, b, P if b else 2 * P))

                for a in range(2):
                    act.activation(K[a][64:96, :], kpe[64:96, :], ACT.Copy).then_inc(kpe_there.sem, 1)
                self.weights_hi(act, plan, 0, 0, 2 * P)
                self.weights_hi(act, plan, 0, 1, P)
                with act.Fori(0, turns - 1) as i:
                    turn(i)
                turn(turns - 1, last=True)

            @block.vector
            def _(dve):
                O = A[:, 0:8, :]
                with dve.Fori(0, turns) as i:
                    for a in range(2):
                        uses.over(dve, 0, i, a)
                        self.rotate(dve, Q[a], tmp, step, lambda n: step.at(i * 4 + (a * 2 + n)))\
                            .then_inc(rotated.sem, 1)
                        dve.wait_ge(rotated.sem, rotated.at(i * 2 + (a + 1)))
                    self.maximum(dve, i, 0)
                    self.maximum(dve, i, 1)
                    self.normalise(dve, uses, i, 0)
                    self.attend_dve(dve, uses, i, lambda rows, cols: O[rows, bass.ds(i, 1), cols]
                                    .rearrange("p f c -> p (f c)"))
        self.passed_blocks(plan, turns)
        uses.passed(turns)
        self.attend_passed(turns)
        kpe_there.passed(2)
        rotated.passed(2 * turns)
        step.passed(4 * turns)

    def fox_rows(self):
        n = FOX_HEADS
        z, tmp, lf, one, lc, nlc = (self.arena[0:n, k, :] for k in (10, 11, 12, 13, 14, 15))
        d, pl, stored = self.dve_step, self.pool_step, self.ev["stored"]
        with self.nc.Block() as block:
            @block.gpsimd
            def _(pool):
                pool.memset(one, 1.0).then_inc(pl.sem, 1)

            @block.scalar
            def _(act):
                self.log_forget(act, None, z, tmp, lf, n)

            @block.vector
            def _(dve):
                self.log_forget(None, dve, z, tmp, lf, n)
                dve.wait_ge(d.sem, d.at(1))
                dve.wait_ge(pl.sem, pl.at(1))
                dve.tensor_tensor_scan(lc, one, lf, 0.0, ALU.mult, ALU.add).then_inc(d.sem, 1)
                dve.wait_ge(d.sem, d.at(2))
                dve.tensor_scalar(nlc, lc, -1.0, None, ALU.mult).then_inc(d.sem, 1)

            @block.sync
            def _(sp):
                sp.wait_ge(d.sem, d.at(2))
                sp.dma_start(self.dram["log_cum"][0], lc).then_inc(stored.sem, 16)
                sp.wait_ge(d.sem, d.at(3))
                sp.dma_start(self.dram["log_cum"][1], nlc).then_inc(stored.sem, 16)
                sp.wait_ge(stored.sem, stored.at(32))
        d.passed(3)
        pl.passed(1)
        self.act_step.passed(3)
        stored.passed(32)

    def fox_heads(self):
        nc, ps, ev = self.nc, self.ps, self.ev
        self.attention_buffers()
        Q, K, VT = self.Q, self.K, self.VT
        w = self.weights("o_w_in_2")
        plan, turns = Plan(1, 1, 1, 1), FOX_HEADS // 2
        kdim = FOX_D + 2
        gate, sig = self.arena[:, 22, :], self.arena[:, 23, :]
        starts = (2 * D, 0, D, 3 * D + FOX_HEADS)
        uses = self.attend_uses(gates=True)
        used, free, dma = self.used, self.free, self.dma
        ones_set, gated, scores = self.pool_step, ev["h_hi"], ev["scores_done"]
        with nc.Block() as block:
            @block.sync
            def _(sp):
                sp.wait_ge(ones_set.sem, ones_set.at(4))
                with sp.Fori(0, turns) as i:
                    for b in range(4):
                        at = i * P + starts[b] if starts[b] else (i * 2) * (P // 2)
                        self.load_weights(sp, plan, i, b, [(self.slot(b, KT), w[:, :, bass.ds(at, P)])])
                        if b == 1:
                            sp.wait_ge(scores.sem, scores.at(i * STEPS))
                            for a in range(2):
                                for side, tile, row in ((0, Q[a], 65), (1, K[a], 64)):
                                    sp.dma_start(tile[row:row + 1, :],
                                                 self.dram["log_cum"][side][bass.ds(i * 2 + a, 1), :])\
                                      .then_inc(dma[a].sem, 16)

            @block.gpsimd
            def _(pool):
                for tile in (*Q, *K):
                    pool.memset(tile[64:66, :], 1.0).then_inc(ones_set.sem, 1)
                with pool.Fori(0, turns) as i:
                    for b in range(4):
                        self.weights_lo(pool, plan, i, b)

            @block.tensor
            def _(pe):
                with pe.Fori(0, turns) as i:
                    for b in range(3):
                        uses.clear(pe, b % 2, i, b // 2)
                        self.project(pe, plan, i, b, ps[b % 2], range(KT), range(KT))
                    uses.over(pe, 0, i, 0)
                    self.turn_v(pe, uses, i)
                    uses.over(pe, 1, i, 0)
                    uses.over(pe, 0, i, 1)
                    for a in range(2):
                        pe.wait_ge(dma[a].sem, dma[a].at(i * 32 + 32))
                    for j in range(2):
                        self.score(pe, uses, i, j, kdim)
                    uses.clear(pe, 3, i, 0)
                    self.project(pe, plan, i, 3, ps[3], range(KT), range(KT))
                    self.attend_pe(pe, uses, i, kdim)

            @block.scalar
            def _(act):
                def turn(i, last=False):
                    for b in range(3):
                        act.wait_ge(used.sem, used.at(plan.n(i, b) + 3))
                        if b == 0:
                            act.activation(VT, ps[0][:, :], ACT.Copy).then_inc(free[0].sem, 1)
                        elif b == 1:
                            act.activation(Q[0][0:64, :], ps[1][0:64, :], ACT.Copy, scale=FOX_D ** -0.5)
                            act.activation(Q[1][0:64, :], ps[1][64:128, :], ACT.Copy, scale=FOX_D ** -0.5)\
                               .then_inc(free[1].sem, 1)
                        else:
                            act.activation(K[0][0:64, :], ps[0][0:64, :], ACT.Copy)
                            act.activation(K[1][0:64, :], ps[0][64:128, :], ACT.Copy).then_inc(free[0].sem, 1)
                        if b < 2:
                            self.weights_hi(act, plan, i, b + 2)
                    self.take_v(act, i)
                    self.exponentials(act, i, 0)
                    self.exponentials(act, i, 1)
                    act.wait_ge(used.sem, used.at(plan.n(i, 3) + 3))
                    act.activation(sig, ps[3][:, :], ACT.Sigmoid).then_inc(gated.sem, 1)
                    self.attend_act(act, i, None if last else lambda eng, b: self.weights_hi(eng, plan, i + 1, b))

                self.weights_hi(act, plan, 0, 0)
                self.weights_hi(act, plan, 0, 1)
                with act.Fori(0, turns - 1) as i:
                    turn(i)
                turn(turns - 1, last=True)

            @block.vector
            def _(dve):
                with dve.Fori(0, turns) as i:
                    self.maximum(dve, i, 0)
                    self.maximum(dve, i, 1)
                    self.normalise(dve, uses, i, 0)
                    dve.wait_ge(gated.sem, gated.at(i + 1))
                    uses.clear(dve, 3, i, 0)
                    dve.tensor_tensor(gate, ps[3][:, :], sig, ALU.mult).then_inc(free[3].sem, 1)
                    uses.over(dve, 3, i, 0)
                    self.attend_dve(dve, uses, i, lambda rows, cols: gate[rows, cols])
        self.passed_blocks(plan, turns)
        uses.passed(turns)
        self.attend_passed(turns)
        ones_set.passed(4)
        gated.passed(turns)
        for a in range(2):
            dma[a].passed(32 * turns)


def program(nc, dram):
    with ExitStack() as ctx:
        k = Kernel(nc, dram, ctx)
        k.start_credits()
        k.load_x()

        i_gate, f_gate = 2 * M_QK + 2 * M_V, 2 * M_QK + 2 * M_V + M_HEADS
        k.gates("l0_norm_mix", "l0_mlstm_w_in", ((0, i_gate, M_HEADS), (32, f_gate, M_HEADS)), "gates")
        k.mlstm_rows()
        k.mlstm_heads()
        k.mlstm_norm()
        k.out_projection("l0_mlstm_w_out")

        k.ffn_up("l0_norm_ffn")
        k.ffn_down()
        k.norm("final_norm")

        k.dense("e_w_in_2", E_QS, 3, 8, gain="e_g_in_2")
        k.dense("e_w_in_2", E_GATE, 4, 0)
        k.silu_gates()
        k.sliding_window()
        k.angles()
        k.low_rank()
        k.mla_heads()
        k.out_projection("e_w_out_2")

        k.gates("o_g_in_2", "o_w_in_2", ((0, 3 * D, FOX_HEADS),), "o_b_f")
        k.fox_rows()
        k.fox_heads()
        k.out_projection("o_w_out_2")

        k.norm("g_final_2")
        k.store()


WEIGHTS = ["l0_mlstm_w_in", "l0_mlstm_w_out", "l0_ffn_w_up", "l0_ffn_w_down",
           "e_w_in_2", "e_w_q_up_2", "e_w_kv_up_2", "e_w_out_2", "o_w_in_2", "o_w_out_2"]


def column_layout(inputs):
    cols = np.zeros((P, N_COLS), np.float32)
    for name, (at, n) in COLS.items():
        if name in inputs and name != "o_b_f":
            cols[:, at:at + n] = np.asarray(inputs[name]).reshape(n, P).T
    gates = np.asarray(inputs["l0_mlstm_b_gates"])
    cols[0:M_HEADS, COLS["gates"][0]] = gates[:M_HEADS]
    cols[32:32 + M_HEADS, COLS["gates"][0]] = gates[M_HEADS:]
    cols[0:FOX_HEADS, COLS["o_b_f"][0]] = np.asarray(inputs["o_b_f_2"])[0]
    cols[:, COLS["sinks"][0]:COLS["sinks"][0] + SWA_HEADS] = np.asarray(inputs["e_sinks_2"])
    taps = np.concatenate([np.asarray(inputs["l0_ffn_conv_w"]), np.asarray(inputs["l0_ffn_conv_b"])[None]])
    conv = taps.reshape(4, 2, FT, P).transpose(3, 2, 1, 0).reshape(P, FT, 8)
    return cols, np.ascontiguousarray(conv)


def kernel(**inputs):
    import concourse.bacc as bacc
    from concourse.bass_utils import run_bass_kernel_spmd

    nc = bacc.Bacc("TRN2", target_bir_lowering=False, num_devices=1)
    cols, conv = column_layout(inputs)
    arrays = {"consts": shape_constants(), "cols": cols, "conv": conv,
              "x": np.asarray(inputs["x"]).reshape(TOK, D),
              "positions": np.asarray(inputs["positions_2"]).reshape(1, TOK)}
    for name in WEIGHTS:
        w = np.asarray(inputs[name])
        arrays[name] = w.reshape(w.shape[-2:])
    arrays = {name: np.ascontiguousarray(a) for name, a in arrays.items()}
    dram = {name: nc.dram_tensor(f"in_{name}", a.shape, mybir.dt.from_np(a.dtype), kind="ExternalInput").ap()
            for name, a in arrays.items()}
    dram["x_kept"] = nc.dram_tensor("x_kept", (P, 2, KT, HALF), F32, kind="Internal").ap()
    dram["log_cum"] = nc.dram_tensor("log_cum", (2, FOX_HEADS, TOK), F32, kind="Internal").ap()
    dram["out"] = nc.dram_tensor("out", (TOK, D), F32, kind="ExternalOutput").ap()
    program(nc, dram)
    done = run_bass_kernel_spmd(nc, [{f"in_{name}": a for name, a in arrays.items()}], core_ids=[0])
    return done.results[0]["out"].reshape(1, TOK, D)
```

```python
from contextlib import ExitStack

import concourse.bass as bass
from concourse import mybir
import numpy as np

F32 = mybir.dt.float32
F32R = mybir.dt.float32r
I32 = mybir.dt.int32
ACT = mybir.ActivationFunctionType
ALU = mybir.AluOpType
AX = mybir.AxisListType

P = 128
TOK = 1024
D = 1024
KT = D // P
HALF = TOK // 2
NT = TOK // P
EPS = 1e-6
D_FF = 2816
FT = D_FF // P
BIG = 1e30

M_HEADS, M_DQK, M_DV = 4, 128, 256
M_QK, M_V = M_HEADS * M_DQK, M_HEADS * M_DV

MLA_HEADS, MLA_NOPE, MLA_ROPE, MLA_V = 8, 64, 32, 64
MLA_DK = MLA_NOPE + MLA_ROPE
Q_RANK, KV_RANK = 256, 128
SWA_HEADS, SWA_KV, SWA_D = 8, 2, 64
FOX_HEADS, FOX_D = 16, 64

E_CQ, E_CKV = 0, Q_RANK
E_KPE = E_CKV + KV_RANK
E_QS = E_KPE + MLA_ROPE
E_KS = E_QS + SWA_HEADS * SWA_D
E_VS = E_KS + SWA_KV * SWA_D
E_GATE = E_VS + SWA_KV * SWA_D

TWO_PI_1 = 6.28125
TWO_PI_2 = float(np.float32(0.0019350051879882812))
TWO_PI_3 = float(2 * np.pi - TWO_PI_1 - TWO_PI_2)
ROUND = 12582912.0
PI_BELOW = 3.1415925

ORDER = [(a, qt) for a in range(2) for g in (1, 0) for qt in range(4 * g, 4 * g + 4)]
STEPS = len(ORDER)
GROUPS = STEPS // 4
TURNED = [0]
for _, _qt in ORDER:
    TURNED.append(TURNED[-1] + _qt // 4 + 1)

ARENA_TILES = 28
X_AT = 18


C_IDENT, C_ONES, C_CAUSAL, C_LATER, C_SWA = 0, 128, 256, 384, 512
C_SLOPE = C_SWA + 512
C_ONEHOT = C_SLOPE + SWA_HEADS
C_FREQ = C_ONEHOT + 16
C_SIGN = C_FREQ + 1
C_TOTAL = C_SIGN + 1


def shape_constants():
    c = np.zeros((P, C_TOTAL), np.float32)
    r = np.arange(P)
    c[:, C_IDENT:C_IDENT + P] = np.eye(P)
    c[:, C_ONES:C_ONES + P] = 1
    c[:, C_CAUSAL:C_CAUSAL + P] = np.where(r[None, :] <= r[:, None], 0, -BIG)
    c[:, C_LATER:C_LATER + P] = np.where(r[:, None] <= r[None, :], 0, BIG)
    dist = P + r[:, None] - np.arange(2 * P)[None, :]
    inside = (dist >= 0) & (dist < P)
    first = inside & (np.arange(2 * P)[None, :] >= P)
    c[:, C_SWA:C_SWA + 2 * P] = np.where(first, -dist, -100 * BIG)
    c[:, C_SWA + 2 * P:C_SWA + 4 * P] = np.where(inside, -dist, -100 * BIG)
    c[:, C_SLOPE:C_SLOPE + SWA_HEADS] = 2.0 ** (-8.0 * (np.arange(SWA_HEADS) + 1.0) / SWA_HEADS)
    c[:, C_ONEHOT:C_ONEHOT + 16] = (r[:, None] % 32 == np.arange(16)[None, :]) & (r[:, None] % 32 < 16)
    inv = 1.0 / (np.float32(10000.0) ** (np.arange(0, MLA_ROPE, 2, dtype=np.float32) / MLA_ROPE))
    c[:, C_FREQ] = inv.astype(np.float32)[r % 16]
    c[:, C_SIGN] = np.where(r % 32 < 16, -1, 1)
    return c


COLS = {}
for _name, _n in (("l0_norm_mix", 8), ("l0_mlstm_head_norm", 8), ("l0_norm_ffn", 8), ("final_norm", 8),
                  ("e_g_in_2", 8), ("e_g_q_a_2", 2), ("e_g_kv_a_2", 1), ("o_g_in_2", 8),
                  ("gates", 1), ("o_b_f", 1), ("sinks", 8)):
    COLS[_name] = (sum(n for _, n in COLS.values()), _n)
N_COLS = sum(n for _, n in COLS.values())


class Tally:

    def __init__(self, sem, credit=0):
        self.sem, self.base, self.credit = sem, 0, credit

    def at(self, n):
        return self.base + n

    def passed(self, n):
        self.base += n


class Plan:

    def __init__(self, *parts, after=None, first=0):
        self.parts, self.nb = parts, len(parts)
        self.first = after[0].n(after[1], 0) if after else first
        self.loaded = [after[0].total(after[1], s) if after else 0 for s in range(2)]

    def n(self, i, b):
        return i * self.nb + (self.first + b)

    def total(self, turns, s):
        return self.loaded[s] + 16 * turns * sum(self.parts[s::2])

    def loads(self, i, b):
        s = b % 2
        return i * (16 * sum(self.parts[s::2])) + (self.loaded[s] + 16 * sum(self.parts[s:b + 1:2]))


class Uses:

    def __init__(self, kernel, per_turn):
        self.per_turn = per_turn
        self.free = {**dict(enumerate(kernel.free)), "t0": kernel.tfree[0], "t1": kernel.tfree[1]}

    def clear(self, eng, pair, i, use):
        t = self.free[pair]
        eng.wait_ge(t.sem, t.at(i * self.per_turn[pair] + (use + 1)))

    def over(self, eng, pair, i, use):
        t = self.free[pair]
        eng.wait_ge(t.sem, t.at(i * self.per_turn[pair] + (use + 2)))

    def passed(self, turns):
        for pair, n in self.per_turn.items():
            self.free[pair].passed(n * turns)


class Kernel:
    def __init__(self, nc, dram, ctx):
        self.nc, self.dram = nc, dram

        def sb(name, shape, dt=F32):
            return ctx.enter_context(nc.sbuf_tensor(name, shape, dt))

        self.hhi = sb("hhi", [P, KT, TOK], F32R)
        self.hlo = sb("hlo", [P, KT, TOK], F32R)
        self.whi = sb("whi", [P, 2, KT * P], F32R)
        self.wlo = sb("wlo", [P, 2, KT * P], F32R)
        self.raw = sb("raw", [P, 2, KT * P])
        self.consts = sb("consts", [P, C_TOTAL])
        self.cols = sb("cols", [P, N_COLS])
        self.conv = sb("conv", [P, FT, 8])
        self.small = sb("small", [P, 192])
        self.arena = sb("arena", [P, ARENA_TILES, TOK])
        flat = self.arena[:, :, :].rearrange("p a t -> p (a t)")
        self.flat = flat
        self.x = flat[:, X_AT * TOK:(X_AT + 8) * TOK].rearrange("p (h k c) -> p h k c", h=2, k=KT)
        self.ps = [ctx.enter_context(nc.psum_tensor(f"ps{n}", [P, TOK], F32)) for n in range(4)]
        self.sums = self.small[:, 88:88 + NT]
        self.ident = self.consts[:, C_IDENT:C_IDENT + P]
        self.ones = self.consts[:, C_ONES:C_ONES + P]

        def tally(name, credit=0):
            return Tally(ctx.enter_context(nc.semaphore(name)), credit)

        self.loaded = [tally("weights_loaded0"), tally("weights_loaded1")]
        self.hi_done = tally("weights_hi_done")
        self.split = tally("weights_split", 2)
        self.used = tally("weights_used", 2)
        self.free = [tally(f"pair_free{n}", 1) for n in range(4)]
        self.tfree = [tally(f"transposed_free{n}", 1) for n in range(2)]
        self.dma = [tally(f"dma{n}") for n in range(NT)]
        self.dve_step = tally("dve_step")
        self.act_step = tally("act_step")
        self.pool_step = tally("pool_step")
        self.pe_step = tally("pe_step")
        self.latent_step, self.latent_root, self.latent_pe, self.latent_squared, self.angle_step, self.angle_act = (
            tally(n) for n in ("latent_step", "latent_root", "latent_pe", "latent_squared", "angle_step", "angle_act"))
        self.row_step = tally("row_step")
        self.norm_step, self.norm_root, self.norm_pe_step = (tally(n) for n in ("norm_step", "norm_root", "norm_pe_step"))
        self.ev = {n: tally(n) for n in (
            "squared", "summed", "scaled", "h_hi", "h_split", "evacuated", "act_split", "stored",
            "q_ready", "k_ready", "h_split_vector", "gated", "vt_done", "t_done", "t_out",
            "scores_done", "max_ready", "exp_done", "p_ready", "pv_done", "o_ready", "decay_ready",
            "sk_ready", "rows_ready", "bcast_done")}

    def col(self, name, k=0, n=1, rows=slice(0, P)):
        at = COLS[name][0] + k
        return self.cols[rows, at:at + n]

    def start(self):
        come = self.ev["stored"]
        with self.nc.Block() as block:
            @block.sync
            def _(sp):
                sp.dma_start(self.consts[:, :], self.dram["consts"]).then_inc(come.sem, 16)
                for t in range(NT):
                    sp.dma_start(self.arena[:, t, :], self.dram["x"][t * P:(t + 1) * P, :]).then_inc(self.dma[t].sem, 16)
                sp.dma_start(self.cols[:, :], self.dram["cols"]).then_inc(come.sem, 16)
                sp.dma_start(self.conv[:, :, :], self.dram["conv"]).then_inc(come.sem, 16)
                for t in (self.split, self.used, *self.free, *self.tfree):
                    if t.credit:
                        sp.sem_inc(t.sem, t.credit)
                sp.wait_ge(come.sem, 48)
        come.passed(48)

    def load_weights(self, sp, plan, i, b, parts):
        n, s = plan.n(i, b), b % 2
        sp.wait_ge(self.split.sem, self.split.at(n + 1))
        for dst, src in parts:
            sp.dma_start(dst, src).then_inc(self.loaded[s].sem, 16)

    def slot(self, b, kt, width=P):
        return self.raw[:, b % 2, 0:kt * width].rearrange("p (k c) -> p k c", k=kt)

    def weights_hi(self, act, plan, i, b, width=KT * P):
        n, s = plan.n(i, b), b % 2
        act.wait_ge(self.loaded[s].sem, self.loaded[s].at(plan.loads(i, b)))
        act.wait_ge(self.used.sem, self.used.at(n + 1))
        act.activation(self.whi[:, s, 0:width], self.raw[:, s, 0:width], ACT.Copy).then_inc(self.hi_done.sem, 1)

    def weights_lo(self, pool, plan, i, b, width=KT * P):
        n, s = plan.n(i, b), b % 2
        pool.wait_ge(self.hi_done.sem, self.hi_done.at(n + 1))
        pool.tensor_tensor(self.wlo[:, s, 0:width], self.raw[:, s, 0:width],
                           self.whi[:, s, 0:width].bitcast(F32), ALU.subtract).then_inc(self.split.sem, 1)

    def load_ahead(self, sp, ahead, blocks):
        for b, source in enumerate(blocks):
            self.load_weights(sp, ahead, 0, b, [(self.slot(b, KT), source)])

    def first_blocks(self, name, columns=(0, P)):
        w = self.weights(name)
        return [w[:, :, c:c + P] for c in columns]

    def project(self, pe, plan, i, b, out, weight_tiles, moving, new_h=False, kept=False):
        n, s = plan.n(i, b), b % 2
        pe.wait_ge(self.split.sem, self.split.at(n + 3))
        terms = [(w, k, part) for w, k in zip(weight_tiles, moving) for part in range(3)]
        for at, (w, k, part) in enumerate(terms):
            weights = (self.wlo if part == 2 else self.whi)[:, s, w * P:(w + 1) * P]
            if new_h and part == 0:
                self.h_tile_ready(pe, k)
            if kept and at == len(terms) - 3:
                pe.wait_ge(self.ev["stored"].sem, self.ev["stored"].at(16))
            for h in range(2):
                mov = (self.hlo if part == 1 else self.hhi)[:, k, h * HALF:(h + 1) * HALF]
                mm = pe.matmul(out[:, h * HALF:(h + 1) * HALF], weights, mov,
                               start=at == 0, stop=at == len(terms) - 1)
        mm.then_inc(self.used.sem, 1)

    def passed_blocks(self, plan, turns):
        for s in range(2):
            self.loaded[s].passed(plan.total(turns, s))
        for t in (self.hi_done, self.split, self.used):
            t.passed(plan.n(turns, 0))

    def weights(self, name, rows=None):
        w = self.dram[name]
        return w.rearrange("(k p) n -> p k n", p=P)

    def load_x(self):
        nc, ps, x = self.nc, self.ps, self.x
        free, pe_step = self.free, self.pe_step

        with nc.Block() as block:
            @block.tensor
            def _(pe):
                for t in range(NT):
                    pe.wait_ge(self.dma[t].sem, self.dma[t].at(16))
                    pe.wait_ge(free[t % 4].sem, free[t % 4].at(t // 4 + 1))
                    for k in range(KT):
                        mm = pe.transpose(ps[t % 4][:, k * P:(k + 1) * P], self.arena[:, t, k * P:(k + 1) * P], self.ident)
                    mm.then_inc(pe_step.sem, 1)

            @block.vector
            def _(dve):
                for t in range(NT):
                    dve.wait_ge(pe_step.sem, pe_step.at(t + 1))
                    dve.tensor_copy(x[:, t // 4, :, (t % 4) * P:(t % 4 + 1) * P],
                                    ps[t % 4][:, :].rearrange("p (k c) -> p k c", k=KT)).then_inc(free[t % 4].sem, 1)

            @block.scalar
            def _(act):
                for t in range(NT):
                    act.wait_ge(self.dma[t].sem, self.dma[t].at(16))
                    act.activation(self.arena[:, 8 + t, :], self.arena[:, t, :], ACT.Square,
                                   accum_out=self.sums[:, t:t + 1])
        for n in range(4):
            free[n].passed(2)
        for t in self.dma:
            t.passed(16)
        pe_step.passed(NT)

    def h_part(self, eng, k, source):
        h_hi, by_pool, by_vector = self.ev["h_hi"], self.ev["h_split"], self.ev["h_split_vector"]
        eng.wait_ge(h_hi.sem, h_hi.at(k + 1))
        eng.tensor_tensor(self.hlo[:, k, :], source, self.hhi[:, k, :].bitcast(F32), ALU.subtract)\
           .then_inc((by_pool if k % 2 else by_vector).sem, 1)

    def h_tile_ready(self, pe, k):
        t = self.ev["h_split" if k % 2 else "h_split_vector"]
        pe.wait_ge(t.sem, t.at(k // 2 + 1))

    def h_passed(self):
        self.ev["h_hi"].passed(KT)
        self.ev["h_split"].passed(KT // 2)
        self.ev["h_split_vector"].passed(KT // 2)

    TOTAL_AT = 15

    def norm_act(self, act, into_h=True, summed_before=True):
        squared, summed, scaled, h_hi = (self.ev[n] for n in ("squared", "summed", "scaled", "h_hi"))
        for k in range(0 if summed_before else KT):
            if k >= 2:
                act.wait_ge(summed.sem, summed.at(k - 1))
            act.activation(self.arena[:, k % 2, :].rearrange("p (h c) -> p h c", h=2), self.x[:, :, k, :], ACT.Square)\
               .then_inc(squared.sem, 1)
        r = self.sums
        act.wait_ge(self.norm_step.sem, self.norm_step.at(2))
        act.activation(r, r, ACT.Sqrt).then_inc(self.norm_root.sem, 1)
        if into_h:
            for k in range(KT):
                act.wait_ge(scaled.sem, scaled.at(k + 1))
                act.activation(self.hhi[:, k, :], self.arena[:, 6 + k, :], ACT.Copy).then_inc(h_hi.sem, 1)

    def norm_pool(self, pool):
        for k in range(1, KT, 2):
            self.h_part(pool, k, self.arena[:, 6 + k, :])

    def norm_pe(self, pe, summed_before=True, columns=False):
        ps, summed, pe_step, step = self.ps, self.ev["summed"], self.norm_pe_step, self.norm_step
        total, diagonals = self.arena[:, self.TOTAL_AT, :], self.arena[:, 5, :]
        if not summed_before:
            pe.wait_ge(summed.sem, summed.at(KT))
        if not columns:
            for t in range(NT):
                mm = pe.matmul(ps[2][:, t:t + 1], total[:, t * P:(t + 1) * P], self.ones[:, 0:1], start=True, stop=True)
            mm.then_inc(pe_step.sem, 1)
        pe.wait_ge(step.sem, step.at(3))
        for c in range(2):
            mm = pe.matmul(ps[3][:, c * HALF:(c + 1) * HALF], self.ones, diagonals[:, c * HALF:(c + 1) * HALF],
                           start=True, stop=True)
        mm.then_inc(pe_step.sem, 1)

    def norm_dve(self, dve, gain, into_h=True, summed_before=True, columns=False):
        x, ps, step, pe_step = self.x, self.ps, self.norm_step, self.norm_pe_step
        squared, summed, scaled = self.ev["squared"], self.ev["summed"], self.ev["scaled"]
        total = self.arena[:, self.TOTAL_AT, :]
        r = self.sums
        halves = lambda a: a.rearrange("p (h c) -> p h c", h=2)
        for k in range(0 if summed_before else KT):
            dve.wait_ge(squared.sem, squared.at(k + 1))
            if k:
                dve.wait_ge(summed.sem, summed.at(k))
                dve.tensor_tensor(total, total, self.arena[:, k % 2, :], ALU.add).then_inc(summed.sem, 1)
            else:
                dve.tensor_copy(total, self.arena[:, 0, :]).then_inc(summed.sem, 1)
        if not columns:
            dve.wait_ge(pe_step.sem, pe_step.at(1))
        dve.tensor_scalar(r, self.sums if columns else ps[2][:, 0:NT], 1.0 / D, EPS, ALU.mult, ALU.add)\
           .then_inc(step.sem, 1)
        dve.wait_ge(step.sem, step.at(1))
        dve.reciprocal(r, r).then_inc(step.sem, 1)
        dve.wait_ge(self.norm_root.sem, self.norm_root.at(1))
        dve.tensor_tensor(self.arena[:, 5, :].rearrange("p (t c) -> p t c", t=NT),
                          self.ident.unsqueeze(1).broadcast_to((P, NT, P)),
                          r.unsqueeze(2).broadcast_to((P, NT, P)), ALU.mult).then_inc(step.sem, 1)
        dve.wait_ge(pe_step.sem, pe_step.at(1 if columns else 2))
        for k in range(KT):
            out = halves(self.arena[:, 6 + k, :]) if into_h else x[:, :, k, :]
            dve.scalar_tensor_tensor(out, x[:, :, k, :], self.col(gain, k), halves(ps[3][:, :]),
                                     ALU.mult, ALU.mult).then_inc(scaled.sem, 1)
            if into_h and k % 2:
                self.h_part(dve, k - 1, self.arena[:, 5 + k, :])

    def norm_passed(self, into_h=True, summed_before=True, columns=False):
        self.ev["scaled"].passed(KT)
        if not summed_before:
            self.ev["squared"].passed(KT)
            self.ev["summed"].passed(KT)
        self.norm_step.passed(3)
        self.norm_root.passed(1)
        self.norm_pe_step.passed(1 if columns else 2)
        if into_h:
            self.h_passed()
            self.ev["stored"].passed(16)

    def keep_x(self, sp):
        sp.dma_start(self.dram["x_kept"], self.x).then_inc(self.ev["stored"].sem, 16)

    def norm(self, gain):
        with self.nc.Block() as block:
            @block.scalar
            def _(act):
                self.norm_act(act, into_h=False)

            @block.tensor
            def _(pe):
                self.norm_pe(pe)

            @block.vector
            def _(dve):
                self.norm_dve(dve, gain, into_h=False)
        self.norm_passed(into_h=False)

    def out_projection(self, name):
        nc, ps, x = self.nc, self.ps, self.x
        plan, turns = Plan(1, 1), KT // 2
        w = self.weights(name)
        kept = [self.arena[:, n, :].rearrange("p (h c) -> p h c", h=2) for n in (26, 27)]
        used, free, dma = self.used, self.free, self.dma
        new, square, total = [self.arena[:, n, :] for n in (8, 9)], [self.arena[:, n, :] for n in (0, 1)], self.arena[:, self.TOTAL_AT, :]
        copied, squared, summed = self.ev["scaled"], self.ev["squared"], self.ev["summed"]
        halves = lambda a: a.rearrange("p (h c) -> p h c", h=2)
        with nc.Block() as block:
            @block.sync
            def _(sp):
                def residual(i, b):
                    sp.wait_ge(free[b].sem, free[b].at(i + 1))
                    sp.dma_start(kept[b], self.dram["x_kept"][:, :, bass.ds(i * 2 + b, 1), :]).then_inc(dma[b].sem, 16)

                residual(0, 0)
                residual(0, 1)
                with sp.Fori(1, turns) as i:
                    for b in range(2):
                        self.load_weights(sp, plan, i, b, [(self.slot(b, KT), w[:, :, bass.ds(i * (2 * P) + b * P, P)])])
                        residual(i, b)

            @block.scalar
            def _(act):
                for k in range(KT):
                    act.activation(self.hhi[:, k, :], self.arena[:, k, :], ACT.Copy).then_inc(self.ev["h_hi"].sem, 1)
                def turn(i, last=False):
                    for b in range(2):
                        if not last:
                            self.weights_hi(act, plan, i + 1, b)
                        act.wait_ge(free[b].sem, free[b].at(i + 2))
                        act.activation(square[b], new[b], ACT.Square).then_inc(squared.sem, 1)

                with act.Fori(0, turns - 1) as i:
                    turn(i)
                turn(turns - 1, last=True)

            @block.gpsimd
            def _(pool):
                for k in range(1, KT, 2):
                    self.h_part(pool, k, self.arena[:, k, :])
                with pool.Fori(1, turns) as i:
                    for b in range(2):
                        self.weights_lo(pool, plan, i, b)

            @block.tensor
            def _(pe):
                for b in range(2):
                    self.project(pe, plan, 0, b, ps[b], range(KT), range(KT), new_h=b == 0)
                with pe.Fori(1, turns) as i:
                    for b in range(2):
                        pe.wait_ge(free[b].sem, free[b].at(i + 1))
                        self.project(pe, plan, i, b, ps[b], range(KT), range(KT))

            @block.vector
            def _(dve):
                for k in range(0, KT, 2):
                    self.h_part(dve, k, self.arena[:, k, :])
                def add(n, b):
                    dve.wait_ge(squared.sem, squared.at(n + 1))
                    dve.wait_ge(summed.sem, summed.at(n + 1))
                    dve.tensor_tensor(total, total, square[b], ALU.add).then_inc(summed.sem, 1)

                def turn(i, first=False):
                    for b in range(2):
                        n = plan.n(i, b)
                        dve.wait_ge(used.sem, used.at(n + 3))
                        dve.wait_ge(dma[b].sem, dma[b].at(i * 16 + 16))
                        if first and b == 0:
                            dve.memset(total, 0.0).then_inc(summed.sem, 1)
                        if not first:
                            dve.wait_ge(copied.sem, copied.at(n - 1))
                        dve.tensor_tensor(halves(new[b]), halves(ps[b][:, :]), kept[b], ALU.add).then_inc(free[b].sem, 1)
                        dve.wait_ge(free[b].sem, free[b].at(i + 2))
                        dve.tensor_scalar(x[:, :, bass.ds(i * 2 + b, 1), :].rearrange("p h k c -> p h (k c)"),
                                          halves(new[b]), 1.0, None, ALU.mult).then_inc(copied.sem, 1)
                        if not (first and b == 0):
                            add(n - 1, 1 - b)

                turn(0, first=True)
                with dve.Fori(1, turns) as i:
                    turn(i)
                add(KT - 1, 1)
        self.passed_blocks(plan, turns)
        self.h_passed()
        copied.passed(KT)
        squared.passed(KT)
        summed.passed(KT + 1)
        for b in range(2):
            free[b].passed(turns)
            dma[b].passed(16 * turns)

    def store(self):
        nc, ps, x, dma = self.nc, self.ps, self.x, self.dma
        free, pe_step, squared, step, root = self.free, self.pe_step, self.ev["squared"], self.norm_step, self.norm_root
        gain, gain_come, r = self.arena[:, 17, :], self.ev["stored"], self.sums
        with nc.Block() as block:
            @block.tensor
            def _(pe):
                for t in range(NT):
                    pe.wait_ge(free[t % 4].sem, free[t % 4].at(t // 4 + 1))
                    for k in range(KT):
                        mm = pe.transpose(ps[t % 4][:, k * P:(k + 1) * P],
                                          x[:, t // 4, k, (t % 4) * P:(t % 4 + 1) * P], self.ident)
                    mm.then_inc(pe_step.sem, 1)

            @block.scalar
            def _(act):
                for g in range(NT // 4):
                    cols = r[:, 4 * g:4 * g + 4]
                    for t in range(4 * g, 4 * g + 4):
                        act.wait_ge(pe_step.sem, pe_step.at(t + 1))
                        act.activation(self.arena[:, 8 + t, :], ps[t % 4][:, :], ACT.Square, accum_out=r[:, t:t + 1])\
                           .then_inc(squared.sem, 1)
                    act.wait_ge(step.sem, step.at(2 * g + 2))
                    act.activation(cols, cols, ACT.Sqrt).then_inc(root.sem, 1)

            @block.vector
            def _(dve):
                dve.wait_ge(gain_come.sem, gain_come.at(16))
                for g in range(NT // 4):
                    cols = r[:, 4 * g:4 * g + 4]
                    dve.wait_ge(squared.sem, squared.at(4 * g + 4))
                    dve.tensor_scalar(cols, cols, 1.0 / D, EPS, ALU.mult, ALU.add).then_inc(step.sem, 1)
                    dve.wait_ge(step.sem, step.at(2 * g + 1))
                    dve.reciprocal(cols, cols).then_inc(step.sem, 1)
                    dve.wait_ge(root.sem, root.at(g + 1))
                    for t in range(4 * g, 4 * g + 4):
                        dve.scalar_tensor_tensor(self.arena[:, t, :], ps[t % 4][:, :], r[:, t:t + 1], gain,
                                                 ALU.mult, ALU.mult).then_inc(free[t % 4].sem, 1)

            @block.sync
            def _(sp):
                sp.dma_start(gain, self.dram["g_final"].partition_broadcast(P)).then_inc(gain_come.sem, 16)
                for t in range(NT):
                    sp.wait_ge(free[t % 4].sem, free[t % 4].at(t // 4 + 2))
                    sp.dma_start(self.dram["out"][t * P:(t + 1) * P, :], self.arena[:, t, :]).then_inc(dma[t].sem, 16)
                for t in range(NT):
                    sp.wait_ge(dma[t].sem, dma[t].at(16))
        for n in range(4):
            free[n].passed(2)
        for t in dma:
            t.passed(16)
        for t, n in ((pe_step, NT), (squared, NT), (step, 4), (root, 2), (gain_come, 16)):
            t.passed(n)

    def gates(self, gain, name, parts, bias, tile, next_blocks, columns=False):
        nc, ps = self.nc, self.ps
        plan = Plan(0, len(parts), first=-1)
        ahead = Plan(1, 1, after=(plan, 1))
        w = self.weights(name)
        cleared, out = self.pool_step, self.ev["evacuated"]
        with nc.Block() as block:
            @block.gpsimd
            def _(pool):
                pool.memset(self.raw[:, 1, :], 0.0).then_inc(cleared.sem, 1)
                self.weights_lo(pool, plan, 0, 1)
                self.weights_lo(pool, ahead, 0, 0)
                self.norm_pool(pool)
                self.weights_lo(pool, ahead, 0, 1)

            @block.sync
            def _(sp):
                sp.wait_ge(cleared.sem, cleared.at(1))
                self.load_weights(sp, plan, 0, 1, [(self.slot(1, KT)[:, :, at:at + n], w[:, :, c:c + n])
                                                   for at, c, n in parts])
                first, second = self.first_blocks(name, next_blocks)
                self.load_weights(sp, ahead, 0, 0, [(self.slot(0, KT), first)])
                self.keep_x(sp)
                self.load_weights(sp, ahead, 0, 1, [(self.slot(1, KT), second)])

            @block.scalar
            def _(act):
                self.weights_hi(act, plan, 0, 1)
                self.weights_hi(act, ahead, 0, 0)
                self.norm_act(act)
                act.wait_ge(self.used.sem, self.used.at(3))
                act.activation(self.arena[:, tile, :], ps[0][:, :], ACT.Identity, bias=self.col(bias))\
                   .then_inc(out.sem, 1)
                self.weights_hi(act, ahead, 0, 1)

            @block.tensor
            def _(pe):
                self.norm_pe(pe, columns=columns)
                self.project(pe, plan, 0, 1, ps[0], range(KT), range(KT), new_h=True, kept=True)

            @block.vector
            def _(dve):
                self.norm_dve(dve, gain, columns=columns)
        self.norm_passed(columns=columns)
        self.passed_blocks(plan, 1)
        cleared.passed(1)
        out.passed(1)

    def log_forget(self, act, dve, z, tmp, out, n):
        a, d = self.act_step, self.row_step
        if act is not None:
            act.activation(tmp, z, ACT.Abs).then_inc(a.sem, 1)
            act.wait_ge(a.sem, a.at(1))
            act.activation(tmp, tmp, ACT.Exp, scale=-1.0).then_inc(a.sem, 1)
            act.wait_ge(a.sem, a.at(2))
            act.activation(tmp, tmp, ACT.Ln, bias=self.ones[0:n, 0:1]).then_inc(a.sem, 1)
        else:
            dve.wait_ge(a.sem, a.at(3))
            dve.scalar_tensor_tensor(out, z, 0.0, tmp, ALU.min, ALU.subtract).then_inc(d.sem, 1)

    def mlstm_row_tiles(self):
        return [self.arena[0:M_HEADS, k, :] for k in (10, 11, 12, 13, 14, 15, 16)]

    def mlstm_rows_pool(self, pool):
        pool.memset(self.mlstm_row_tiles()[4], 1.0).then_inc(self.pool_step.sem, 1)

    def mlstm_rows_act(self, act):
        _, z, tmp, lf, _, _, _ = self.mlstm_row_tiles()
        act.wait_ge(self.row_step.sem, self.row_step.at(1))
        self.log_forget(act, None, z, tmp, lf, M_HEADS)

    def mlstm_rows_pe(self, pe):
        pe.wait_ge(self.row_step.sem, self.row_step.at(5))
        for t in range(NT):
            mm = pe.transpose(self.ps[3][:, t * M_HEADS:(t + 1) * M_HEADS],
                              self.mlstm_row_tiles()[6][:, t * P:(t + 1) * P], self.ident[0:M_HEADS, 0:M_HEADS])
        mm.then_inc(self.pe_step.sem, 1)

    def mlstm_rows_dve(self, dve):
        n = M_HEADS
        logits, z, tmp, lf, one, f, a = self.mlstm_row_tiles()
        row, d, pl = self.arena[:, 27, :], self.row_step, self.pool_step
        dve.tensor_copy(z, self.arena[32:32 + n, 10, :]).then_inc(d.sem, 1)
        self.log_forget(None, dve, z, tmp, lf, n)
        dve.wait_ge(d.sem, d.at(2))
        dve.wait_ge(pl.sem, pl.at(1))
        dve.tensor_tensor_scan(f, one, lf, 0.0, ALU.mult, ALU.add).then_inc(d.sem, 1)
        dve.wait_ge(d.sem, d.at(3))
        dve.tensor_tensor(a, logits, f, ALU.subtract).then_inc(d.sem, 1)
        dve.wait_ge(d.sem, d.at(4))
        dve.tensor_tensor_scan(row[0:n, :], a, a, 0.0, ALU.max, ALU.max).then_inc(d.sem, 1)
        dve.wait_ge(d.sem, d.at(5))
        dve.scalar_tensor_tensor(row[96:96 + n, :], f, -1.0, row[0:n, :], ALU.mult, ALU.subtract).then_inc(d.sem, 1)
        dve.wait_ge(self.pe_step.sem, self.pe_step.at(1))
        dve.tensor_copy(self.small[:, 8:8 + NT * n], self.ps[3][:, 0:NT * n]).then_inc(d.sem, 1)
        dve.wait_ge(d.sem, d.at(7))

    def mlstm_rows_passed(self):
        self.row_step.passed(7)
        self.act_step.passed(3)
        self.pool_step.passed(1)
        self.pe_step.passed(1)

    def mlstm_heads(self):
        nc, ps, A = self.nc, self.ps, self.arena
        w = self.weights("l0_mlstm_w_in")
        plan, turns = Plan(1, 1, 1, 1, 1, 1), M_HEADS
        used, free, tfree = self.used, self.free, self.tfree
        O = A[:, 0:8, :]
        SSQ = A[:, 8:12, :]
        q, k = A[:, 19, :], A[:, 20, :]
        E = [A[:, 21, :], A[:, 22, :]]
        VT = E
        OG = [A[:, 23, :], A[:, 24, :]]
        MB, EM = A[:, 25, :], A[:, 26, :]
        V = self.flat[:, 17 * TOK:19 * TOK].rearrange("p (t v) -> p t v", t=NT)
        rows = A[:, 27, :]
        AB = E[0]
        HT = [MB, E[1]]
        sk_at = [12 * TOK + sum(TOK - P * r for r in range(s)) - P * s for s in range(NT)]
        sk = [self.flat[:, at:at + TOK] for at in sk_at]
        masked = [self.flat[:, 16896 + n * P:16896 + (n + 1) * P] for n in range(2)]
        a_cols = self.small[:, 8:8 + NT * M_HEADS].rearrange("p (t h) -> p t h", h=M_HEADS)
        a_head, gain = self.small[:, 40:48], self.small[:, 48:50]
        ev = self.ev
        v_turned, picked, bcast = ev["vt_done"], ev["rows_ready"], ev["bcast_done"]
        scores, decay, masked_ready = ev["scores_done"], ev["exp_done"], ev["max_ready"]
        sums, absd, squared, head_done = ev["pv_done"], ev["p_ready"], ev["squared"], ev["o_ready"]
        step = self.dve_step
        STEPS = 9
        uses = Uses(self, {0: 8, 1: 7, 3: 3, "t0": 3, "t1": 3})
        columns = (lambda i: i * M_DQK, lambda i: i * M_DQK + M_QK,
                   lambda i: i * M_DV + 2 * M_QK, lambda i: i * M_DV + (2 * M_QK + P),
                   lambda i: i * M_DV + (2 * M_QK + M_V), lambda i: i * M_DV + (2 * M_QK + M_V + P))

        def pair(b):
            return 1 - b % 2

        def num_bank(th, n):
            return (ps[2] if th == 0 else ps[0])[:, n * HALF:(n + 1) * HALF]

        with nc.Block() as block:
            @block.sync
            def _(sp):
                def loads(i, b):
                    self.load_weights(sp, plan, i, b, [(self.slot(b, KT), w[:, :, bass.ds(columns[b](i), P)])])

                for b in range(2, 6):
                    loads(0, b)
                with sp.Fori(1, turns) as i:
                    for b in range(6):
                        loads(i, b)

            @block.gpsimd
            def _(pool):
                self.mlstm_rows_pool(pool)
                for b in range(2, 6):
                    self.weights_lo(pool, plan, 0, b)
                with pool.Fori(1, turns) as i:
                    for b in range(6):
                        self.weights_lo(pool, plan, i, b)

            @block.tensor
            def _(pe):
                def turn(i, first=False):
                    for b in range(6):
                        uses.clear(pe, pair(b), i, b // 2)
                        self.project(pe, plan, i, b, ps[pair(b)], range(KT), range(KT))
                        if first and b == 1:
                            self.mlstm_rows_pe(pe)
                        if b < 4:
                            continue
                        dv = b - 4
                        uses.over(pe, pair(dv), i, 1)
                        for g in range(2):
                            uses.clear(pe, f"t{g}", i, dv)
                            for t in range(4):
                                mm = pe.transpose(ps[2][:, g * HALF + t * P:g * HALF + (t + 1) * P],
                                                  VT[dv][:, (g * 4 + t) * P:(g * 4 + t + 1) * P], self.ident)
                            mm.then_inc(v_turned.sem, 1)
                    for r in range(2):
                        pe.wait_ge(picked.sem, picked.at(i * 2 + (r + 1)))
                        uses.clear(pe, 3, i, r)
                        at = 64 if r else 32
                        for c in range(2):
                            mm = pe.matmul(ps[3][:, c * HALF:(c + 1) * HALF], self.ones[at:at + M_HEADS, :],
                                           rows[at:at + M_HEADS, c * HALF:(c + 1) * HALF], start=True, stop=True)
                        mm.then_inc(bcast.sem, 1)
                    uses.over(pe, 1, i, 0)
                    uses.over(pe, 0, i, 0)
                    for s in range(NT):
                        uses.clear(pe, s % 2, i, 3 + s // 2)
                        for lo, hi in ((s * P, HALF), (max(s * P, HALF), TOK)):
                            if lo < hi:
                                mm = pe.matmul(ps[s % 2][:, lo:hi], k[:, s * P:(s + 1) * P], q[:, lo:hi],
                                               start=True, stop=True)
                        mm.then_inc(scores.sem, 1)
                    for g in range(2):
                        uses.over(pe, f"t{g}", i, 1)
                    for th in range(2):
                        if th == 0:
                            for g in range(2):
                                uses.clear(pe, f"t{g}", i, 2)
                            uses.clear(pe, 3, i, 2)
                        else:
                            uses.clear(pe, 0, i, 7)
                        tiles = 4 * (th + 1)
                        for n in range(3):
                            for s in range(tiles):
                                if n == 0:
                                    uses.over(pe, s % 2, i, 3 + s // 2)
                                lo = max(s * P, th * HALF)
                                out = num_bank(th, n) if n < 2 else ps[3][:, th * HALF:(th + 1) * HALF]
                                mm = pe.matmul(out[:, lo - th * HALF:HALF],
                                               V[:, s, n * P:(n + 1) * P] if n < 2 else self.ones,
                                               sk[s][:, lo:(th + 1) * HALF], start=s == 0, stop=s == tiles - 1,
                                               skip_group_check=True)
                        mm.then_inc(sums.sem, 1)

                turn(0, first=True)
                with pe.Fori(1, turns) as i:
                    turn(i)

            @block.scalar
            def _(act):
                act.sem_inc(head_done.sem, 1)
                self.mlstm_rows_act(act)
                def turn(i, last=False):
                    for b in range(6):
                        if b == 2:
                            act.wait_ge(head_done.sem, head_done.at(i + 1))
                        act.wait_ge(used.sem, used.at(plan.n(i, b) + 3))
                        out, func = ((q, ACT.Copy), (k, ACT.Copy), (VT[0], ACT.Copy), (VT[1], ACT.Copy),
                                     (OG[0], ACT.Sigmoid), (OG[1], ACT.Sigmoid))[b]
                        act.activation(out, ps[pair(b)][:, :], func, scale=M_DQK ** -0.5 if b == 0 else 1.0)\
                           .then_inc(free[pair(b)].sem, 1)
                        if b + 2 < 6:
                            self.weights_hi(act, plan, i, b + 2)
                    for dv in range(2):
                        for g in range(2):
                            act.wait_ge(v_turned.sem, v_turned.at(i * 4 + (dv * 2 + g + 1)))
                            act.activation(V[:, g * 4:g * 4 + 4, dv * P:(dv + 1) * P],
                                           ps[2][:, g * HALF:(g + 1) * HALF].rearrange("p (t v) -> p t v", t=4),
                                           ACT.Copy).then_inc(tfree[g].sem, 1)
                    if not last:
                        for b in range(2):
                            self.weights_hi(act, plan, i + 1, b)
                    act.wait_ge(bcast.sem, bcast.at(i * 2 + 2))
                    act.activation(EM, ps[3][:, :], ACT.Exp).then_inc(free[3].sem, 1)
                    for s in range(NT):
                        act.wait_ge(masked_ready.sem, masked_ready.at(i * NT + (s + 1)))
                        if s >= 2:
                            uses.over(act, s % 2, i, 2 + s // 2)
                        if s < NT - 1:
                            act.activation(E[s % 2][:, (s + 1) * P:], MB[:, (s + 1) * P:], ACT.Exp, scale=-1.0,
                                           bias=a_head[:, s:s + 1])
                        act.activation(E[s % 2][:, s * P:(s + 1) * P], masked[s % 2], ACT.Exp, scale=-1.0,
                                       bias=a_head[:, s:s + 1]).then_inc(decay.sem, 1)
                    uses.over(act, 0, i, 6)
                    act.wait_ge(sums.sem, sums.at(i * 2 + 1))
                    act.activation(AB[:, 0:HALF], ps[3][:, 0:HALF], ACT.Abs).then_inc(absd.sem, 1)
                    act.wait_ge(sums.sem, sums.at(i * 2 + 2))
                    act.activation(AB[:, HALF:TOK], ps[3][:, HALF:TOK], ACT.Abs).then_inc(free[3].sem, 1)
                    uses.over(act, "t1", i, 2)
                    act.activation(EM[:, 0:HALF], HT[0][:, HALF:TOK], ACT.Square).then_inc(squared.sem, 1)
                    uses.over(act, 0, i, 7)
                    act.activation(EM[:, HALF:TOK], HT[1][:, HALF:TOK], ACT.Square).then_inc(squared.sem, 1)

                with act.Fori(0, turns - 1) as i:
                    turn(i)
                turn(turns - 1, last=True)

            @block.vector
            def _(dve):
                self.mlstm_rows_dve(dve)
                with dve.Fori(0, turns) as i:
                    count = [0]

                    def done(ins):
                        count[0] += 1
                        ins.then_inc(step.sem, 1)
                        dve.wait_ge(step.sem, step.at(i * STEPS + count[0]))

                    done(dve.tensor_scalar(a_head, a_cols[:, :, bass.ds(i, 1)].rearrange("p t h -> p (t h)"),
                                           1.0, None, ALU.mult))
                    at = COLS["l0_mlstm_head_norm"][0]
                    done(dve.tensor_scalar(gain, self.cols[:, bass.ds(i * 2 + at, 2)], 1.0, None, ALU.mult))
                    for r in range(2):
                        to = 64 if r else 32
                        dve.tensor_scalar(rows[to:to + M_HEADS, :], rows[96 * r:96 * r + M_HEADS, :],
                                          self.consts[96 * r:96 * r + M_HEADS, bass.ds(i + C_ONEHOT, 1)], None,
                                          ALU.mult).then_inc(picked.sem, 1)
                    dve.wait_ge(bcast.sem, bcast.at(i * 2 + 1))
                    dve.tensor_copy(MB, ps[3][:, :]).then_inc(free[3].sem, 1)
                    uses.over(dve, 3, i, 0)

                    def mask(s):
                        dve.tensor_tensor(masked[s % 2], MB[:, s * P:(s + 1) * P],
                                          self.consts[:, C_LATER:C_LATER + P], ALU.add)\
                           .then_inc(masked_ready.sem, 1)

                    mask(0)
                    mask(1)
                    for s in range(NT):
                        dve.wait_ge(scores.sem, scores.at(i * NT + (s + 1)))
                        dve.wait_ge(decay.sem, decay.at(i * NT + (s + 1)))
                        dve.tensor_tensor(sk[s][:, s * P:], ps[s % 2][:, s * P:], E[s % 2][:, s * P:], ALU.mult)\
                           .then_inc(free[s % 2].sem, 1)
                        if s + 2 < NT:
                            mask(s + 2)
                    for th in range(2):
                        cols = slice(th * HALF, (th + 1) * HALF)
                        if th == 0:
                            dve.wait_ge(absd.sem, absd.at(i + 1))
                        else:
                            uses.over(dve, 3, i, 2)
                        done(dve.tensor_tensor(AB[:, cols], AB[:, cols], EM[:, cols], ALU.max))
                        done(dve.reciprocal(AB[:, cols], AB[:, cols]))
                        if th == 0:
                            dve.tensor_tensor(HT[0][:, 0:HALF], num_bank(0, 0), AB[:, cols], ALU.mult)\
                               .then_inc(tfree[0].sem, 1)
                            dve.tensor_tensor(HT[0][:, HALF:TOK], num_bank(0, 1), AB[:, cols], ALU.mult)\
                               .then_inc(tfree[1].sem, 1)
                            uses.over(dve, "t0", i, 2)
                            uses.over(dve, "t1", i, 2)
                        else:
                            done(dve.tensor_tensor(HT[1][:, 0:HALF], num_bank(1, 0), AB[:, cols], ALU.mult))
                            dve.tensor_tensor(HT[1][:, HALF:TOK], num_bank(1, 1), AB[:, cols], ALU.mult)\
                               .then_inc(free[0].sem, 1)
                            uses.over(dve, 0, i, 7)
                        for n in range(2):
                            out = O[:, bass.ds(i * 2 + n, 1), cols].rearrange("p f c -> p (f c)")
                            dve.scalar_tensor_tensor(out, HT[th][:, n * HALF:(n + 1) * HALF], gain[:, n:n + 1],
                                                     OG[n][:, cols], ALU.mult, ALU.mult)
                        ssq = SSQ[:, bass.ds(i, 1), cols].rearrange("p f c -> p (f c)")
                        done(dve.tensor_tensor(ssq, HT[th][:, 0:HALF], HT[th][:, 0:HALF], ALU.mult))
                        dve.wait_ge(squared.sem, squared.at(i * 2 + (th + 1)))
                        last = dve.tensor_tensor(ssq, ssq, EM[:, cols], ALU.add)
                    last.then_inc(head_done.sem, 1)
                    assert count[0] == STEPS, count
        self.mlstm_rows_passed()
        self.passed_blocks(plan, turns)
        uses.passed(turns)
        for t, n in ((v_turned, 4), (picked, 2), (bcast, 2), (scores, NT), (decay, NT), (masked_ready, NT),
                     (sums, 2), (absd, 1), (squared, 2), (step, STEPS)):
            t.passed(turns * n)
        head_done.passed(turns + 1)

    def mlstm_norm(self):
        nc, ps, A = self.nc, self.ps, self.arena
        step, pe_step, act_step = self.dve_step, self.pe_step, self.act_step
        r = self.small[:, 88:88 + M_HEADS * NT]
        diagonals = [A[:, 12 + h, :] for h in range(M_HEADS)]
        ahead = Plan(1, 1)
        with nc.Block() as block:
            @block.sync
            def _(sp):
                self.load_ahead(sp, ahead, self.first_blocks("l0_mlstm_w_out"))

            @block.gpsimd
            def _(pool):
                for b in range(2):
                    self.weights_lo(pool, ahead, 0, b)

            @block.tensor
            def _(pe):
                for h in range(M_HEADS):
                    for t in range(NT):
                        mm = pe.matmul(ps[0][:, h * NT + t:h * NT + t + 1], A[:, 8 + h, t * P:(t + 1) * P],
                                       self.ones[:, 0:1], start=True, stop=True)
                mm.then_inc(pe_step.sem, 1)
                for h in range(M_HEADS):
                    pe.wait_ge(step.sem, step.at(3 + h))
                    for c in range(2):
                        mm = pe.matmul(ps[h][:, c * HALF:(c + 1) * HALF], self.ones,
                                       diagonals[h][:, c * HALF:(c + 1) * HALF], start=True, stop=True)
                    mm.then_inc(pe_step.sem, 1)

            @block.scalar
            def _(act):
                act.wait_ge(step.sem, step.at(2))
                act.activation(r, r, ACT.Sqrt).then_inc(act_step.sem, 1)
                for b in range(2):
                    self.weights_hi(act, ahead, 0, b)

            @block.vector
            def _(dve):
                dve.wait_ge(pe_step.sem, pe_step.at(1))
                dve.tensor_scalar(r, ps[0][:, 0:M_HEADS * NT], 1.0 / M_DV, EPS, ALU.mult, ALU.add).then_inc(step.sem, 1)
                dve.wait_ge(step.sem, step.at(1))
                dve.reciprocal(r, r).then_inc(step.sem, 1)
                dve.wait_ge(act_step.sem, act_step.at(1))

                def diagonal(h):
                    dve.tensor_tensor(diagonals[h].rearrange("p (t c) -> p t c", t=NT),
                                      self.ident.unsqueeze(1).broadcast_to((P, NT, P)),
                                      r[:, h * NT:(h + 1) * NT].unsqueeze(2).broadcast_to((P, NT, P)), ALU.mult)\
                       .then_inc(step.sem, 1)

                diagonal(0)
                for h in range(M_HEADS):
                    if h + 1 < M_HEADS:
                        diagonal(h + 1)
                    dve.wait_ge(pe_step.sem, pe_step.at(h + 2))
                    for n in range(2):
                        dve.tensor_tensor(A[:, 2 * h + n, :], A[:, 2 * h + n, :], ps[h][:, :], ALU.mult)
        step.passed(2 + M_HEADS)
        pe_step.passed(1 + M_HEADS)
        act_step.passed(1)

    def ffn_up(self, gain):
        nc, ps = self.nc, self.ps
        plan, turns = Plan(1, 1), FT
        w = self.weights("l0_ffn_w_up")
        act_t = self.flat[:, 0:FT * TOK].rearrange("p (h f c) -> p h f c", h=2, f=FT)
        conv_out = [self.arena[:, FT + n, :] for n in range(2)]
        gate, prod = self.arena[:, FT + 2, :], self.arena[:, FT + 3, :]
        taps = self.small[:, 0:8]
        halves = lambda a: a.rearrange("p (h c) -> p h c", h=2)
        used, free = self.used, self.free
        start, gated, taps_ready = (self.ev[n] for n in ("exp_done", "max_ready", "q_ready"))
        written, step = self.ev["act_split"], self.dve_step
        with nc.Block() as block:
            @block.sync
            def _(sp):
                def loads(i):
                    for b in range(2):
                        self.load_weights(sp, plan, i, b, [(self.slot(b, KT), w[:, :, bass.ds(i * P + b * D_FF, P)])])

                loads(0)
                self.keep_x(sp)
                with sp.Fori(1, turns) as i:
                    loads(i)
                for b in range(2):
                    self.load_weights(sp, plan, turns, b, [(self.raw[:, b, :], self.dram["l0_ffn_w_down"][b * P:(b + 1) * P, :])])

            @block.gpsimd
            def _(pool):
                for b in range(2):
                    self.weights_lo(pool, plan, 0, b)
                self.norm_pool(pool)
                with pool.Fori(1, turns) as i:
                    for b in range(2):
                        self.weights_lo(pool, plan, i, b)
                for b in range(2):
                    self.weights_lo(pool, plan, turns, b)

            @block.tensor
            def _(pe):
                self.norm_pe(pe)
                for b in range(2):
                    self.project(pe, plan, 0, b, ps[b], range(KT), range(KT), new_h=b == 0, kept=b == 0)
                with pe.Fori(1, turns) as i:
                    for b in range(2):
                        pe.wait_ge(free[b].sem, free[b].at(i + 1))
                        self.project(pe, plan, i, b, ps[b], range(KT), range(KT))

            @block.scalar
            def _(act):
                act.sem_inc(written.sem, 1)
                for b in range(2):
                    self.weights_hi(act, plan, 0, b)
                self.norm_act(act)
                with act.Fori(0, turns) as i:
                    for b in range(2):
                        self.weights_hi(act, plan, i + 1, b)
                        act.wait_ge(used.sem, used.at(plan.n(i, b) + 3))
                        act.wait_ge(taps_ready.sem, taps_ready.at(i + 1))
                        if b == 0:
                            act.wait_ge(written.sem, written.at(i + 1))
                        act.activation(conv_out[b], ps[b][:, :], ACT.Identity, scale=taps[:, b * 4 + 2:b * 4 + 3],
                                       bias=taps[:, b * 4 + 3:b * 4 + 4]).then_inc(start.sem, 1)
                    act.wait_ge(free[0].sem, free[0].at(i + 2))
                    act.activation(gate, conv_out[0], ACT.Sigmoid).then_inc(gated.sem, 1)

            @block.vector
            def _(dve):
                self.norm_dve(dve, gain)
                with dve.Fori(0, turns) as i:
                    dve.wait_ge(written.sem, written.at(i + 1))
                    dve.tensor_scalar(taps, self.conv[:, bass.ds(i, 1), :].rearrange("p f c -> p (f c)"),
                                      1.0, None, ALU.mult).then_inc(taps_ready.sem, 1)
                    dve.wait_ge(taps_ready.sem, taps_ready.at(i + 1))
                    for b in range(2):
                        dve.wait_ge(start.sem, start.at(i * 2 + b + 1))
                        dve.scalar_tensor_tensor(conv_out[b][:, 1:TOK], ps[b][:, 0:TOK - 1], taps[:, b * 4 + 1:b * 4 + 2],
                                                 conv_out[b][:, 1:TOK], ALU.mult, ALU.add).then_inc(step.sem, 1)
                        dve.wait_ge(step.sem, step.at(i * 3 + b + 1))
                        dve.scalar_tensor_tensor(conv_out[b][:, 2:TOK], ps[b][:, 0:TOK - 2], taps[:, b * 4:b * 4 + 1],
                                                 conv_out[b][:, 2:TOK], ALU.mult, ALU.add).then_inc(free[b].sem, 1)
                        dve.wait_ge(free[b].sem, free[b].at(i + 2))
                    dve.tensor_tensor(prod, conv_out[0], conv_out[1], ALU.mult).then_inc(step.sem, 1)
                    dve.wait_ge(step.sem, step.at(i * 3 + 3))
                    dve.wait_ge(gated.sem, gated.at(i + 1))
                    dve.tensor_tensor(act_t[:, :, bass.ds(i, 1), :].rearrange("p h f c -> p h (f c)"),
                                      halves(prod), halves(gate), ALU.mult).then_inc(written.sem, 1)
        self.norm_passed()
        self.passed_blocks(plan, turns)
        for b in range(2):
            free[b].passed(turns)
        start.passed(2 * turns)
        gated.passed(turns)
        taps_ready.passed(turns)
        written.passed(turns + 1)
        step.passed(3 * turns)

    def ffn_down(self):
        nc, ps, x = self.nc, self.ps, self.x
        plan = Plan(1, 1)
        w = self.dram["l0_ffn_w_down"].rearrange("(f p) n -> p f n", p=P)
        act_t = self.flat[:, 0:FT * TOK].rearrange("p (h f c) -> p h f c", h=2, f=FT)
        kept = self.flat[:, 26 * TOK:28 * TOK].rearrange("p (s c) -> p s c", s=4)
        ahi, alo = self.hhi[:, 0, :].rearrange("p (s c) -> p s c", s=2), self.hlo[:, 0, :].rearrange("p (s c) -> p s c", s=2)
        used, free, dma = self.used, self.free, self.dma
        a_hi, a_split = self.ev["h_hi"], self.ev["act_split"]
        square = self.flat[:, 11 * TOK:15 * TOK].rearrange("p (o c) -> p o c", o=KT)
        total, squared, summed = self.arena[:, self.TOTAL_AT, :], self.ev["squared"], self.ev["summed"]
        PAIRS = FT // 2
        HALVES = (1, 0)

        def bank(o):
            return ps[o // 2][:, (o % 2) * HALF:(o % 2 + 1) * HALF]

        with nc.Block() as block:
            @block.sync
            def _(sp):
                def loads(turn, i):
                    for b in range(2):
                        self.load_weights(sp, plan, turn, b, [
                            (self.raw[:, b, :], w[:, bass.ds(i * 2 + b, 1), :].rearrange("p f n -> p (f n)"))])

                def residual(g, o):
                    if g or o >= 4:
                        prior = g * KT + o - 4
                        at = (prior % KT) // 2
                        sp.wait_ge(free[at].sem, free[at].at(prior // KT * 2 + prior % 2 + 2))
                    sp.dma_start(kept[:, o % 4, :], self.dram["x_kept"][:, HALVES[g], o, :]).then_inc(dma[o % 4].sem, 16)

                with sp.Fori(1, PAIRS) as i:
                    loads(i, i)
                for o in range(4):
                    residual(0, o)
                loads(PAIRS, 0)
                loads(PAIRS + 1, 1)
                for o in range(4, KT):
                    residual(0, o)
                with sp.Fori(2, PAIRS) as i:
                    loads(i + PAIRS, i)
                for o in range(KT):
                    residual(1, o)

            @block.scalar
            def _(act):
                def squares(g):
                    for o in range(KT):
                        act.wait_ge(free[o // 2].sem, free[o // 2].at(2 * g + o % 2 + 2))
                        if g:
                            act.wait_ge(summed.sem, summed.at(o + 1))
                        act.activation(square[:, o, :], x[:, HALVES[g], o, :], ACT.Square).then_inc(squared.sem, 1)

                def turns(lo, hi):
                    with act.Fori(lo, hi) as i:
                        for b in range(2):
                            self.weights_hi(act, plan, i, b)

                turns(1, PAIRS + 1)
                squares(0)
                turns(PAIRS + 1, 2 * PAIRS)
                squares(1)

            @block.gpsimd
            def _(pool):
                with pool.Fori(1, 2 * PAIRS) as i:
                    for b in range(2):
                        self.weights_lo(pool, plan, i, b)

            @block.tensor
            def _(pe):
                def pair(turn, first=False, last=False, again=False):
                    for b in range(2):
                        pe.wait_ge(self.split.sem, self.split.at(plan.n(turn, b) + 3))
                        pe.wait_ge(a_split.sem, a_split.at(plan.n(turn, b) + 1))
                        for o in range(KT):
                            if again and b == 0:
                                pe.wait_ge(free[o // 2].sem, free[o // 2].at(o % 2 + 2))
                            for wt, mov in ((self.whi, ahi), (self.whi, alo), (self.wlo, ahi)):
                                mm = pe.matmul(bank(o), wt[:, b, o * P:(o + 1) * P], mov[:, b, :],
                                               start=first and b == 0 and wt is self.whi and mov is ahi,
                                               stop=last and b == 1 and wt is self.wlo, skip_group_check=True)
                        mm.then_inc(used.sem, 1)

                for g in range(2):
                    pair(g * PAIRS, first=True, again=g == 1)
                    with pe.Fori(g * PAIRS + 1, (g + 1) * PAIRS - 1) as i:
                        pair(i)
                    pair((g + 1) * PAIRS - 1, last=True)

            @block.vector
            def _(dve):
                def split(turn, half, i):
                    for b in range(2):
                        n = plan.n(turn, b)
                        tile = act_t[:, half, bass.ds(i * 2 + b, 1), :].rearrange("p f c -> p (f c)")
                        dve.wait_ge(used.sem, used.at(n + 1))
                        dve.tensor_scalar(ahi[:, b, :], tile, 1.0, None, ALU.mult).then_inc(a_hi.sem, 1)
                        dve.wait_ge(a_hi.sem, a_hi.at(n + 1))
                        dve.tensor_tensor(alo[:, b, :], tile, ahi[:, b, :].bitcast(F32), ALU.subtract)\
                           .then_inc(a_split.sem, 1)

                def add(g, o):
                    out = total[:, HALVES[g] * HALF:(HALVES[g] + 1) * HALF]
                    dve.wait_ge(squared.sem, squared.at(g * KT + o + 1))
                    if o:
                        dve.wait_ge(summed.sem, summed.at(g * KT + o))
                        dve.tensor_tensor(out, out, square[:, o, :], ALU.add).then_inc(summed.sem, 1)
                    else:
                        dve.tensor_copy(out, square[:, o, :]).then_inc(summed.sem, 1)

                def sums(g):
                    dve.wait_ge(used.sem, used.at(plan.n((g + 1) * PAIRS, 0) + 2))
                    for o in range(KT):
                        dve.wait_ge(dma[o % 4].sem, dma[o % 4].at(16 * (2 * g + o // 4) + 16))
                        dve.tensor_tensor(x[:, HALVES[g], o, :], bank(o), kept[:, o % 4, :], ALU.add)\
                           .then_inc(free[o // 2].sem, 1)
                        if g and o >= 2:
                            add(g, o - 2)
                    for o in range(KT - 2 if g else 0, KT):
                        add(g, o)

                with dve.Fori(0, PAIRS) as i:
                    split(i, HALVES[0], i)
                split(PAIRS, HALVES[1], 0)
                sums(0)
                with dve.Fori(1, PAIRS) as i:
                    split(i + PAIRS, HALVES[1], i)
                sums(1)
        self.passed_blocks(plan, 2 * PAIRS)
        for n in range(4):
            free[n].passed(4)
            dma[n].passed(64)
        a_hi.passed(2 * FT)
        a_split.passed(2 * FT)
        squared.passed(2 * KT)
        summed.passed(2 * KT)

    Q_AT, K_AT, VT_AT, V_AT, P_AT, PT_AT = 8, 10, 12, 13, 14, 16

    def attention_buffers(self):
        A = self.arena
        self.Q = [A[:, self.Q_AT + a, :] for a in range(2)]
        self.K = [A[:, self.K_AT + a, :] for a in range(2)]
        self.VT = A[:, self.VT_AT, :]
        self.V = A[:, self.V_AT, :].rearrange("p (t v) -> p t v", t=NT)
        self.probs = [A[:, self.P_AT + n, :] for n in range(2)]
        at = self.PT_AT * TOK
        self.probs_t = [self.flat[:, at:at + 4 * HALF].rearrange("p (t c) -> p t c", t=4),
                        self.flat[:, at + 4 * HALF:at + 12 * HALF].rearrange("p (t c) -> p t c", t=8)]
        self.neg_max = self.small[:, 52:54]
        self.total = self.small[:, 54:56]
        self.inverse = self.small[:, 56:58]

    def attend_uses(self, gates):
        self.first_step = {0: 1, 1: 1} if gates else {0: 2, 1: 2}
        self.first_output = 2 if gates else 0
        turned = TURNED[-1] // 2 + 1
        return Uses(self, {0: self.first_step[0] + NT, 1: self.first_step[1] + NT, "t0": turned, "t1": turned,
                           3: self.first_output + GROUPS})

    @staticmethod
    def turned_use(n):
        return n // 2 + (1 if n >= TURNED[2] else 0)

    V_USE = TURNED[2] // 2

    def turn_v(self, pe, uses, i):
        vt_done = self.ev["vt_done"]
        for g in range(2):
            uses.clear(pe, f"t{g}", i, self.V_USE)
            for t in range(4):
                mm = pe.transpose(self.ps[2][:, g * HALF + t * P:g * HALF + (t + 1) * P],
                                  self.VT[:, (g * 4 + t) * P:(g * 4 + t + 1) * P], self.ident)
            mm.then_inc(vt_done.sem, 1)

    def take_v(self, act, i):
        vt_done = self.ev["vt_done"]
        for g in range(2):
            act.wait_ge(vt_done.sem, vt_done.at(i * 2 + (g + 1)))
            act.activation(self.V[:, g * 4:g * 4 + 4, :],
                           self.ps[2][:, g * HALF:(g + 1) * HALF].rearrange("p (t v) -> p t v", t=4),
                           ACT.Copy).then_inc(self.tfree[g].sem, 1)

    def score(self, pe, uses, i, j, kdim):
        ps, scores = self.ps, self.ev["scores_done"]
        a, qt = ORDER[j]
        uses.clear(pe, j % 2, i, self.first_step[j % 2] + j // 2)
        keys = (qt + 1) * P
        for lo in range(0, keys, HALF):
            hi = min(keys, lo + HALF)
            mm = pe.matmul(ps[j % 2][:, lo:hi], self.Q[a][0:kdim, qt * P:(qt + 1) * P],
                           self.K[a][0:kdim, lo:hi], start=True, stop=True)
        mm.then_inc(scores.sem, 1)

    def attend_pe(self, pe, uses, i, kdim, v_there):
        ps, t_done, pv_done, p_ready = self.ps, self.ev["t_done"], self.ev["pv_done"], self.ev["p_ready"]

        def turn(j):
            qt = ORDER[j][1]
            pe.wait_ge(p_ready.sem, p_ready.at(i * STEPS + (j + 1)))
            for c in range(qt // 4 + 1):
                n = TURNED[j] + c
                uses.clear(pe, f"t{n % 2}", i, self.turned_use(n))
                for t in range(c * 4, min(c * 4 + 4, qt + 1)):
                    mm = pe.transpose(ps[2][:, (n % 2) * HALF + (t % 4) * P:(n % 2) * HALF + (t % 4 + 1) * P],
                                      self.probs[j % 2][:, t * P:(t + 1) * P], self.ident)
                mm.then_inc(t_done.sem, 1)

        def outputs(m, part):
            a, last_qt = ORDER[4 * m + 3]
            g = last_qt // 4
            if part == 0:
                last = TURNED[4 * m + 4] - 1
                uses.over(pe, f"t{last % 2}", i, self.turned_use(last))
                uses.clear(pe, 3, i, self.first_output + m - 1)
            for t in range(part * (g + 1), (part + 1) * (g + 1)):
                lo = max(t * P - g * HALF, 0)
                bank = (m % 2) * HALF
                mm = pe.matmul(ps[3][a * 64:a * 64 + 64, bank + lo:bank + HALF],
                               self.V[:, t, a * 64:a * 64 + 64], self.probs_t[g][:, t, lo:HALF],
                               start=t == 0, stop=t == 4 * g + 3, skip_group_check=True)
            if part == 3:
                mm.then_inc(pv_done.sem, 1)

        for j in range(STEPS):
            turn(j)
            if j + 2 < STEPS:
                self.score(pe, uses, i, j + 2, kdim)
            if j == 1:
                v_there()
                self.turn_v(pe, uses, i)
            if j >= 4:
                outputs(j // 4 - 1, j % 4)
        for part in range(4):
            outputs(GROUPS - 1, part)

    def exponentials(self, act, i, j):
        max_ready = self.ev["max_ready"]
        act.wait_ge(max_ready.sem, max_ready.at(i * STEPS + (j + 1)))
        keys = (ORDER[j][1] + 1) * P
        act.activation(self.probs[j % 2][:, 0:keys], self.ps[j % 2][:, 0:keys], ACT.Exp,
                       bias=self.neg_max[:, j % 2:j % 2 + 1],
                       accum_out=self.total[:, j % 2:j % 2 + 1]).then_inc(self.free[j % 2].sem, 1)

    def take_turned(self, act, i, j):
        t_done, qt = self.ev["t_done"], ORDER[j][1]
        for c in range(qt // 4 + 1):
            n = TURNED[j] + c
            blocks = min(qt + 1 - 4 * c, 4)
            act.wait_ge(t_done.sem, t_done.at(i * TURNED[-1] + (n + 1)))
            act.activation(self.probs_t[qt // 4][:, 4 * c:4 * c + blocks, (qt % 4) * P:(qt % 4 + 1) * P],
                           self.ps[2][:, (n % 2) * HALF:(n % 2) * HALF + blocks * P]
                           .rearrange("p (t c) -> p t c", t=blocks), ACT.Copy).then_inc(self.tfree[n % 2].sem, 1)

    def attend_act(self, act, i, next_weights):
        for j in range(STEPS):
            if j and j + 1 < STEPS:
                self.exponentials(act, i, j + 1)
            self.take_turned(act, i, j)
            if j == 1:
                self.take_v(act, i)
            if j in (8, 10):
                next_weights((j - 8) // 2)

    def maximum(self, dve, i, j):
        scores, masked, max_ready = (self.ev[n] for n in ("scores_done", "exp_done", "max_ready"))
        qt, s = ORDER[j][1], self.ps[j % 2]
        dve.wait_ge(scores.sem, scores.at(i * STEPS + (j + 1)))
        dve.tensor_tensor(s[:, qt * P:(qt + 1) * P], s[:, qt * P:(qt + 1) * P],
                          self.consts[:, C_CAUSAL:C_CAUSAL + P], ALU.add).then_inc(masked.sem, 1)
        dve.wait_ge(masked.sem, masked.at(i * STEPS + (j + 1)))
        dve.tensor_reduce(self.neg_max[:, j % 2:j % 2 + 1], s[:, 0:(qt + 1) * P], AX.X, ALU.max,
                          negate=True).then_inc(max_ready.sem, 1)

    def normalise(self, dve, uses, i, j):
        inverted, p_ready = self.ev["sk_ready"], self.ev["p_ready"]
        r = self.inverse[:, j % 2:j % 2 + 1]
        uses.over(dve, j % 2, i, self.first_step[j % 2] + j // 2)
        dve.reciprocal(r, self.total[:, j % 2:j % 2 + 1]).then_inc(inverted.sem, 1)
        dve.wait_ge(inverted.sem, inverted.at(i * STEPS + (j + 1)))
        p = self.probs[j % 2][:, 0:(ORDER[j][1] + 1) * P]
        dve.tensor_scalar(p, p, r, None, ALU.mult).then_inc(p_ready.sem, 1)

    def attend_dve(self, dve, uses, i, gates):
        pv_done = self.ev["pv_done"]

        def outputs(m):
            a, last_qt = ORDER[4 * m + 3]
            g, bank = last_qt // 4, (m % 2) * HALF
            rows, cols = slice(a * 64, a * 64 + 64), slice(g * HALF, (g + 1) * HALF)
            dve.wait_ge(pv_done.sem, pv_done.at(i * GROUPS + (m + 1)))
            dve.tensor_tensor(self.arena[rows, bass.ds(i, 1), cols].rearrange("p f c -> p (f c)"),
                              self.ps[3][rows, bank:bank + HALF], gates(rows, cols), ALU.mult)\
               .then_inc(self.free[3].sem, 1)

        for j in range(1, STEPS):
            self.normalise(dve, uses, i, j)
            if j + 1 < STEPS:
                self.maximum(dve, i, j + 1)
            if j >= 8 and j % 4 == 0:
                outputs(j // 4 - 2)
        outputs(GROUPS - 2)
        outputs(GROUPS - 1)

    def attend_passed(self, turns):
        for name, n in (("vt_done", 2), ("scores_done", STEPS), ("max_ready", STEPS),
                        ("exp_done", STEPS), ("sk_ready", STEPS), ("p_ready", STEPS),
                        ("t_done", TURNED[-1]), ("pv_done", GROUPS)):
            self.ev[name].passed(turns * n)

    ROPE_AT, KPE_AT, TMP_AT, LATENT_AT = 24, 25, 26, 14

    def rotate(self, dve, tile, tmp, step, at):
        cos, sin = self.arena[64:96, self.ROPE_AT, :], self.arena[96:128, self.ROPE_AT, :]
        dve.tensor_tensor(tmp[64:96, :], tile[96:128, :], sin, ALU.mult).then_inc(step.sem, 1)
        dve.tensor_tensor(tile[64:96, :], tile[64:96, :], cos, ALU.mult).then_inc(step.sem, 1)
        dve.wait_ge(step.sem, at(2))
        return dve.tensor_tensor(tile[64:96, :], tile[64:96, :], tmp[64:96, :], ALU.add)

    def angle_tiles(self):
        rows = slice(64, 128)
        return [self.arena[rows, n, :] for n in (27, 26, 22, 23, 27)] + [self.small[:, 60:61]]

    def angles_dve(self, dve):
        ints, pos, ang, turns_, r, half_pi = self.angle_tiles()
        out, d = self.arena[:, self.ROPE_AT, :], self.angle_step
        count = [0]

        def done(ins):
            count[0] += 1
            ins.then_inc(d.sem, 1)
            dve.wait_ge(d.sem, d.at(count[0]))

        done(dve.memset(half_pi, float(np.pi / 2)))
        dve.wait_ge(self.dma[0].sem, self.dma[0].at(16))
        done(dve.tensor_copy(pos, ints.bitcast(I32)))
        done(dve.tensor_scalar(ang, pos, self.consts[64:128, C_FREQ:C_FREQ + 1], None, ALU.mult))
        done(dve.tensor_scalar(turns_, ang, float(1 / (2 * np.pi)), ROUND, ALU.mult, ALU.add))
        done(dve.tensor_scalar(turns_, turns_, -ROUND, None, ALU.add))
        for part in (TWO_PI_1, TWO_PI_2, TWO_PI_3):
            done(dve.scalar_tensor_tensor(r, turns_, -part, ang if part == TWO_PI_1 else r, ALU.mult, ALU.add))
        done(dve.tensor_scalar(r, r, PI_BELOW, -PI_BELOW, ALU.min, ALU.max))
        assert count[0] == 9

    def angles_act(self, act):
        r, half_pi = self.angle_tiles()[4:]
        out, a, d = self.arena[:, self.ROPE_AT, :], self.angle_act, self.angle_step
        act.wait_ge(d.sem, d.at(9))
        act.activation(out[64:96, :], r[0:32, :], ACT.Abs).then_inc(a.sem, 1)
        act.wait_ge(a.sem, a.at(1))
        act.activation(out[64:96, :], out[64:96, :], ACT.Sin, scale=-1.0, bias=half_pi[64:96, :]).then_inc(a.sem, 1)
        act.activation(out[96:128, :], r[32:64, :], ACT.Sin).then_inc(a.sem, 1)

    def even_projections(self):
        nc, ps, A = self.nc, self.ps, self.arena
        w = self.weights("e_w_in_2")
        low = Plan(1, 1, 1, 3)
        window = Plan(1, 1, after=(low, 1))
        gate = Plan(1, 1, after=(window, 3))
        TURNS_WINDOW, TURNS_GATE = 3, 4
        swap = E_KPE + MLA_ROPE // 2
        columns = [[(0, P, E_CQ)], [(0, P, E_CQ + P)], [(0, P, E_CKV)],
                   [(64, MLA_ROPE, E_KPE), (96, MLA_ROPE // 2, swap), (96 + MLA_ROPE // 2, MLA_ROPE // 2, E_KPE)]]
        latent = [A[:, self.LATENT_AT + n, :] for n in range(3)]
        squares = [A[:, 17 + n, :] for n in range(3)]
        diagonals = [A[:, 20 + n, :] for n in range(2)]
        sig = [A[:, 17 + n, :] for n in range(2)]
        groups = ((0, 1), (2,))
        kpe, tmp = A[:, self.KPE_AT, :], A[:, self.TMP_AT, :]
        r = self.small[:, 96:96 + 2 * NT]
        used, free, stored, gated = self.used, self.free, self.ev["stored"], self.ev["exp_done"]
        step, root, pe_step, squared, turned = (self.latent_step, self.latent_root, self.latent_pe, self.latent_squared,
                                                self.dve_step)

        def dense_loads(sp, plan, turns, column):
            with sp.Fori(0, turns) as i:
                for b in range(2):
                    self.load_weights(sp, plan, i, b, [
                        (self.slot(b, KT), w[:, :, bass.ds(i * (2 * P) + (column + b * P), P)])])

        def dense_turn(pe, plan, i):
            for b in range(2):
                pe.wait_ge(free[b].sem, free[b].at(i + (plan.first // 2 + 1)))
                self.project(pe, plan, i, b, ps[b], range(KT), range(KT))

        def tile(at, i, b):
            return A[:, bass.ds(i * 2 + (at + b), 1), :].rearrange("p f c -> p (f c)")

        with nc.Block() as block:
            @block.sync
            def _(sp):
                for b in range(4):
                    if b == 2:
                        self.keep_x(sp)
                    self.load_weights(sp, low, 0, b, [(self.slot(b, KT)[:, :, at:at + n], w[:, :, c:c + n])
                                                      for at, n, c in columns[b]])
                    if b == 0:
                        sp.dma_start(self.angle_tiles()[0].bitcast(I32), self.dram["positions"].partition_broadcast(64))\
                          .then_inc(self.dma[0].sem, 16)
                dense_loads(sp, window, TURNS_WINDOW, E_QS)
                dense_loads(sp, gate, TURNS_GATE, E_GATE)

            @block.gpsimd
            def _(pool):
                self.weights_lo(pool, low, 0, 0)
                self.weights_lo(pool, low, 0, 1)
                self.norm_pool(pool)
                self.weights_lo(pool, low, 0, 2)
                self.weights_lo(pool, low, 0, 3)
                for plan, turns in ((window, TURNS_WINDOW), (gate, TURNS_GATE)):
                    with pool.Fori(0, turns) as i:
                        for b in range(2):
                            self.weights_lo(pool, plan, i, b)

            @block.tensor
            def _(pe):
                self.norm_pe(pe, summed_before=False)
                for b in range(4):
                    pe.wait_ge(free[b % 2].sem, free[b % 2].at(b // 2 + 1))
                    self.project(pe, low, 0, b, ps[b % 2], range(KT), range(KT), new_h=b == 0, kept=b == 0)
                dense_turn(pe, window, 0)
                pe.wait_ge(squared.sem, squared.at(3))
                for g, tiles in enumerate(groups):
                    for t in range(NT):
                        for n in tiles:
                            mm = pe.matmul(ps[2][:, g * NT + t:g * NT + t + 1], squares[n][:, t * P:(t + 1) * P],
                                           self.ones[:, 0:1], start=n == tiles[0], stop=n == tiles[-1])
                mm.then_inc(pe_step.sem, 1)
                with pe.Fori(1, TURNS_WINDOW) as i:
                    dense_turn(pe, window, i)
                for g in range(2):
                    pe.wait_ge(step.sem, step.at(3 + 2 * g))
                    for c in range(2):
                        mm = pe.matmul(ps[2 + g][:, c * HALF:(c + 1) * HALF], self.ones,
                                       diagonals[g][:, c * HALF:(c + 1) * HALF], start=True, stop=True)
                    mm.then_inc(pe_step.sem, 1)
                with pe.Fori(0, TURNS_GATE) as i:
                    dense_turn(pe, gate, i)

            @block.scalar
            def _(act):
                self.weights_hi(act, low, 0, 0)
                self.weights_hi(act, low, 0, 1)
                self.norm_act(act, summed_before=False)
                for b in range(4):
                    if b < 2:
                        self.weights_hi(act, low, 0, b + 2)
                    else:
                        self.weights_hi(act, window, 0, b - 2)
                    act.wait_ge(used.sem, used.at(b + 3))
                    act.activation((latent + [kpe])[b], ps[b % 2][:, :], ACT.Copy).then_inc(free[b % 2].sem, 1)
                for n in range(3):
                    act.wait_ge(free[n % 2].sem, free[n % 2].at(n // 2 + 2))
                    act.activation(squares[n], latent[n], ACT.Square).then_inc(squared.sem, 1)
                with act.Fori(1, TURNS_WINDOW) as i:
                    for b in range(2):
                        self.weights_hi(act, window, i, b)
                act.wait_ge(step.sem, step.at(2))
                act.activation(r, r, ACT.Sqrt).then_inc(root.sem, 1)
                self.weights_hi(act, gate, 0, 0)
                self.angles_act(act)
                self.weights_hi(act, gate, 0, 1)

                def turn(i, last=False):
                    for b in range(2):
                        if not last:
                            self.weights_hi(act, gate, i + 1, b)
                        act.wait_ge(used.sem, used.at(gate.n(i, b) + 3))
                        act.activation(sig[b], ps[b][:, :], ACT.Sigmoid).then_inc(gated.sem, 1)

                with act.Fori(0, TURNS_GATE - 1) as i:
                    turn(i)
                turn(TURNS_GATE - 1, last=True)

            @block.vector
            def _(dve):
                self.norm_dve(dve, "e_g_in_2", summed_before=False)
                dve.wait_ge(stored.sem, stored.at(16))
                self.angles_dve(dve)

                def window_turn(i):
                    for b in range(2):
                        dve.wait_ge(used.sem, used.at(window.n(i, b) + 3))
                        dve.tensor_scalar(tile(8, i, b), ps[b][:, :], 1.0, None, ALU.mult).then_inc(free[b].sem, 1)

                window_turn(0)
                dve.wait_ge(pe_step.sem, pe_step.at(1))
                for g, tiles in enumerate(groups):
                    ins = dve.tensor_scalar(r[:, g * NT:(g + 1) * NT], ps[2][:, g * NT:(g + 1) * NT], 1.0 / (P * len(tiles)),
                                            EPS, ALU.mult, ALU.add)
                ins.then_inc(step.sem, 1)
                dve.wait_ge(step.sem, step.at(1))
                dve.reciprocal(r, r).then_inc(step.sem, 1)
                with dve.Fori(1, TURNS_WINDOW) as i:
                    window_turn(i)
                dve.wait_ge(root.sem, root.at(1))
                for g in range(2):
                    dve.tensor_tensor(diagonals[g].rearrange("p (t c) -> p t c", t=NT),
                                      self.ident.unsqueeze(1).broadcast_to((P, NT, P)),
                                      r[:, g * NT:(g + 1) * NT].unsqueeze(2).broadcast_to((P, NT, P)), ALU.mult)\
                       .then_inc(step.sem, 2)
                for g, tiles in enumerate(groups):
                    dve.wait_ge(pe_step.sem, pe_step.at(g + 2))
                    for n in tiles:
                        gain = self.col("e_g_q_a_2", n) if g == 0 else self.col("e_g_kv_a_2")
                        dve.scalar_tensor_tensor(latent[n], latent[n], gain, ps[2 + g][:, :], ALU.mult, ALU.mult)
                dve.wait_ge(self.angle_act.sem, self.angle_act.at(3))
                sin = A[96:128, self.ROPE_AT, :]
                dve.tensor_scalar(sin, sin, self.consts[96:128, C_SIGN:C_SIGN + 1], None, ALU.mult)\
                   .then_inc(self.angle_step.sem, 1)
                dve.wait_ge(self.angle_step.sem, self.angle_step.at(10))
                self.rotate(dve, kpe, tmp, turned, turned.at)
                with dve.Fori(0, TURNS_GATE) as i:
                    for b in range(2):
                        dve.wait_ge(gated.sem, gated.at(i * 2 + (b + 1)))
                        dve.tensor_tensor(tile(0, i, b), ps[b][:, :], sig[b], ALU.mult).then_inc(free[b].sem, 1)
        self.norm_passed(summed_before=False)
        self.passed_blocks(gate, TURNS_GATE)
        for b in range(2):
            free[b].passed(2 + TURNS_WINDOW + TURNS_GATE)
        self.dma[0].passed(16)
        for t, n in ((gated, 2 * TURNS_GATE), (step, 6), (root, 1), (pe_step, 3), (squared, 3), (turned, 2),
                     (self.angle_step, 10), (self.angle_act, 3)):
            t.passed(n)

    def window_operands(self):
        nc, ps, A = self.nc, self.ps, self.arena
        keys, v_tok = self.swa_buffers()
        pe_step, keys_done = self.pe_step, self.act_step
        with nc.Block() as block:
            @block.scalar
            def _(act):
                for g in range(SWA_KV):
                    act.activation(keys[g][:, P:P + TOK], A[g * 64:g * 64 + 64, 12, :], ACT.Copy).then_inc(keys_done.sem, 1)
                act.wait_ge(keys_done.sem, keys_done.at(2))
                act.wait_ge(pe_step.sem, pe_step.at(1))
                act.activation(v_tok[:, 1:1 + NT, :], ps[0][:, :].rearrange("p (t v) -> p t v", t=NT), ACT.Copy)

            @block.gpsimd
            def _(pool):
                for g in range(SWA_KV):
                    pool.memset(keys[g][:, 0:P], 0.0)
                pool.wait_ge(keys_done.sem, keys_done.at(2))
                pool.memset(v_tok[:, 0, :], 0.0)

            @block.tensor
            def _(pe):
                for t in range(NT):
                    mm = pe.transpose(ps[0][:, t * P:(t + 1) * P], A[:, 13, t * P:(t + 1) * P], self.ident)
                mm.then_inc(pe_step.sem, 1)
        pe_step.passed(1)
        keys_done.passed(2)

    def swa_buffers(self):
        at = 21 * TOK
        keys = [self.flat[0:64, at + g * (P + TOK):at + (g + 1) * (P + TOK)] for g in range(SWA_KV)]
        at = 12 * TOK
        return keys, self.flat[:, at:at + (NT + 1) * P].rearrange("p (t v) -> p t v", t=NT + 1)

    def sliding_window(self):
        nc, ps, A, ev = self.nc, self.ps, self.arena, self.ev
        keys, v_tok = self.swa_buffers()
        H, G = SWA_HEADS, SWA_HEADS // SWA_KV
        q_tiles = A[:, 8:12, :]
        q = [self.flat[0:64, at * TOK:at * TOK + H * P].rearrange("p (f a c) -> p f a c", f=H // 2, a=2) for at in (24, 25)]
        v = [self.flat[:, 24 * TOK - (n + 1) * 2 * P:24 * TOK - n * 2 * P].rearrange("p (t c) -> p t c", t=2)
             for n in range(2)]
        s = [self.flat[:, at * TOK:(at + 2) * TOK].rearrange("p (h k) -> p h k", h=H) for at in (17, 19)]
        p_t = self.flat[:, 26 * TOK:28 * TOK].rearrange("p (t h q) -> p t h q", t=2, h=H)
        sinks = self.col("sinks", 0, H)
        neg_sinks = self.small[:, 64:64 + H]
        neg_max, total, sink = ([self.small[:, 72 + (2 * n + u) * H:72 + (2 * n + u + 1) * H] for u in range(2)]
                                for n in range(3))
        free, step, small = self.free, self.dve_step, ev["q_ready"]
        q_staged, v_staged, scores, max_ready = (ev[n] for n in ("k_ready", "vt_done", "scores_done", "max_ready"))
        exp_done, p_ready, t_done, pv_done = (ev[n] for n in ("exp_done", "p_ready", "t_done", "pv_done"))
        STEPS = 4

        def score(pe, i, u):
            pe.wait_ge(q_staged.sem, q_staged.at(i * 2 + 2))
            for h in range(H):
                if h % G == 0:
                    pe.wait_ge(free[h // G].sem, free[h // G].at(i + 1))
                mm = pe.matmul(ps[h // G][:, h % G * 2 * P:(h % G + 1) * 2 * P], q[u][:, h // 2, h % 2, :],
                               keys[h // G][:, bass.ds(i * P, 2 * P)], start=True, stop=True)
                if h % G == G - 1:
                    mm.then_inc(scores.sem, 1)

        def turn(pe, i, u):
            pe.wait_ge(p_ready.sem, p_ready.at(i + 1))
            for t in range(2):
                pe.wait_ge(free[2 + t].sem, free[2 + t].at(i * (2 - t) + 1))
                for h in range(H):
                    mm = pe.transpose(ps[2 + t][:, h * P:(h + 1) * P], s[u][:, h, t * P:(t + 1) * P], self.ident)
                mm.then_inc(t_done.sem, 1)

        def outputs(pe, i, u):
            pe.wait_ge(v_staged.sem, v_staged.at(i + 1))
            for t in range(2):
                pe.wait_ge(free[2 + t].sem, free[2 + t].at(i * (2 - t) + 2))
            for h in range(H):
                g = h // G
                for t in range(2):
                    mm = pe.matmul(ps[2][h % 2 * 64:h % 2 * 64 + 64, h // 2 * P:(h // 2 + 1) * P],
                                   v[u][:, t, g * 64:g * 64 + 64], p_t[:, t, h, :], start=t == 0, stop=t == 1,
                                   skip_group_check=True)
            mm.then_inc(pv_done.sem, 1)

        def stage_q(dve, i, u):
            for a in range(2):
                dve.tensor_scalar(q[u][:, :, a, :], q_tiles[a * 64:a * 64 + 64, :, bass.ds(i * P, P)], SWA_D ** -0.5, None,
                                  ALU.mult).then_inc(q_staged.sem, 1)

        def stage_v(dve, i, u):
            dve.tensor_scalar(v[u], v_tok[:, bass.ds(i, 2), :], 1.0, None, ALU.mult).then_inc(v_staged.sem, 1)

        def maximum(dve, i, u, first=False):
            table = C_SWA + (0 if first else 2 * P)
            for g in range(SWA_KV):
                heads = slice(g * G, (g + 1) * G)
                dve.wait_ge(scores.sem, scores.at(i * 2 + (g + 1)))
                for h in range(g * G, (g + 1) * G):
                    ins = dve.scalar_tensor_tensor(s[u][:, h, :], self.consts[:, table:table + 2 * P],
                                                   self.consts[:, C_SLOPE + h:C_SLOPE + h + 1],
                                                   ps[g][:, h % G * 2 * P:(h % G + 1) * 2 * P], ALU.mult, ALU.add)
                ins.then_inc(free[g].sem, 1)
                dve.wait_ge(free[g].sem, free[g].at(i + 2))
                dve.tensor_reduce(neg_max[u][:, heads], s[u][:, heads, :], AX.X, ALU.max, negate=True).then_inc(step.sem, 1)
                dve.wait_ge(step.sem, step.at(i * STEPS + (2 * g + 1)))
                dve.tensor_tensor(neg_max[u][:, heads], neg_max[u][:, heads], neg_sinks[:, heads], ALU.min)\
                   .then_inc(step.sem, 1)
                dve.wait_ge(step.sem, step.at(i * STEPS + (2 * g + 2)))
                dve.tensor_tensor(sink[u][:, heads], sinks[:, heads], neg_max[u][:, heads], ALU.add)\
                   .then_inc(max_ready.sem, 1)

        def normalise(dve, i, u):
            dve.wait_ge(exp_done.sem, exp_done.at(i + 1))
            dve.tensor_tensor(total[u], total[u], sink[u], ALU.add).then_inc(small.sem, 1)
            dve.wait_ge(small.sem, small.at(i * 2 + 1))
            dve.reciprocal(total[u], total[u]).then_inc(small.sem, 1)
            dve.wait_ge(small.sem, small.at(i * 2 + 2))
            dve.tensor_tensor(s[u], s[u], total[u].unsqueeze(2).broadcast_to((P, H, 2 * P)), ALU.mult)\
               .then_inc(p_ready.sem, 1)

        def gate_outputs(dve, i):
            dve.wait_ge(pv_done.sem, pv_done.at(i + 1))
            out = A[:, 4:8, bass.ds(i * P, P)]
            dve.tensor_tensor(out, ps[2][:, 0:4 * P].rearrange("p (f c) -> p f c", f=4), out, ALU.mult)\
               .then_inc(free[2].sem, 1)

        def exponentials(act, i, u):
            for h in range(H):
                if h % G == 0:
                    act.wait_ge(max_ready.sem, max_ready.at(i * 2 + (h // G + 1)))
                act.activation(s[u][:, h, :], s[u][:, h, :], ACT.Exp, bias=neg_max[u][:, h:h + 1],
                               accum_out=total[u][:, h:h + 1])
            act.activation(sink[u], sink[u], ACT.Exp).then_inc(exp_done.sem, 1)

        def take_transposed(act, i):
            for t in range(2):
                act.wait_ge(t_done.sem, t_done.at(i * 2 + (t + 1)))
                act.activation(p_t[:, t, :, :], ps[2 + t][:, :].rearrange("p (h q) -> p h q", h=H), ACT.Copy)\
                   .then_inc(free[2 + t].sem, 1)

        def tensor_turn(pe, i, u, ahead=True):
            turn(pe, i, u)
            if ahead:
                score(pe, i + 2, u)
            outputs(pe, i, u)

        def vector_turn(dve, i, u, first=False, ahead=True, last=False):
            normalise(dve, i, u)
            if ahead:
                stage_q(dve, i + 2, u)
            if not first:
                if not last:
                    maximum(dve, i + 1, 1 - u)
                gate_outputs(dve, i - 1)
                if not last:
                    stage_v(dve, i + 1, 1 - u)

        def scalar_turn(act, i, u, last=False):
            if not last:
                exponentials(act, i + 1, 1 - u)
            take_transposed(act, i)

        PAIRED = (NT - 4) // 2
        with nc.Block() as block:
            @block.tensor
            def _(pe):
                score(pe, 0, 0)
                score(pe, 1, 1)
                tensor_turn(pe, 0, 0)
                with pe.Fori(0, PAIRED) as n:
                    tensor_turn(pe, n * 2 + 1, 1)
                    tensor_turn(pe, n * 2 + 2, 0)
                tensor_turn(pe, NT - 3, 1)
                tensor_turn(pe, NT - 2, 0, ahead=False)
                tensor_turn(pe, NT - 1, 1, ahead=False)

            @block.vector
            def _(dve):
                dve.tensor_scalar(neg_sinks, sinks, -1.0, None, ALU.mult)
                for u in range(2):
                    stage_q(dve, u, u)
                    stage_v(dve, u, u)
                maximum(dve, 0, 0, first=True)
                maximum(dve, 1, 1)
                vector_turn(dve, 0, 0, first=True)
                with dve.Fori(0, PAIRED) as n:
                    vector_turn(dve, n * 2 + 1, 1)
                    vector_turn(dve, n * 2 + 2, 0)
                vector_turn(dve, NT - 3, 1)
                vector_turn(dve, NT - 2, 0, ahead=False)
                vector_turn(dve, NT - 1, 1, ahead=False, last=True)
                gate_outputs(dve, NT - 1)

            @block.scalar
            def _(act):
                exponentials(act, 0, 0)
                with act.Fori(0, NT // 2 - 1) as n:
                    scalar_turn(act, n * 2, 0)
                    scalar_turn(act, n * 2 + 1, 1)
                scalar_turn(act, NT - 2, 0)
                scalar_turn(act, NT - 1, 1, last=True)
        for t, n in ((q_staged, 2), (v_staged, 1), (scores, 2), (max_ready, 2), (exp_done, 1), (p_ready, 1),
                     (t_done, 2), (pv_done, 1), (step, STEPS), (small, 2), (free[0], 1), (free[1], 1), (free[2], 2),
                     (free[3], 1)):
            t.passed(n * NT)

    def mla_heads(self):
        nc, ps, ev, A = self.nc, self.ps, self.ev, self.arena
        self.attention_buffers()
        Q, K, VT = self.Q, self.K, self.VT
        wq, wkv = self.weights("e_w_q_up_2"), self.weights("e_w_kv_up_2")
        plan, turns = Plan(3, 1, 3, 1), MLA_HEADS // 2
        ahead = Plan(1, 1, after=(plan, turns))
        uses = self.attend_uses(gates=False)
        used, free = self.used, self.free
        kpe, tmp = A[:, self.KPE_AT, :], A[:, self.TMP_AT, :]
        l_hi, l_split = ev["h_hi"], ev["h_split_vector"]
        rotated, kpe_there, step = ev["q_ready"], ev["k_ready"], ev["rows_ready"]
        swap = MLA_ROPE // 2
        KV = MLA_NOPE + MLA_V
        with nc.Block() as block:
            @block.sync
            def _(sp):
                with sp.Fori(0, turns) as i:
                    for a in range(2):
                        at = i * (2 * MLA_DK) + a * MLA_DK
                        slot = self.slot(2 * a, 2)
                        self.load_weights(sp, plan, i, 2 * a, [
                            (slot[:, :, 0:MLA_DK], wq[:, :, bass.ds(at, MLA_DK)]),
                            (slot[:, :, MLA_DK:MLA_DK + swap], wq[:, :, bass.ds(at + (MLA_NOPE + swap), swap)]),
                            (slot[:, :, MLA_DK + swap:P], wq[:, :, bass.ds(at + MLA_NOPE, swap)])])
                        self.load_weights(sp, plan, i, 2 * a + 1, [
                            (self.slot(1, 1), wkv[:, :, bass.ds(i * (2 * KV) + a * KV, KV)])])
                self.load_ahead(sp, ahead, self.first_blocks("e_w_out_2"))

            @block.gpsimd
            def _(pool):
                with pool.Fori(0, turns) as i:
                    for b in range(4):
                        self.weights_lo(pool, plan, i, b, P if b % 2 else 2 * P)
                for b in range(2):
                    self.weights_lo(pool, ahead, 0, b)

            @block.tensor
            def _(pe):
                pe.wait_ge(l_split.sem, l_split.at(3))
                with pe.Fori(0, turns) as i:
                    for b in range(4):
                        uses.clear(pe, b % 2, i, b // 2)
                        self.project(pe, plan, i, b, ps[b % 2], (0,) if b % 2 else (0, 1), (2,) if b % 2 else (0, 1))
                    pe.wait_ge(kpe_there.sem, kpe_there.at(2))
                    pe.wait_ge(rotated.sem, rotated.at(i * 2 + 1))
                    for j in range(2):
                        self.score(pe, uses, i, j, MLA_DK)
                    self.attend_pe(pe, uses, i, MLA_DK, v_there=lambda: uses.over(pe, 1, i, 1))

            @block.scalar
            def _(act):
                def turn(i, last=False):
                    for b in range(4):
                        a = b // 2
                        act.wait_ge(used.sem, used.at(plan.n(i, b) + 3))
                        if b % 2 == 0:
                            act.activation(Q[a], ps[0][:, :], ACT.Copy, scale=MLA_DK ** -0.5).then_inc(free[0].sem, 1)
                        else:
                            act.activation(K[a][0:64, :], ps[1][0:64, :], ACT.Copy)
                            act.activation(VT[a * 64:a * 64 + 64, :], ps[1][64:128, :], ACT.Copy)\
                               .then_inc(free[1].sem, 1)
                        if b < 2:
                            self.weights_hi(act, plan, i, b + 2, P if b % 2 else 2 * P)
                    self.exponentials(act, i, 0)
                    self.exponentials(act, i, 1)
                    self.attend_act(act, i, (lambda b: self.weights_hi(act, ahead, 0, b)) if last else
                                    lambda b: self.weights_hi(act, plan, i + 1, b, P if b else 2 * P))

                for n in range(3):
                    act.activation(self.hhi[:, n, :], A[:, self.LATENT_AT + n, :], ACT.Copy).then_inc(l_hi.sem, 1)
                for a in range(2):
                    act.activation(K[a][64:96, :], kpe[64:96, :], ACT.Copy).then_inc(kpe_there.sem, 1)
                self.weights_hi(act, plan, 0, 0, 2 * P)
                self.weights_hi(act, plan, 0, 1, P)
                with act.Fori(0, turns - 1) as i:
                    turn(i)
                turn(turns - 1, last=True)

            @block.vector
            def _(dve):
                O = A[:, 0:8, :]
                for n in range(3):
                    dve.wait_ge(l_hi.sem, l_hi.at(n + 1))
                    dve.tensor_tensor(self.hlo[:, n, :], A[:, self.LATENT_AT + n, :], self.hhi[:, n, :].bitcast(F32),
                                      ALU.subtract).then_inc(l_split.sem, 1)
                with dve.Fori(0, turns) as i:
                    for a in range(2):
                        uses.over(dve, 0, i, a)
                        self.rotate(dve, Q[a], tmp, step, lambda n: step.at(i * 4 + (a * 2 + n)))\
                            .then_inc(rotated.sem, 1)
                        dve.wait_ge(rotated.sem, rotated.at(i * 2 + (a + 1)))
                    self.maximum(dve, i, 0)
                    self.maximum(dve, i, 1)
                    self.normalise(dve, uses, i, 0)
                    self.attend_dve(dve, uses, i, lambda rows, cols: O[rows, bass.ds(i, 1), cols]
                                    .rearrange("p f c -> p (f c)"))
        self.passed_blocks(plan, turns)
        uses.passed(turns)
        self.attend_passed(turns)
        kpe_there.passed(2)
        l_hi.passed(3)
        l_split.passed(3)
        rotated.passed(2 * turns)
        step.passed(4 * turns)

    def fox_row_tiles(self):
        return [self.arena[0:FOX_HEADS, k, :] for k in (24, 25, 26, 27, 16, 17)]

    def fox_rows_act(self, act):
        z, tmp, lf = self.fox_row_tiles()[0:3]
        self.log_forget(act, None, z, tmp, lf, FOX_HEADS)

    def fox_rows_dve(self, dve):
        z, tmp, lf, one, lc, nlc = self.fox_row_tiles()
        d = self.row_step
        dve.memset(one, 1.0).then_inc(d.sem, 1)
        self.log_forget(None, dve, z, tmp, lf, FOX_HEADS)
        dve.wait_ge(d.sem, d.at(2))
        dve.tensor_tensor_scan(lc, one, lf, 0.0, ALU.mult, ALU.add).then_inc(d.sem, 1)
        dve.wait_ge(d.sem, d.at(3))
        dve.tensor_scalar(nlc, lc, -1.0, None, ALU.mult).then_inc(d.sem, 1)

    def fox_rows_sp(self, sp):
        d, stored = self.row_step, self.ev["stored"]
        for side in range(2):
            sp.wait_ge(d.sem, d.at(3 + side))
            sp.dma_start(self.dram["log_cum"][side], self.fox_row_tiles()[4 + side]).then_inc(stored.sem, 16)
        sp.wait_ge(stored.sem, stored.at(32))

    def fox_heads(self):
        nc, ps, ev = self.nc, self.ps, self.ev
        self.attention_buffers()
        Q, K, VT = self.Q, self.K, self.VT
        w = self.weights("o_w_in_2")
        plan, turns = Plan(1, 1, 1, 1), FOX_HEADS // 2
        ahead = Plan(1, 1, after=(plan, turns))
        kdim = FOX_D + 2
        gate, sig = self.arena[:, 22, :], self.arena[:, 23, :]
        starts = (3 * D + FOX_HEADS, 0, D, 2 * D)
        uses = self.attend_uses(gates=True)
        used, free, dma = self.used, self.free, self.dma
        ones_set, gated, first_k, scores = self.pool_step, ev["h_hi"], ev["k_ready"], ev["scores_done"]
        with nc.Block() as block:
            @block.sync
            def _(sp):
                sp.wait_ge(ones_set.sem, ones_set.at(4))
                def turn(i, first=False):
                    for b in range(4):
                        at = i * P + starts[b] if starts[b] else (i * 2) * (P // 2)
                        if b >= 2 or not first:
                            self.load_weights(sp, plan, i, b, [(self.slot(b, KT), w[:, :, bass.ds(at, P)])])
                        if b == 1 and first:
                            self.fox_rows_sp(sp)
                        if b == 1:
                            sp.wait_ge(scores.sem, scores.at(i * STEPS))
                            for a in range(2):
                                for side, tile, row in ((0, Q[a], 65), (1, K[a], 64)):
                                    sp.dma_start(tile[row:row + 1, :],
                                                 self.dram["log_cum"][side][bass.ds(i * 2 + a, 1), :])\
                                      .then_inc(dma[a].sem, 16)

                turn(0, first=True)
                with sp.Fori(1, turns) as i:
                    turn(i)
                self.load_ahead(sp, ahead, self.first_blocks("o_w_out_2"))

            @block.gpsimd
            def _(pool):
                for tile in (*Q, *K):
                    pool.memset(tile[64:66, :], 1.0).then_inc(ones_set.sem, 1)
                for b in range(2, 4):
                    self.weights_lo(pool, plan, 0, b)
                with pool.Fori(1, turns) as i:
                    for b in range(4):
                        self.weights_lo(pool, plan, i, b)
                for b in range(2):
                    self.weights_lo(pool, ahead, 0, b)

            @block.tensor
            def _(pe):
                with pe.Fori(0, turns) as i:
                    for b, pair in enumerate((3, 0, 1)):
                        uses.clear(pe, pair, i, 0)
                        self.project(pe, plan, i, b, ps[pair], range(KT), range(KT))
                    for a in range(2):
                        pe.wait_ge(dma[a].sem, dma[a].at(i * 32 + 32))
                    uses.over(pe, 0, i, 0)
                    pe.wait_ge(first_k.sem, first_k.at(i + 1))
                    self.score(pe, uses, i, 0, kdim)
                    self.score(pe, uses, i, 1, kdim)
                    uses.clear(pe, 3, i, 1)
                    self.project(pe, plan, i, 3, ps[3], range(KT), range(KT))
                    self.attend_pe(pe, uses, i, kdim, v_there=lambda: uses.over(pe, 3, i, 1))

            @block.scalar
            def _(act):
                def turn(i, last=False):
                    for b in range(3):
                        act.wait_ge(used.sem, used.at(plan.n(i, b) + 3))
                        if b == 0:
                            act.activation(sig, ps[3][:, :], ACT.Sigmoid).then_inc(gated.sem, 1)
                        elif b == 1:
                            act.activation(Q[0][0:64, :], ps[0][0:64, :], ACT.Copy, scale=FOX_D ** -0.5)
                            act.activation(Q[1][0:64, :], ps[0][64:128, :], ACT.Copy, scale=FOX_D ** -0.5)\
                               .then_inc(free[0].sem, 1)
                        else:
                            act.activation(K[0][0:64, :], ps[1][0:64, :], ACT.Copy).then_inc(first_k.sem, 1)
                            act.activation(K[1][0:64, :], ps[1][64:128, :], ACT.Copy).then_inc(free[1].sem, 1)
                        if b < 2:
                            self.weights_hi(act, plan, i, b + 2)
                    self.exponentials(act, i, 0)
                    self.exponentials(act, i, 1)
                    act.wait_ge(used.sem, used.at(plan.n(i, 3) + 3))
                    act.activation(VT, ps[3][:, :], ACT.Copy).then_inc(free[3].sem, 1)
                    self.attend_act(act, i, (lambda b: self.weights_hi(act, ahead, 0, b)) if last else
                                    lambda b: self.weights_hi(act, plan, i + 1, b))

                self.fox_rows_act(act)
                with act.Fori(0, turns - 1) as i:
                    turn(i)
                turn(turns - 1, last=True)

            @block.vector
            def _(dve):
                self.fox_rows_dve(dve)
                with dve.Fori(0, turns) as i:
                    dve.wait_ge(gated.sem, gated.at(i + 1))
                    uses.clear(dve, 3, i, 0)
                    dve.tensor_tensor(gate, ps[3][:, :], sig, ALU.mult).then_inc(free[3].sem, 1)
                    uses.over(dve, 3, i, 0)
                    self.maximum(dve, i, 0)
                    self.maximum(dve, i, 1)
                    self.normalise(dve, uses, i, 0)
                    self.attend_dve(dve, uses, i, lambda rows, cols: gate[rows, cols])
        self.passed_blocks(plan, turns)
        uses.passed(turns)
        self.attend_passed(turns)
        ones_set.passed(4)
        self.row_step.passed(4)
        self.act_step.passed(3)
        ev["stored"].passed(32)
        gated.passed(turns)
        first_k.passed(turns)
        for a in range(2):
            dma[a].passed(32 * turns)


def program(nc, dram):
    with ExitStack() as ctx:
        k = Kernel(nc, dram, ctx)
        k.start()
        k.load_x()

        i_gate, f_gate = 2 * M_QK + 2 * M_V, 2 * M_QK + 2 * M_V + M_HEADS
        k.gates("l0_norm_mix", "l0_mlstm_w_in", ((0, i_gate, M_HEADS), (32, f_gate, M_HEADS)), "gates", 10,
                next_blocks=(0, M_QK), columns=True)
        k.mlstm_heads()
        k.mlstm_norm()
        k.out_projection("l0_mlstm_w_out")

        k.ffn_up("l0_norm_ffn")
        k.ffn_down()
        k.norm("final_norm")

        k.even_projections()
        k.window_operands()
        k.sliding_window()
        k.mla_heads()
        k.out_projection("e_w_out_2")

        k.gates("o_g_in_2", "o_w_in_2", ((0, 3 * D, FOX_HEADS),), "o_b_f", 24,
                next_blocks=(3 * D + FOX_HEADS, 0))
        k.fox_heads()
        k.out_projection("o_w_out_2")

        k.store()


WEIGHTS = ["l0_mlstm_w_in", "l0_mlstm_w_out", "l0_ffn_w_up", "l0_ffn_w_down",
           "e_w_in_2", "e_w_q_up_2", "e_w_kv_up_2", "e_w_out_2", "o_w_in_2", "o_w_out_2"]


def column_layout(inputs):
    cols = np.zeros((P, N_COLS), np.float32)
    for name, (at, n) in COLS.items():
        if name in inputs and name != "o_b_f":
            cols[:, at:at + n] = np.asarray(inputs[name]).reshape(n, P).T
    gates = np.asarray(inputs["l0_mlstm_b_gates"])
    cols[0:M_HEADS, COLS["gates"][0]] = gates[:M_HEADS]
    cols[32:32 + M_HEADS, COLS["gates"][0]] = gates[M_HEADS:]
    cols[0:FOX_HEADS, COLS["o_b_f"][0]] = np.asarray(inputs["o_b_f_2"])[0]
    cols[:, COLS["sinks"][0]:COLS["sinks"][0] + SWA_HEADS] = np.asarray(inputs["e_sinks_2"])
    taps = np.concatenate([np.asarray(inputs["l0_ffn_conv_w"]), np.asarray(inputs["l0_ffn_conv_b"])[None]])
    conv = taps.reshape(4, 2, FT, P).transpose(3, 2, 1, 0).reshape(P, FT, 8)
    return cols, np.ascontiguousarray(conv)


def kernel(**inputs):
    import concourse.bacc as bacc
    from concourse.bass_utils import run_bass_kernel_spmd

    nc = bacc.Bacc("TRN2", target_bir_lowering=False, num_devices=1)
    cols, conv = column_layout(inputs)
    arrays = {"consts": shape_constants(), "cols": cols, "conv": conv,
              "x": np.asarray(inputs["x"]).reshape(TOK, D),
              "g_final": np.asarray(inputs["g_final_2"]).reshape(1, D),
              "positions": np.asarray(inputs["positions_2"]).reshape(1, TOK)}
    for name in WEIGHTS:
        w = np.asarray(inputs[name])
        arrays[name] = w.reshape(w.shape[-2:])
    arrays = {name: np.ascontiguousarray(a) for name, a in arrays.items()}
    dram = {name: nc.dram_tensor(f"in_{name}", a.shape, mybir.dt.from_np(a.dtype), kind="ExternalInput").ap()
            for name, a in arrays.items()}
    dram["x_kept"] = nc.dram_tensor("x_kept", (P, 2, KT, HALF), F32, kind="Internal").ap()
    dram["log_cum"] = nc.dram_tensor("log_cum", (2, FOX_HEADS, TOK), F32, kind="Internal").ap()
    dram["out"] = nc.dram_tensor("out", (TOK, D), F32, kind="ExternalOutput").ap()
    program(nc, dram)
    done = run_bass_kernel_spmd(nc, [{f"in_{name}": a for name, a in arrays.items()}], core_ids=[0])
    return done.results[0]["out"].reshape(1, TOK, D)
```
